# Optimizing a Trainium2 kernel written in Bass

```python
import math
import jax, jax.numpy as jnp
from jax import lax
import numpy as np

D_MODEL = 1024
BATCH = 1
SEQ = 1024
DEPTH = 2

GRID_W = 64
CTX_LEN = 256
N_MIXERS = 2
MLA_HEADS = 16
QK_NOPE = 64
QK_ROPE = 32
V_DIM = 64
Q_RANK = 256
KV_RANK = 128
ROPE_BASE = 10000.0
Q_BLOCK = 128
HY_ORDER = 2
HY_EMB = 33
HY_BANDS = (HY_EMB - 1) // 2
HY_FILTER_HIDDEN = 64
HY_SHORT = 3
HY_TARGET = 1e-2
HY_FAST_PCT = 0.3
HY_SLOW_PCT = 1.5
D_FF = 4 * D_MODEL
EPS = 1e-6
N_MLA = (DEPTH + 1) // 2
N_HY = DEPTH // 2

kernel_name = "hybrid_mla_hyena_dit_prefix"

def rmsnorm(x, g):
    xf = x.astype(jnp.float32)
    y = xf * lax.rsqrt(jnp.mean(xf * xf, axis=-1, keepdims=True) + EPS)
    return (y * g.astype(jnp.float32)).astype(x.dtype)

def modulate(h, shift, scale):
    return h * (1.0 + scale) + shift

def axial_rope_tables(L):
    rows = L // GRID_W
    t = jnp.arange(rows * GRID_W)
    row = (t // GRID_W).astype(jnp.float32)
    col = (t % GRID_W).astype(jnp.float32)
    n_freq = QK_ROPE // 4
    inv = ROPE_BASE ** (-jnp.arange(n_freq, dtype=jnp.float32) / n_freq)
    ang = jnp.concatenate([row[:, None] * inv, col[:, None] * inv], axis=-1)
    return jnp.cos(ang), jnp.sin(ang)

def apply_rope(x, cos, sin):
    xf = x.astype(jnp.float32)
    x1, x2 = xf[..., : QK_ROPE // 2], xf[..., QK_ROPE // 2:]
    out = jnp.concatenate([x1 * cos - x2 * sin, x1 * sin + x2 * cos], axis=-1)
    return out.astype(x.dtype)

def mla_qkv(h, w_dq, g_q, w_uq, w_dkv, g_kv, w_ukv):
    B, L, _ = h.shape
    cq = rmsnorm(h @ w_dq, g_q)
    q = (cq @ w_uq).reshape(B, L, MLA_HEADS, QK_NOPE + QK_ROPE)
    kv_a = h @ w_dkv
    ckv = rmsnorm(kv_a[..., :KV_RANK], g_kv)
    k_rope = kv_a[..., KV_RANK:]
    kv = (ckv @ w_ukv).reshape(B, L, MLA_HEADS, QK_NOPE + V_DIM)
    return q[..., :QK_NOPE], q[..., QK_NOPE:], kv[..., :QK_NOPE], k_rope, kv[..., QK_NOPE:]

def attend(q_nope, q_rope, k_nope, k_rope, v):
    s = jnp.einsum('bqhd,bkhd->bhqk', q_nope, k_nope) + jnp.einsum('bqhr,bkr->bhqk', q_rope, k_rope)
    s = s.astype(jnp.float32) * (1.0 / math.sqrt(QK_NOPE + QK_ROPE))
    p = jax.nn.softmax(s, axis=-1).astype(v.dtype)
    return jnp.einsum('bhqk,bkhd->bqhd', p, v)

def mla_mixer(h_ctx, h_lat, w_dq, g_q, w_uq, w_dkv, g_kv, w_ukv, w_o, cos, sin, need_ctx):
    B, L, _ = h_lat.shape
    CL = h_ctx.shape[1]
    qn_c, qr_c, kn_c, kr_c, v_c = mla_qkv(h_ctx, w_dq, g_q, w_uq, w_dkv, g_kv, w_ukv)
    qn_l, qr_l, kn_l, kr_l, v_l = mla_qkv(h_lat, w_dq, g_q, w_uq, w_dkv, g_kv, w_ukv)
    qr_l = apply_rope(qr_l, cos[:, None, :], sin[:, None, :])
    kr_l = apply_rope(kr_l, cos, sin)
    kn = jnp.concatenate([kn_c, kn_l], axis=1)
    kr = jnp.concatenate([kr_c, kr_l], axis=1)
    v = jnp.concatenate([v_c, v_l], axis=1)
    nb = L // Q_BLOCK
    qn_b = qn_l.reshape(B, nb, Q_BLOCK, MLA_HEADS, QK_NOPE).swapaxes(0, 1)
    qr_b = qr_l.reshape(B, nb, Q_BLOCK, MLA_HEADS, QK_ROPE).swapaxes(0, 1)
    o = lax.map(lambda q: attend(q[0], q[1], kn, kr, v), (qn_b, qr_b))
    y_lat = o.swapaxes(0, 1).reshape(B, L, MLA_HEADS * V_DIM) @ w_o
    if need_ctx:
        o_c = attend(qn_c, qr_c, kn_c, kr_c, v_c)
        y_ctx = o_c.reshape(B, CL, MLA_HEADS * V_DIM) @ w_o
    else:
        y_ctx = None
    return y_ctx, y_lat

def short_conv(u, w, b):
    up = jnp.pad(u, ((0, 0), (1, 1), (0, 0)))
    return up[:, :-2] * w[0] + up[:, 1:-1] * w[1] + up[:, 2:] * w[2] + b

def hyena_filters(L, w1, b1, w2, b2, w3, freq):
    f32 = jnp.float32
    t = jnp.linspace(0.0, 1.0, L, dtype=f32)[:, None]
    w = (2.0 * math.pi) * jnp.arange(L, dtype=f32)[:, None] / L
    f = jnp.linspace(1e-4, HY_BANDS - 1, HY_BANDS, dtype=f32)[None, :]
    z = jnp.concatenate([t, jnp.cos(f * w), -jnp.sin(f * w)], axis=-1)
    fr = freq.astype(f32)
    hdn = jnp.sin(fr * (z @ w1.astype(f32) + b1.astype(f32)))
    hdn = jnp.sin(fr * (hdn @ w2.astype(f32) + b2.astype(f32)))
    hf = hdn @ w3.astype(f32)
    min_decay = math.log(HY_TARGET) / HY_SLOW_PCT
    max_decay = math.log(HY_TARGET) / HY_FAST_PCT
    deltas = jnp.linspace(min_decay, max_decay, D_MODEL, dtype=f32)
    decay = jnp.exp(-t * jnp.abs(deltas)[None, :])
    hf = hf.reshape(L, HY_ORDER, 2, D_MODEL) * decay[:, None, None, :]
    return hf.transpose(1, 2, 0, 3)

def long_conv(u, h_f, h_b, bias):
    L, D = h_f.shape
    k = jnp.concatenate([h_f, jnp.zeros((1, D), h_f.dtype), h_b[:0:-1]], axis=0)
    K = jnp.fft.rfft(k, n=2 * L, axis=0)
    uf = u.astype(jnp.float32)
    U = jnp.fft.rfft(uf, n=2 * L, axis=1)
    y = jnp.fft.irfft(U * K[None], n=2 * L, axis=1)[:, :L]
    return (y + uf * bias.astype(jnp.float32)).astype(u.dtype)

def hyena_mixer(h, w_in, b_in, w_short, b_short, f_w1, f_b1, f_w2, f_b2, f_w3, f_freq, bias, w_out, b_out):
    L = h.shape[1]
    u = short_conv(h @ w_in + b_in, w_short, b_short)
    x1, x2, v = jnp.split(u, 3, axis=-1)
    filt = hyena_filters(L, f_w1, f_b1, f_w2, f_b2, f_w3, f_freq)
    z = x1 * long_conv(v, filt[0, 0], filt[0, 1], bias[0])
    z = x2 * long_conv(z, filt[1, 0], filt[1, 1], bias[1])
    return z @ w_out + b_out

def sq_relu_mlp(h, w1, w2):
    return jnp.square(jax.nn.relu(h @ w1)) @ w2

def setup_inputs(seed: int = 0) -> dict:
    key = jax.random.key(seed)
    ks = iter(jax.random.split(key, 40))
    f32 = jnp.float32
    D = D_MODEL

    def nrm(shape, scale):
        return jax.random.normal(next(ks), shape, f32) * scale

    return {
        "x": nrm((BATCH, SEQ, D), 1.0),
        "c": nrm((BATCH, D), 1.0),
        "ctx": nrm((BATCH, CTX_LEN, D), 1.0),
        "c_ctx": nrm((D,), 1.0),
        "ada_w": nrm((DEPTH, D, 6 * D), 0.5 * D ** -0.5),
        "ada_b": nrm((DEPTH, 6 * D), 0.02),
        "norm_g": 1.0 + nrm((DEPTH, 4, D), 0.05),
        "mla_w_dq": nrm((N_MLA, D, Q_RANK), D ** -0.5),
        "mla_g_q": 1.0 + nrm((N_MLA, Q_RANK), 0.05),
        "mla_w_uq": nrm((N_MLA, Q_RANK, MLA_HEADS * (QK_NOPE + QK_ROPE)), Q_RANK ** -0.5),
        "mla_w_dkv": nrm((N_MLA, D, KV_RANK + QK_ROPE), D ** -0.5),
        "mla_g_kv": 1.0 + nrm((N_MLA, KV_RANK), 0.05),
        "mla_w_ukv": nrm((N_MLA, KV_RANK, MLA_HEADS * (QK_NOPE + V_DIM)), KV_RANK ** -0.5),
        "mla_w_o": nrm((N_MLA, MLA_HEADS * V_DIM, D), (MLA_HEADS * V_DIM) ** -0.5),
        "hy_w_in": nrm((N_HY, D, 3 * D), D ** -0.5),
        "hy_b_in": nrm((N_HY, 3 * D), 0.02),
        "hy_w_short": nrm((N_HY, HY_SHORT, 3 * D), HY_SHORT ** -0.5),
        "hy_b_short": nrm((N_HY, 3 * D), 0.02),
        "hy_f_w1": nrm((N_HY, HY_EMB, HY_FILTER_HIDDEN), HY_EMB ** -0.5),
        "hy_f_b1": nrm((N_HY, HY_FILTER_HIDDEN), 0.02),
        "hy_f_w2": nrm((N_HY, HY_FILTER_HIDDEN, HY_FILTER_HIDDEN), HY_FILTER_HIDDEN ** -0.5),
        "hy_f_b2": nrm((N_HY, HY_FILTER_HIDDEN), 0.02),
        "hy_f_w3": nrm((N_HY, HY_FILTER_HIDDEN, HY_ORDER * 2 * D), HY_FILTER_HIDDEN ** -0.5),
        "hy_f_freq": 1.0 + nrm((N_HY, HY_FILTER_HIDDEN), 0.05),
        "hy_bias": nrm((N_HY, HY_ORDER, D), 0.5),
        "hy_w_out": nrm((N_HY, D, D), D ** -0.5),
        "hy_b_out": nrm((N_HY, D), 0.02),
        "mlp_w1": nrm((DEPTH, D, D_FF), D ** -0.5),
        "mlp_w2": nrm((DEPTH, D_FF, D), D_FF ** -0.5),
    }

def reference(x, c, ctx, c_ctx, ada_w, ada_b, norm_g, mla_w_dq, mla_g_q, mla_w_uq, mla_w_dkv,
              mla_g_kv, mla_w_ukv, mla_w_o, hy_w_in, hy_b_in, hy_w_short, hy_b_short, hy_f_w1,
              hy_f_b1, hy_f_w2, hy_f_b2, hy_f_w3, hy_f_freq, hy_bias, hy_w_out, hy_b_out,
              mlp_w1, mlp_w2):
    L = x.shape[1]
    cos, sin = axial_rope_tables(L)
    s_lat = jax.nn.silu(c)
    s_ctx = jax.nn.silu(c_ctx)
    xc = ctx
    for i in range(DEPTH):
        last = i == DEPTH - 1
        j = i // N_MIXERS
        g_pre1, g_post1, g_pre2, g_post2 = norm_g[i, 0], norm_g[i, 1], norm_g[i, 2], norm_g[i, 3]
        sh1, sc1, gt1, sh2, sc2, gt2 = jnp.split((s_lat @ ada_w[i] + ada_b[i])[:, None, :], 6, axis=-1)
        csh1, csc1, cgt1, csh2, csc2, cgt2 = jnp.split(s_ctx @ ada_w[i] + ada_b[i], 6, axis=-1)

        h_lat = modulate(rmsnorm(x, g_pre1), sh1, sc1)
        h_ctx = modulate(rmsnorm(xc, g_pre1), csh1, csc1)
        if i % N_MIXERS == 0:
            y_ctx, y_lat = mla_mixer(h_ctx, h_lat, mla_w_dq[j], mla_g_q[j], mla_w_uq[j], mla_w_dkv[j],
                                     mla_g_kv[j], mla_w_ukv[j], mla_w_o[j], cos, sin, not last)
        else:
            hy_args = (hy_w_in[j], hy_b_in[j], hy_w_short[j], hy_b_short[j], hy_f_w1[j], hy_f_b1[j],
                       hy_f_w2[j], hy_f_b2[j], hy_f_w3[j], hy_f_freq[j], hy_bias[j], hy_w_out[j], hy_b_out[j])
            y_lat = hyena_mixer(h_lat, *hy_args)
            y_ctx = None if last else hyena_mixer(h_ctx, *hy_args)
        x = x + gt1 * rmsnorm(y_lat, g_post1)

        m_lat = sq_relu_mlp(modulate(rmsnorm(x, g_pre2), sh2, sc2), mlp_w1[i], mlp_w2[i])
        x = x + gt2 * rmsnorm(m_lat, g_post2)

        if not last:
            xc = xc + cgt1 * rmsnorm(y_ctx, g_post1)
            m_ctx = sq_relu_mlp(modulate(rmsnorm(xc, g_pre2), csh2, csc2), mlp_w1[i], mlp_w2[i])
            xc = xc + cgt2 * rmsnorm(m_ctx, g_post2)
    return x


_drawn_inputs = setup_inputs


def setup_inputs(seed=0):
    import zlib

    import numpy as np

    out = dict(_drawn_inputs(seed))
    spreads = {}
    factors = {'mla_g_q': 8.0,
     'hy_b_in': 3.509,
     'hy_b_short': 3.132,
     'hy_f_freq': 3.014,
     'hy_bias': 4.456,
     'hy_b_out': 64.0,
     'hy_f_b2': 3.282}
    for name, (base, spread) in spreads.items():
        noise = np.random.default_rng([zlib.crc32(name.encode()), seed]).standard_normal(out[name].shape)
        drawn = base * np.exp(spread * noise) if base else spread * noise
        out[name] = __import__('jax').numpy.asarray(drawn.astype(out[name].dtype))
    for name, factor in factors.items():
        out[name] = (out[name] * factor).astype(out[name].dtype)
    return out
```

```python
import math

import numpy as np

import concourse.bass as bass
import concourse.mybir as mybir

F32 = mybir.dt.float32
F32R = mybir.dt.float32r
ALU = mybir.AluOpType
ACT = mybir.ActivationFunctionType
AXX = mybir.AxisListType.X

P = 128
D = 1024
T = 1024
C = 256
KEYS = T + C
KT = D // P
TT = T // P
HALF = 512
HEADS = 16
NOPE, ROPE, VD = 64, 32, 64
QR, KVR = 256, 128
FF = 4 * D
CHUNK = 512
NCHUNK = FF // CHUNK
HIDT = CHUNK // P
EMB, FH = 33, 64
EPS = 1e-6
GRID_W, ROPE_BASE = 64, 10000.0
SCALE = 1.0 / math.sqrt(NOPE + ROPE)
ORDERS = 2
NFFT = 2 * T
R4 = math.sqrt(0.5)

V_ADAB = 0
V_NORMG = 96
V_BIN = 160
V_WSH = 184
V_BSH = 256
V_BOUT = 280
V_GQ = 288
V_GKV = 290
V_C = 291
V_CCTX = 299
V_FB1, V_FB2, V_FREQ = 307, 308, 309
NVEC = 384



def rope_table():
    t = np.arange(T)
    inv = ROPE_BASE ** (-np.arange(ROPE // 4) / (ROPE // 4))
    ang = np.concatenate([(t // GRID_W)[:, None] * inv, (t % GRID_W)[:, None] * inv], axis=1).T
    out = np.zeros((P, KEYS))
    out[:NOPE] = 1.0
    out[NOPE:NOPE + 16, :T] = out[NOPE + 16:NOPE + 32, :T] = np.cos(ang)
    out[NOPE + 32:NOPE + 48, :T] = -np.sin(ang)
    out[NOPE + 48:, :T] = np.sin(ang)
    out[NOPE:NOPE + 32, T:] = 1.0
    return out.astype(np.float32)


def rope_sum():
    m = np.zeros((P, P), np.float32)
    for j in range(ROPE):
        for o in (NOPE + j, NOPE + ROPE + j):
            m[NOPE + j, o] = m[NOPE + ROPE + j, o] = 1.0
    return m


def filter_positions():
    t = np.linspace(0.0, 1.0, T, dtype=np.float32).astype(np.float64)[:, None]
    w = (2.0 * math.pi) * np.arange(T)[:, None] / T
    f = np.linspace(1e-4, (EMB - 1) // 2 - 1, (EMB - 1) // 2)[None, :]
    return np.concatenate([t, np.cos(f * w), -np.sin(f * w)], axis=1).T.astype(np.float32).copy()


def filter_decay():
    t = np.linspace(0.0, 1.0, T)[:, None]
    deltas = np.linspace(math.log(1e-2) / 1.5, math.log(1e-2) / 0.3, D)
    return np.exp(-t * np.abs(deltas)[None, :]).astype(np.float32)


def dft_steps():
    b = np.arange(256)[:, None]
    fwd = np.zeros((7, P, 8, P))
    inv = np.zeros((7, P, 8, P))

    def cut(m, i, j):
        return m[i * P:(i + 1) * P, j * P:(j + 1) * P]

    f0 = 8 * np.arange(P)[None, :]
    f4 = f0 + 4
    ang0, ang4 = 2 * np.pi * b * f0 / NFFT, 2 * np.pi * b * f4 / NFFT
    c0, s0, c4, s4 = np.cos(ang0), -np.sin(ang0), np.cos(ang4), -np.sin(ang4)
    s0[:, 0] = (-1.0) ** b[:, 0]
    for k in range(2):
        for n, m in enumerate((c0, s0, c4, s4)):
            fwd[0, :, 2 * n + k] = cut(m, k, 0)
    i0, j0 = 2 * c0.T / NFFT, 2 * s0.T / NFFT
    i0[0] /= 2
    j0[0] /= 2
    i4, j4 = 2 * c4.T / NFFT, 2 * s4.T / NFFT
    for m in range(2):
        for n, (re, im) in enumerate(((i0, j0), (i4, j4))):
            inv[0, :, 4 * n + 2 * m] = cut(re, 0, m)
            inv[0, :, 4 * n + 2 * m + 1] = cut(im, 0, m)
    for c in (1, 2, 3):
        f = c + 8 * np.arange(256)[None, :]
        ang = 2 * np.pi * b * f / NFFT
        co, si = np.cos(ang), np.sin(ang)
        ic, isn = 2 * co.T / NFFT, 2 * si.T / NFFT
        for m in range(2):
            for k in range(2):
                fwd[2 * c - 1, :, 4 * m + k] = cut(co, k, m)
                fwd[2 * c - 1, :, 4 * m + 2 + k] = cut(-si, k, m)
                fwd[2 * c, :, 4 * m + k] = cut(-si, k, m)
                fwd[2 * c, :, 4 * m + 2 + k] = cut(-co, k, m)
                inv[2 * c - 1, :, 4 * m + k] = cut(ic, k, m)
                inv[2 * c - 1, :, 4 * m + 2 + k] = cut(-isn, k, m)
                inv[2 * c, :, 4 * m + k] = cut(isn, k, m)
                inv[2 * c, :, 4 * m + 2 + k] = cut(ic, k, m)
    return (fwd.reshape(7, P, 8 * P).astype(np.float32), inv.reshape(7, P, 8 * P).astype(np.float32))



FIXED = 16512
KB = 1024

N_LAT, N_CTX, N_CQ, N_CKV, N_POST1, N_PRE2, N_POST2, N_PREH, N_POSTH, N_PREM, N_POSTM = 0, 2, 3, 5, 8, 10, 12, 14, 16, 18, 20
A_LAT, A_CTX, A_MLP0, A_HY, A_MLP1 = 0, 16, 24, 40, 56
B_ATT, B_MLP0, B_HY, B_MLP1 = 0, 16, 32, 48
W_FILT = 0
W_DOWN = W_FILT + 16
W_HEAD = W_DOWN + 4
W_O = W_HEAD + 8
W_MLP0 = W_O + 8
W_IN = W_MLP0 + 8 * NCHUNK
W_CONV = W_IN + 24
W_OUT = W_CONV + 28
W_MLP1 = W_OUT + 8
W_END = W_MLP1 + 8 * NCHUNK


class Chain:

    def __init__(self, eng, sem):
        self.eng, self.sem, self.base, self.n = eng, sem, 0, 0

    def did(self, inst):
        inst.then_inc(self.sem, 1)
        self.n += 1

    def wait(self):
        self.eng.wait_ge(self.sem, self.base + self.n)

    def enter(self, i, per):
        self.before, self.per = self.base + self.n, per
        self.base, self.n = self.before + i * per, 0

    def leave(self, rounds):
        assert self.n == self.per, (self.n, self.per)
        self.base, self.n = self.before + rounds * self.per, 0


def build_program(nc, x, ctx, vecs, ada_w, w_down, w_head, w_o, w_in, w_out, mlp_w1, mlp_w2,
                  f_w1, f_w2, f_w3, hy_bias, rope, ropesum, ident, zpos, decay, dft_fwd, dft_inv, out):
    at = [FIXED]

    def fixed(name, shape, dt=F32):
        off = at[0]
        at[0] += -(-int(np.prod(shape[1:])) * 4 // 32) * 32
        return nc.alloc_sbuf_tensor_at(name, list(shape), dt, offset=off)

    raw = [fixed(f"w_raw{s}", [P, 1024]) for s in range(2)]
    whi = [fixed(f"w_hi{s}", [P, 8, P], F32R) for s in range(2)]
    wlo = [fixed(f"w_lo{s}", [P, 8, P], F32R) for s in range(2)]
    idm = fixed("idm", [P, P])
    ones = fixed("ones", [P, P])
    vec = fixed("vec", [P, NVEC])
    mod = fixed("mod", [P, 112])
    fac = fixed("fac", [P, 72])
    sil = fixed("sil", [P, 16])
    sile = fixed("sile", [P, 16])
    eps = fixed("eps", [P, 1])
    mx = fixed("mx", [P, 4])
    mxr = fixed("mxr", [P, 4])
    zero = fixed("zero", [P, 1])
    notop = fixed("notop", [P, 1])
    ARENA = -(-at[0] // 64) * 64

    def arena(name, kb, shape, dt=F32):
        return nc.alloc_sbuf_tensor_at(name, list(shape), dt, offset=ARENA + int(kb * KB))

    f_s = arena("f_s", 0, [P, 4, 2, D])
    f_d = arena("f_d", 32, [P, 4, 2, D])
    rg_hi = [arena(f"rg_hi{s}", 64 + 16 * s, [P, 4, HALF], F32R) for s in range(2)]
    rg_lo = [arena(f"rg_lo{s}", 72 + 16 * s, [P, 4, HALF], F32R) for s in range(2)]
    bq = arena("bq", 96, [P, 2, D])
    bs = arena("bs", 104, [P, 2, D])
    val = [arena(f"val{s}", 112 + 8 * s, [P, 4, HALF]) for s in range(2)]
    fb = arena("fb", 128, [P, 2, D])
    dec = [arena(f"dec{s}", 136 + 4 * s, [P, D]) for s in range(2)]
    fw3 = arena("fw3", 144, [FH, 2 * D])
    fbias = arena("fbias", 152, [1, 2 * D])
    ko = [arena(f"ko{s}", 160 + 2 * s, [P, HALF]) for s in range(4)]
    hda = arena("hda", 168, [FH, T])
    hdn = arena("hdn", 172, [FH, T])
    hd2 = arena("hd2", 176, [FH, T])
    zp = arena("zp", 128, [EMB, T])
    hd1 = arena("hd1", 132, [FH, T])
    fw12 = arena("fw12", 136, [FH, 2, FH])
    vrow = arena("vrow", 64, [P, NVEC // P, P])
    aacc = arena("aacc", 0, [P, 6 * D])
    aaccc = arena("aaccc", 24, [P, 2 * D])
    araw = [arena(f"araw{s}", 32 + 12 * s, [P, 3 * D]) for s in range(2)]
    xa = arena("xa", 0, [P, KT, T])
    xtm = arena("xtm", 112, [P, TT, D])
    xctm = arena("xctm", 152, [P, 2, D])
    xc = arena("xc", 144, [P, KT, C])
    hh = arena("hh", 32, [P, KT, T], F32R)
    hl = arena("hl", 64, [P, KT, T], F32R)
    hch = arena("hch", 96, [P, KT, C], F32R)
    hcl = arena("hcl", 104, [P, KT, C], F32R)
    asq = arena("asq", 112, [P, KT, HALF])
    arstd = arena("arstd", 128, [P, KEYS])
    atmp = [arena(f"atmp{s}", 136 + 2 * s, [P, HALF]) for s in range(2)]
    assum = arena("assum", 140, [P, HALF])
    astd = arena("astd", 142, [P, HALF])
    cq = arena("cq", 144, [P, 2, T])
    ckv = arena("ckv", 152, [P, KEYS])
    krt = arena("krt", 112, [P, KEYS])
    cqh = arena("cqh", 118, [P, 2, T], F32R)
    cql = arena("cql", 126, [P, 2, T], F32R)
    ckvh = arena("ckvh", 134, [P, KEYS], F32R)
    ckvl = arena("ckvl", 139, [P, KEYS], F32R)
    rtab = arena("rtab", 160, [P, KEYS])
    rsm = arena("rsm", 117, [P, P])
    csq = arena("csq", 165, [P, 2, HALF])
    crstd = arena("crstd", 169, [P, KEYS])
    cssum = arena("cssum", 174, [P, HALF])
    cstd = arena("cstd", 176, [P, HALF])
    ao = arena("ao", 0, [P, KT, T])
    qh = arena("qh", 32, [P, 2, T], F32R)
    ql = arena("ql", 40, [P, 2, T], F32R)
    kh = arena("kh", 48, [P, 2, KEYS], F32R)
    kl = arena("kl", 58, [P, 2, KEYS], F32R)
    vh = arena("vh", 68, [P, 10, 2, P], F32R)
    vl = arena("vl", 78, [P, 10, 2, P], F32R)
    pr = arena("pr", 88, [P, 2, 2, KEYS])
    pth = [arena(f"pth{s}", 144 + 2 * s, [P, 2, 256], F32R) for s in range(4)]
    ptl = [arena(f"ptl{s}", 152 + 2 * s, [P, 2, 256], F32R) for s in range(4)]
    qf = [arena(f"qf{s}", 165 + 2 * s, [P, HALF]) for s in range(2)]
    rc = arena("rc", 169, [P, 256])
    xm = arena("xm", 128, [P, KT, T])
    y = arena("y", 96, [P, KT, T])
    hidh = arena("hidh", 0, [P, HIDT, T], F32R)
    hidl = arena("hidl", 16, [P, HIDT, T], F32R)
    msq = arena("msq", 0, [P, KT, HALF])
    mr = [arena(f"mr{s}", 160 + 2 * s, [P, HALF]) for s in range(2)]
    ms2 = [arena(f"ms2{s}", 164 + 2 * s, [P, HALF]) for s in range(2)]
    mrstd = arena("mrstd", 168, [P, T])
    mtmp = [arena(f"mtmp{s}", 172 + 2 * s, [P, HALF]) for s in range(2)]
    mssum = arena("mssum", 176, [P, HALF])
    mstd = arena("mstd", 178, [P, HALF])
    ub = [arena(f"ub{s}", 96 + 5 * s, [P, T + 2]) for s in range(2)]
    uc = [arena(f"uc{s}", 106 + 4 * s, [P, T]) for s in range(2)]
    ut = [arena(f"ut{s}", 114 + 4 * s, [P, TT, P]) for s in range(2)]
    src = arena("src", 128, [P, 4, 2, D])
    pz = arena("pz", 0, [P, 4, 4, D])
    ks = [arena(f"ks{s}", 160 + 6 * s, [P, 3, HALF]) for s in range(2)]
    pt = [arena(f"pt{s}", 172 + 2 * s, [P, HALF]) for s in range(2)]
    gate = arena("gate", 64, [P, 4, 2, D])
    zh = arena("zh", 0, [P, KT, T], F32R)
    zl = arena("zl", 32, [P, KT, T], F32R)
    ot = [arena(f"ot{s}", 4 * s, [P, D]) for s in range(2)]

    ps = nc.alloc_psum_tensor("ps", [P, 8, HALF], F32)
    psf = ps[:, :, :].rearrange("p b n -> p (b n)")

    x_spill = nc.dram_tensor("x_spill", [KT, P, T], F32, kind="Internal").ap()
    spec = nc.dram_tensor("spec", [ORDERS * 8 * 3 * P, D], F32, kind="Internal").ap()
    u_tm = nc.dram_tensor("u_tm", [3 * KT, T, P], F32, kind="Internal").ap()

    names = set()

    def sem(name):
        assert name not in names
        names.add(name)
        return nc.alloc_semaphore(name)

    w_arrived = [sem(f"w_arrived{s}") for s in range(2)]
    w_hi_made, w_staged = sem("w_hi_made"), sem("w_staged")
    const_in, filt_in, filt_w3_in = sem("const_in"), sem("filt_in"), sem("filt_w3_in")
    dec_in = [sem(f"dec_in{s}") for s in range(2)]
    vec_t, vec_made, sil_exp = sem("vec_t"), sem("vec_made"), sem("sil_exp")
    ones_made, zero_made = sem("ones_made"), sem("zero_made")
    dve_chain, act_chain = sem("dve_chain"), sem("act_chain")
    ada_in = [sem(f"ada_in{s}") for s in range(2)]
    ada_acc, ada_sum, mods_made = sem("ada_acc"), sem("ada_sum"), sem("mods_made")
    hd_done, hd_arg, hd_sin = sem("hd_done"), sem("hd_arg"), sem("hd_sin")
    hf_done, hf_free = sem("hf_done"), sem("hf_free")
    fs_done, fs_free = sem("fs_done"), sem("fs_free")
    fr_val, fr_hi, fr_lo = sem("fr_val"), sem("fr_hi"), sem("fr_lo")
    ko_out = [sem(f"ko_out{s}") for s in range(4)]
    x_in, xt_done, xt_free = sem("x_in"), sem("xt_done"), sem("xt_free")
    sq_made, sum_made, ms_made, std_made, rstd_made = sem("sq_made"), sem("sum_made"), sem("ms_made"), sem("std_made"), sem("rstd_made")
    pre_t, pre_hi, pre_lo, post_y, post_x = sem("pre_t"), sem("pre_hi"), sem("pre_lo"), sem("post_y"), sem("post_x")
    x_saved, x_back = sem("x_saved"), sem("x_back")
    dn_done, dn_free = sem("dn_done"), sem("dn_free")
    cn_hi, cn_val, cn_lo = sem("cn_hi"), sem("cn_val"), sem("cn_lo")
    kr_made, kr_done, kr_hi, kr_lo = sem("kr_made"), sem("kr_done"), sem("kr_hi"), sem("kr_lo")
    tab_in, v_ones = sem("tab_in"), sem("v_ones")
    pp_done, pp_free, q_val, pp_hi = sem("pp_done"), sem("pp_free"), sem("q_val"), sem("pp_hi")
    q_lo, k_lo, raw_max, uc_left = sem("q_lo"), sem("k_lo"), sem("raw_max"), sem("uc_left")
    s_done, max_made, p_made = sem("s_done"), sem("max_made"), sem("p_made")
    t_done, t_hi, t_free = sem("t_done"), sem("t_hi"), sem("t_free")
    pv_done, rc_made, o_made = sem("pv_done"), sem("rc_made"), sem("o_made")
    oh_made, ol_made = sem("oh_made"), sem("ol_made")
    wo_done, wo_free = sem("wo_done"), sem("wo_free")
    hid_done, hid_free = [sem(f"hid_done{i}") for i in range(2)], [sem(f"hid_free{i}") for i in range(2)]
    hid_sq, hid_hi, hid_lo = [sem(f"hid_sq{i}") for i in range(2)], [sem(f"hid_hi{i}") for i in range(2)], [sem(f"hid_lo{i}") for i in range(2)]
    acc_done, acc_free = [sem(f"acc_done{i}") for i in range(2)], [sem(f"acc_free{i}") for i in range(2)]
    y_zero = sem("y_zero")
    wi_done, wi_free, uc_mid, uc_made, ut_done, ut_made = (sem("wi_done"), sem("wi_free"), sem("uc_mid"), sem("uc_made"), sem("ut_done"), sem("ut_made"))
    ut_out = [sem(f"ut_out{s}") for s in range(2)]
    src_in, k_ny_in, gate_in = sem("src_in"), sem("k_ny_in"), sem("gate_in")
    k_in = [sem(f"k_in{s}") for s in range(2)]
    cf_done, cf_free = sem("cf_done"), sem("cf_free")
    ci_done, ci_free = sem("ci_done"), sem("ci_free")
    cr_val, cr_hi, cr_lo = sem("cr_val"), sem("cr_hi"), sem("cr_lo")
    pz_made, z_made = sem("pz_made"), sem("z_made")
    zt_done, z_hi, z_lo = sem("zt_done"), sem("z_hi"), sem("z_lo")
    out_done, out_made = sem("out_done"), sem("out_made")
    out_sent = [sem(f"out_sent{s}") for s in range(2)]
    ho_done, ho_free = sem("ho_done"), sem("ho_free")

    def w_tiles(ap):
        return ap.rearrange("(k p) m -> p k m", p=P)

    RING = [(c, n) for c in range(4) for n in range(2)]
    def s_groups(c):
        if c == 0:
            return [((0, 1), (0, 1), 0, 0), ((2, 3), (0, 1), 0, 2), ((4, 5), (2, 3), 1, 0)]
        return [((4 * m, 4 * m + 1, 4 * m + 2, 4 * m + 3), (0, 1, 2, 3), 2 * c + m, 0) for m in range(2)]

    def d_groups(c):
        if c == 0:
            return [((2, 3), (0, 1), 0, 1), ((6, 7), (2, 3), 1, 1)]
        return [((4 * m, 4 * m + 1, 4 * m + 2, 4 * m + 3), (0, 1, 2, 3), 2 * c + m, 1) for m in range(2)]

    S_CNT = [len(s_groups(c)) for c, _ in RING]
    D_CNT = [len(d_groups(c)) for c, _ in RING]
    FS_PER = sum(S_CNT) + sum(D_CNT)
    S_END = [sum(S_CNT[:i + 1]) for i in range(8)]
    D_END = [sum(S_CNT) + sum(D_CNT[:i + 1]) for i in range(8)]
    RING_END = S_END + D_END

    FS_GROUPS = [(c, n, *g) for groups in (s_groups, d_groups) for c, n in RING for g in groups(c)]
    KO_USES = [sum(2 if g[4:] == (0, 0) else 1 for g in FS_GROUPS[q::4]) for q in range(4)]
    STEP_END = [8 + 4 * s for s in range(7)]
    FWD_END = INV_END = STEP_END

    def half(n):
        return slice(n * HALF, (n + 1) * HALF)

    def transform_groups(s, inverse):
        out = []
        for n in range(2):
            if s == 0:
                for q in range(4):
                    out.append((n, (2 * q, 2 * q + 1), (2 * (q // 2), 2 * (q // 2) + 1), 4 * n + q))
            else:
                for m in range(2):
                    out.append((n, tuple(range(4 * m, 4 * m + 4)), (0, 1, 2, 3), STEP_END[s - 1] + 2 * n + m))
        return out

    def pair_tile(p):
        return (p % 2, p // 2) if p < 4 else (2 * (p // 4) + p % 2, p % 4 // 2)

    def pair_groups(p):
        if p < 4:
            return 2 * p, 2 * p + 1
        return 8 * (p // 4) + p % 4, 8 * (p // 4) + 4 + p % 4

    def ring_read(c, n):
        return 4 * (n + 1) if c == 0 else 8 * c + 6 + 2 * n

    def filter_step_src(o8):
        return (0, 1, 3, 5, 0, 2, 4, 6)[o8]

    block = nc.Block()
    with block as blk:

        @blk.sync
        def _(sp):
            def weights(s, source):
                if not (isinstance(s, int) and s < 2):
                    sp.wait_ge(w_staged, s - 1)
                return source

            def load(slot, s, source, shape=None):
                weights(s, source)
                dst = raw[slot][:, :]
                if shape:
                    dst = dst.rearrange("p (k m) -> p k m", k=shape)
                sp.dma_start(dst, source).then_inc(w_arrived[slot], 16)

            sp.dma_start(vrow[:, :, :], vecs.rearrange("(a p) c -> p a c", p=P)).then_inc(const_in, 16)
            sp.dma_start(idm[:, :], ident).then_inc(const_in, 16)
            n = 0
            for l in range(2):
                for k in range(KT):
                    for h in range(2):
                        if n >= 2:
                            sp.wait_ge(ada_acc, n - 1)
                        sp.dma_start(araw[n % 2][:, :], ada_w[l, k * P:(k + 1) * P, h * 3 * D:(h + 1) * 3 * D]).then_inc(ada_in[n % 2], 16)
                        n += 1
            sp.dma_start(zp[:, :], zpos).then_inc(filt_in, 16)
            sp.dma_start(fw12[0:EMB, 0, :], f_w1).then_inc(filt_in, 16)
            sp.dma_start(fw12[:, 1, :], f_w2).then_inc(filt_in, 16)
            sp.dma_start(fbias[:, :], hy_bias.rearrange("(a o) d -> a (o d)", a=1)).then_inc(filt_in, 16)
            sp.wait_ge(hd_sin, 2)
            for o in range(ORDERS):
                if o:
                    sp.wait_ge(hf_done, 32 * o)
                sp.dma_start(fw3[:, :], f_w3[:, o * 2 * D:(o + 1) * 2 * D]).then_inc(filt_w3_in, 16)
                for t in range(TT):
                    if 8 * o + t >= 2:
                        sp.wait_ge(hf_free, 4 + 4 * (8 * o + t - 1))
                    sp.dma_start(dec[t % 2][:, :], decay[t * P:(t + 1) * P, :]).then_inc(dec_in[t % 2], 16)
                    if t < 2:
                        load(t % 2, W_FILT + 8 * o + t, dft_fwd[filter_step_src(t)])
                for s in range(2, 8):
                    load(s % 2, W_FILT + 8 * o + s, dft_fwd[filter_step_src(s)])
            sp.wait_ge(fs_done, 2 * FS_PER)
            for q in range(4):
                sp.wait_ge(ko_out[q], 16 * ORDERS * KO_USES[q])
            sp.dma_start(xtm[:, :, :], x.rearrange("(a p) d -> p a d", p=P)).then_inc(x_in, 16)
            sp.dma_start(xctm[:, :, :], ctx.rearrange("(a p) d -> p a d", p=P)).then_inc(x_in, 16)
            for s in range(4):
                load(s % 2, W_DOWN + s, w_tiles(w_down)[:, :, s * P:(s + 1) * P], 8)
            sp.wait_ge(xt_free, 20)
            sp.dma_start(rtab[:, :], rope).then_inc(tab_in, 16)
            sp.wait_ge(pre_t, A_LAT + 16)
            sp.dma_start(x_spill.rearrange("k p t -> p k t"), xa[:, :, :]).then_inc(x_saved, 16)
            sp.wait_ge(pre_lo, A_CTX + 8)
            sp.dma_start(rsm[:, :], ropesum).then_inc(tab_in, 16)
            for s in range(2):
                load(s % 2, W_HEAD + s, w_head[s])
            with sp.Fori(1, HEADS // 4) as i:
                for s in range(2):
                    load(s, W_HEAD + 2 * i + s, w_head[bass.ds(2 * i + s, 1)].rearrange("a p n -> (a p) n"))
            for s in range(2):
                load(s, W_O + s, w_tiles(w_o)[:, :, s * P:(s + 1) * P], 8)
            with sp.Fori(1, 4) as i:
                for s in range(2):
                    load(s, W_O + 2 * i + s, w_tiles(w_o)[:, :, bass.ds((2 * i + s) * P, P)], 8)
            sp.wait_ge(ol_made, 8)
            sp.wait_ge(x_saved, 16)
            sp.dma_start(xm[:, :, :], x_spill.rearrange("k p t -> p k t")).then_inc(x_back, 16)

            def mlp(layer, base):
                w1 = w_tiles(mlp_w1[layer])
                w2 = mlp_w2[layer].rearrange("(c k p) m -> c p k m", k=HIDT, p=P)

                def step(j, s):
                    if s < 4:
                        load(s % 2, base + 8 * j + s, w1[:, :, bass.ds((4 * j + s) * P, P)], 8)
                    else:
                        load(s % 2, base + 8 * j + s, w2[bass.ds(j, 1), :, :, (s - 4) * 256:(s - 3) * 256].rearrange("c p k m -> (c p) k m"), 4)

                with sp.Fori(0, NCHUNK) as j:
                    for s in range(8):
                        step(j, s)

            mlp(0, W_MLP0)
            for s in range(2):
                load(s, W_IN + s, w_tiles(w_in)[:, :, s * P:(s + 1) * P], 8)
            sp.wait_ge(pre_t, A_HY + 16)
            sp.dma_start(x_spill.rearrange("k p t -> p k t"), xm[:, :, :]).then_inc(x_saved, 16)
            with sp.Fori(1, 12) as i:
                for s in range(2):
                    load(s, W_IN + 2 * i + s, w_tiles(w_in)[:, :, bass.ds((2 * i + s) * P, P)], 8)
            sp.wait_ge(x_saved, 32)
            for s in range(2):
                sp.wait_ge(ut_out[s], 16 * 12)

            def token_major(dst, first, arrived):
                for k in range(KT):
                    sp.dma_start(dst[:, :, :, k * P:(k + 1) * P].rearrange("p a b c -> p (a b) c"),
                                 u_tm[bass.ds(first + k, 1)].rearrange("m (a p) c -> (m p) a c", p=P)).then_inc(arrived, 16)

            token_major(src, 2 * KT, src_in)
            with sp.Fori(0, ORDERS) as o:
                def conv_weights(s):
                    load(s % 2, W_CONV + 14 * o + s, dft_fwd[s])

                def spectrum(p):
                    f, n = pair_tile(p)
                    if p >= 2:
                        sp.wait_ge(cf_free, 16 * o + p - 1)
                    rows = spec[bass.ds((8 * o + f) * 3 * P, 2 * P), half(n)]
                    sp.dma_start(ks[p % 2][:, 0:2, :], rows.rearrange("(a p) d -> p a d", p=P)).then_inc(k_in[p % 2], 16)
                    if f == 0:
                        sp.dma_start(ks[p % 2][:, 2, :], spec[bass.ds(((8 * o + f) * 3 + 2) * P, P), half(n)]).then_inc(k_ny_in, 16)

                conv_weights(0)
                spectrum(0)
                spectrum(1)
                conv_weights(1)
                spectrum(2)
                spectrum(3)
                for c in (1, 2, 3):
                    conv_weights(2 * c)
                    spectrum(4 * c)
                    spectrum(4 * c + 1)
                    if c < 3:
                        conv_weights(2 * c + 1)
                    spectrum(4 * c + 2)
                    spectrum(4 * c + 3)
                for s in range(7):
                    load((7 + s) % 2, W_CONV + 14 * o + 7 + s, dft_inv[s])
                sp.wait_ge(ci_done, 32 * o + 32)
                token_major(gate, KT * o, gate_in)
            for s in range(2):
                load(s, W_OUT + s, w_tiles(w_out)[:, :, s * P:(s + 1) * P], 8)
            sp.wait_ge(z_lo, 16)
            sp.dma_start(xm[:, :, :], x_spill.rearrange("k p t -> p k t")).then_inc(x_back, 16)
            with sp.Fori(1, 4) as i:
                for s in range(2):
                    load(s, W_OUT + 2 * i + s, w_tiles(w_out)[:, :, bass.ds((2 * i + s) * P, P)], 8)
            mlp(1, W_MLP1)
            for t in range(TT):
                sp.wait_ge(out_made, 2 * t + 2)
                sp.dma_start(out[t * P:(t + 1) * P, :], ot[t % 2][:, :]).then_inc(out_sent[t % 2], 16)
            for s in range(2):
                sp.wait_ge(out_sent[s], 16 * 4)

        @blk.gpsimd
        def _(pool):
            nc.gpsimd.memset(zero[:, :], 0.0).then_inc(zero_made, 1)
            pool.wait_ge(zero_made, 1)

            def stage(slot, s, uses, read=None):
                pool.wait_ge(w_arrived[slot], 16 * uses)
                if read:
                    pool.wait_ge(*read)
                hi, lo = (w[slot][:, :, :].rearrange("p k m -> p (k m)") for w in (whi, wlo))
                nc.gpsimd.tensor_tensor(hi, raw[slot][:, :], zero[:, 0:1].to_broadcast([P, 1024]), ALU.add).then_inc(w_hi_made, 1)
                pool.wait_ge(w_hi_made, s + 1)
                nc.gpsimd.tensor_tensor(lo, raw[slot][:, :], hi, ALU.subtract).then_inc(w_staged, 1)

            def uses(s):
                return s // 2 + 1

            done = {}
            for o in range(ORDERS):
                for s in range(8):
                    r = 2 * s + 1
                    done[W_FILT + 8 * o + s] = (fs_done, FS_PER * o + RING_END[r])
            for s, n in enumerate((2, 4, 7, 10)):
                done[W_DOWN + s] = (dn_done, n)
            for g in range(8):
                done[W_HEAD + g] = (pp_done, 10 * g + 10)
            for s in range(8):
                done[W_O + s] = (wo_done, 2 * s + 2)
                done[W_OUT + s] = (ho_done, 2 * s + 2)
            for l, base in enumerate((W_MLP0, W_MLP1)):
                for s in (6, 7):
                    done[base + 8 * (NCHUNK - 1) + s] = (acc_done[l], 16 * (NCHUNK - 1) + 4 * (s - 3))
            for s in range(24):
                done[W_IN + s] = (wi_done, 2 * s + 2)
            for s in (12, 13):
                done[W_CONV + 14 + s] = (ci_done, 32 + INV_END[s - 7])
            for s in range(W_FILT, W_HEAD + 2):
                stage(s % 2, s, uses(s), done.get(s - 2))
            with pool.Fori(1, 4) as i:
                for s in range(2):
                    stage(s, W_HEAD + 2 * i + s, W_HEAD // 2 + i + 1, (pp_done, 20 * i + 10 * s - 10))
            for s in range(W_O, W_O + 2):
                stage(s % 2, s, uses(s), done[s - 2])
            with pool.Fori(1, 4) as i:
                for s in range(2):
                    stage(s, W_O + 2 * i + s, W_O // 2 + i + 1, (wo_done, 4 * i + 2 * s - 2))

            def mlp(l, base):
                def step(j, s):
                    if s < 6:
                        read = (hid_done[l], 8 * j + 2 * (s - 1))
                    else:
                        read = (acc_done[l], 16 * j + 4 * (s - 5))
                    stage(s % 2, base + 8 * j + s, base // 2 + 4 * j + s // 2 + 1, read)

                for s in range(2):
                    stage(s, base + s, uses(base + s), done[base + s - 2])
                with pool.Fori(0, NCHUNK - 1) as j:
                    for s in range(2, 10):
                        step(j, s)
                for s in range(2, 8):
                    step(NCHUNK - 1, s)

            mlp(0, W_MLP0)
            for s in range(W_IN, W_IN + 2):
                stage(s % 2, s, uses(s), done[s - 2])
            with pool.Fori(1, 12) as i:
                for s in range(2):
                    stage(s, W_IN + 2 * i + s, W_IN // 2 + i + 1, (wi_done, 4 * i + 2 * s - 2))
            for s in range(W_CONV, W_CONV + 2):
                stage(s % 2, s, uses(s), done[s - 2])
            with pool.Fori(0, ORDERS - 1) as o:
                for s in range(2, 16):
                    read = (cf_done, 32 * o + FWD_END[s - 2]) if s < 9 else (ci_done, 32 * o + INV_END[s - 9])
                    stage(s % 2, W_CONV + 14 * o + s, W_CONV // 2 + 7 * o + s // 2 + 1, read)
            for s in range(2, 14):
                read = (cf_done, 32 * (ORDERS - 1) + FWD_END[s - 2]) if s < 9 else (ci_done, 32 * (ORDERS - 1) + INV_END[s - 9])
                stage(s % 2, W_CONV + 14 + s, uses(W_CONV + 14 + s), read)
            for s in range(W_OUT, W_OUT + 2):
                stage(s % 2, s, uses(s), done[s - 2])
            with pool.Fori(1, 4) as i:
                for s in range(2):
                    stage(s, W_OUT + 2 * i + s, W_OUT // 2 + i + 1, (ho_done, 4 * i + 2 * s - 2))
            mlp(1, W_MLP1)

        @blk.tensor
        def _(pe):
            def products(dst, terms, done):
                n = len(terms)
                for i, (wh, wl, rh, rl, ready) in enumerate(terms):
                    if ready:
                        pe.wait_ge(*ready)
                    nc.tensor.matmul(dst, wh, rh, start=(i == 0), stop=False)
                    nc.tensor.matmul(dst, wh, rl, start=False, stop=False)
                    last = nc.tensor.matmul(dst, wl, rh, start=False, stop=(i == n - 1))
                last.then_inc(done, 1)

            def w(slot, k):
                return whi[slot][:, k, :], wlo[slot][:, k, :]

            def mean_square(c, ssum, width, bank):
                pe.wait_ge(sum_made, c + 1)
                nc.tensor.matmul(ps[:, bank, 0:width], ones[:, :], ssum[:, 0:width], start=True, stop=True).then_inc(ms_made, 1)

            pe.wait_ge(const_in, 32)
            pe.wait_ge(ones_made, 1)
            for a in range(3):
                last = nc.tensor.transpose(ps[:, 0, a * P:(a + 1) * P], vrow[:, a, :], idm[:, :])
            last.then_inc(vec_t, 1)
            for l in range(2):
                pe.wait_ge(ada_acc, 16 * (l + 1))
                for m in range(48):
                    last = nc.tensor.matmul(ps[:, 1, 64 * l + m:64 * l + m + 1], aacc[:, m * P:(m + 1) * P], ones[:, 0:1], start=True, stop=True)
                if l == 0:
                    for m in range(16):
                        last = nc.tensor.matmul(ps[:, 1, 48 + m:49 + m], aaccc[:, m * P:(m + 1) * P], ones[:, 0:1], start=True, stop=True)
                last.then_inc(ada_sum, 1)
            pe.wait_ge(filt_in, 64)
            for n in range(2):
                last = nc.tensor.matmul(ps[0:FH, 2 + n, :], fw12[0:EMB, 0, :], zp[0:EMB, half(n)], start=True, stop=True)
            last.then_inc(hd_done, 1)
            pe.wait_ge(hd_sin, 1)
            for n in range(2):
                last = nc.tensor.matmul(ps[0:FH, 2 + n, :], fw12[:, 1, :], hd1[:, half(n)], start=True, stop=True)
            last.then_inc(hd_done, 1)
            pe.wait_ge(hd_sin, 2)
            with pe.Fori(0, ORDERS) as o:
                pe.wait_ge(filt_w3_in, 16 * o + 16)
                for t in range(TT):
                    for j in range(4):
                        pe.wait_ge(hf_free, 32 * o + 4 * t + j + 1)
                        nc.tensor.matmul(ps[:, 4 + j, :], hd2[:, t * P:(t + 1) * P], fw3[:, half(j)], start=True, stop=True).then_inc(hf_done, 1)
                idx = 0
                for rnd, groups in ((0, s_groups), (1, d_groups)):
                    for r, (c, n) in enumerate(RING):
                        slot = r % 2
                        pe.wait_ge(fr_lo, 16 * o + 8 * rnd + r + 1)
                        if n == 0:
                            pe.wait_ge(w_staged, W_FILT + 8 * o + 4 * rnd + c + 1)
                        for tiles, rows, _, _ in groups(c):
                            pe.wait_ge(fs_free, FS_PER * o + max(idx + 1, 4))
                            products(ps[:, idx % 4, :],
                                     [(*w(c % 2, a), rg_hi[slot][:, b, :], rg_lo[slot][:, b, :], None) for a, b in zip(tiles, rows)], fs_done)
                            idx += 1
            pe.wait_ge(x_in, 32)
            for g in range(20):
                bank = g % 4
                if g == 0:
                    pe.wait_ge(fs_free, 4 + 2 * FS_PER)
                if g >= 4:
                    pe.wait_ge(xt_free, g - 3)
                for j in range(4):
                    if g < 16:
                        blk_in = xtm[:, 4 * (g % 2) + j, (g // 2) * P:(g // 2 + 1) * P]
                    else:
                        dt = 2 * (g - 16) + j // 2
                        blk_in = xctm[:, j % 2, dt * P:(dt + 1) * P]
                    last = nc.tensor.transpose(ps[:, bank, j * P:(j + 1) * P], blk_in, idm[:, :])
                last.then_inc(xt_done, 1)
            for c in range(2):
                mean_square(N_LAT + c, assum, HALF, 6 + c)
            pe.wait_ge(std_made, 1)
            mean_square(N_CTX, assum, C, 6)
            g = 0
            for s in range(4):
                pe.wait_ge(w_staged, W_DOWN + s + 1)
                for n in range(3 if s >= 2 else 2):
                    if g >= 6:
                        pe.wait_ge(dn_free, g - 5)
                    width = HALF if n < 2 else C
                    rh, rl = (hh, hl) if n < 2 else (hch, hcl)
                    cols = half(n) if n < 2 else slice(0, C)
                    base = A_LAT + 8 * n if n < 2 else A_CTX
                    products(ps[:, g % 6, 0:width],
                             [(*w(s % 2, k), rh[:, k, cols], rl[:, k, cols], (pre_lo, base + k + 1)) for k in range(KT)], dn_done)
                    g += 1
            for c in range(2):
                pe.wait_ge(std_made, N_CQ + c - 1)
                mean_square(N_CQ + c, cssum, HALF, 6 + (c + 1) % 2)
            for c in range(3):
                pe.wait_ge(std_made, N_CKV + c - 1)
                mean_square(N_CKV + c, cssum, HALF if c < 2 else C, 6 + (c + 1) % 2)
            pe.wait_ge(tab_in, 32)
            for c in range(3):
                width = HALF if c < 2 else C
                pe.wait_ge(kr_made, c + 1)
                nc.tensor.matmul(ps[:, 3 + c, 0:width], rsm[:, :], krt[:, c * HALF:c * HALF + width], start=True, stop=True).then_inc(kr_done, 1)
            pe.wait_ge(cn_lo, 5)
            pe.wait_ge(kr_lo, 6)
            with pe.Fori(0, HEADS // 4) as i:
                for gg in range(2):
                    pe.wait_ge(w_staged, W_HEAD + 2 * i + gg + 1)
                    for j in range(10):
                        pe.wait_ge(pp_free, 20 * i + 10 * gg + max(j + 1, 4))
                        bank = j % 4
                        if j < 4:
                            hd, n = j // 2, j % 2
                            products(ps[:, bank, :], [(*w(gg, 2 * k + hd), cqh[:, k, half(n)], cql[:, k, half(n)], None) for k in range(2)], pp_done)
                        elif j < 7:
                            n = j - 4
                            width = HALF if n < 2 else C
                            cols = slice(n * HALF, n * HALF + width)
                            products(ps[:, bank, 0:width], [(*w(gg, 4), ckvh[:, cols], ckvl[:, cols], None)], pp_done)
                        else:
                            tiles = range(4 * (j - 7), min(10, 4 * (j - 7) + 4))
                            for q, t in enumerate(tiles):
                                dst = ps[:, bank, q * P:(q + 1) * P]
                                a, b = ckvh[:, t * P:(t + 1) * P], ckvl[:, t * P:(t + 1) * P]
                                vw_h, vw_l = w(gg, 5)
                                nc.tensor.matmul(dst, a, vw_h, start=True, stop=False)
                                nc.tensor.matmul(dst, a, vw_l, start=False, stop=False)
                                last = nc.tensor.matmul(dst, b, vw_h, start=False, stop=True)
                            last.then_inc(pp_done, 1)
                    G8 = 16 * i + 8 * gg

                    def scores(u, j, cuts):
                        hd, q = u // 4, 2 * (u % 4) + j
                        qs = slice(q * P, (q + 1) * P)
                        for a, b in cuts:
                            dst = psf[:, j * KEYS + a:j * KEYS + b]
                            nc.tensor.matmul(dst, qh[:, hd, qs], kh[:, hd, a:b], start=True, stop=False)
                            nc.tensor.matmul(dst, qh[:, hd, qs], kl[:, hd, a:b], start=False, stop=False)
                            last = nc.tensor.matmul(dst, ql[:, hd, qs], kh[:, hd, a:b], start=False, stop=True)
                        return last

                    def scores_first(u):
                        if u >= 1:
                            pe.wait_ge(p_made, 2 * G8 + 2 * u)
                        scores(u, 0, ((0, 512), (512, 1024), (1024, 1280))).then_inc(s_done, 1)

                    def scores_second(u):
                        if u >= 1:
                            pe.wait_ge(p_made, 2 * G8 + 2 * u)
                        scores(u, 1, ((256, 768), (768, 1280)))

                    def scores_shared(u):
                        pe.wait_ge(p_made, 2 * G8 + 2 * u + 1)
                        scores(u, 1, ((0, 256),)).then_inc(s_done, 1)

                    def turn(u, jj):
                        if jj == 0:
                            pe.wait_ge(p_made, 2 * G8 + 2 * u + 2)
                        if 5 * u + jj >= 2:
                            pe.wait_ge(t_free, 5 * G8 + 5 * u + jj - 1)
                        for k in range(2):
                            for j in range(2):
                                last = nc.tensor.transpose(ps[:, 5 + (5 * u + jj) % 2, k * 256 + j * P:k * 256 + (j + 1) * P],
                                                           pr[:, u % 2, j, (2 * jj + k) * P:(2 * jj + k + 1) * P], idm[:, :])
                        last.then_inc(t_done, 1)

                    def weigh(u, jj):
                        pe.wait_ge(t_free, 5 * G8 + 5 * u + jj + 1)
                        if jj == 0 and u >= 1:
                            pe.wait_ge(o_made, G8 + u)
                        dst = ps[:, 7, 0:256]
                        slot = (5 * u + jj) % 4
                        for k in range(2):
                            t = 2 * jj + k
                            a, b = vh[:, t, u // 4, :], vl[:, t, u // 4, :]
                            nc.tensor.matmul(dst, a, pth[slot][:, k, :], start=(t == 0), stop=False)
                            nc.tensor.matmul(dst, a, ptl[slot][:, k, :], start=False, stop=False)
                            last = nc.tensor.matmul(dst, b, pth[slot][:, k, :], start=False, stop=(t == 9))
                        last.then_inc(pv_done, 1)

                    pe.wait_ge(pp_free, 4 + 20 * i + 10 * gg + 10)
                    scores_first(0)
                    scores_second(0)
                    scores_shared(0)
                    for u in range(8):
                        if u < 7:
                            scores_first(u + 1)
                        turn(u, 0)
                        turn(u, 1)
                        if u < 7:
                            scores_second(u + 1)
                        weigh(u, 0)
                        turn(u, 2)
                        if u < 7:
                            scores_shared(u + 1)
                        weigh(u, 1)
                        turn(u, 3)
                        weigh(u, 2)
                        turn(u, 4)
                        weigh(u, 3)
                        weigh(u, 4)

            def project(base, rows_hi, rows_lo, done, free, first):
                with pe.Fori(0, 4) as i:
                    for s in range(2):
                        pe.wait_ge(w_staged, base + 2 * i + s + 1)
                        for n in range(2):
                            pe.wait_ge(free, 4 * i + 2 * s + n + 1)
                            products(ps[:, 2 * s + n, :],
                                     [(*w(s, k), rows_hi[:, k, half(n)], rows_lo[:, k, half(n)], first(k, n) if s == 0 else None) for k in range(KT)], done)

            def norms(first, ssum):
                for c in range(first, first + 4):
                    pe.wait_ge(std_made, c)
                    mean_square(c, ssum, HALF, 6 + c % 2)

            def mlp(l, pre):
                with pe.Fori(0, NCHUNK) as j:
                    for s in range(4):
                        pe.wait_ge(w_staged, (W_MLP0, W_MLP1)[l] + 8 * j + s + 1)
                        for n in range(2):
                            pe.wait_ge(hid_free[l], 8 * j + 2 * s + n + 1)
                            products(ps[:, (2 * s + n) % 4, :],
                                     [(*w(s % 2, k), hh[:, k, half(n)], hl[:, k, half(n)], (pre_lo, pre + 8 * n + k + 1) if s == 0 else None)
                                      for k in range(KT)], hid_done[l])
                    for s in range(4):
                        pe.wait_ge(w_staged, (W_MLP0, W_MLP1)[l] + 8 * j + 4 + s + 1)
                        for n in range(2):
                            for m in range(2):
                                pe.wait_ge(acc_free[l], 16 * j + 4 * s + 2 * n + m + 1)
                                products(ps[:, 4 + 2 * n + m, :],
                                         [(*w(s % 2, 2 * k + m), hidh[:, k, half(n)], hidl[:, k, half(n)],
                                           (hid_lo[l], 8 * j + 2 * k + n + 1) if s == 0 and m == 0 else None) for k in range(HIDT)], acc_done[l])

            project(W_O, hh, hl, wo_done, wo_free, lambda k, n: (ol_made, k + 1))
            norms(N_POST1, mssum)
            mlp(0, A_MLP0)
            norms(N_POST2, mssum)
            def project_u(i, s, first):
                pe.wait_ge(w_staged, W_IN + 2 * i + s + 1)
                for n in range(2):
                    pe.wait_ge(wi_free, 4 * i + 2 * s + n + 1)
                    products(ps[:, 2 * (s % 2) + n, :],
                             [(*w(s % 2, k), hh[:, k, half(n)], hl[:, k, half(n)], (pre_lo, A_HY + 8 * n + k + 1) if first else None) for k in range(KT)], wi_done)

            def turn_u(i, s):
                pe.wait_ge(uc_made, 2 * i + s + 1)
                for n in range(2):
                    pe.wait_ge(ut_made, 4 * i + 2 * s + n + 1)
                    for q in range(4):
                        last = nc.tensor.transpose(ps[:, 4 + 2 * s + n, q * P:(q + 1) * P], uc[s][:, (4 * n + q) * P:(4 * n + q + 1) * P], idm[:, :])
                    last.then_inc(ut_done, 1)

            project_u(0, 0, True)
            with pe.Fori(0, 11) as i:
                project_u(i, 1, False)
                turn_u(i, 0)
                project_u(i, 2, False)
                turn_u(i, 1)
            project_u(11, 1, False)
            turn_u(11, 0)
            turn_u(11, 1)
            with pe.Fori(0, ORDERS) as o:
                for s in range(7):
                    pe.wait_ge(w_staged, W_CONV + 14 * o + s + 1)
                    cls = (s + 1) // 2
                    for n, tiles, rows, idx in transform_groups(s, False):
                        pe.wait_ge(cr_lo, 16 * o + 2 * cls + n + 1)
                        if cls == 1:
                            pe.wait_ge(cf_free, 16 * o + idx % 8 // 2 + 1)
                        elif cls > 1:
                            pe.wait_ge(cf_free, 16 * o + 4 * (cls - 1) + idx % 4 + 1)
                        products(ps[:, idx % 8, :], [(*w(s % 2, a), rg_hi[n][:, b, :], rg_lo[n][:, b, :], None) for a, b in zip(tiles, rows)], cf_done)
                pe.wait_ge(cf_free, 16 * o + 16)
                for s in range(7):
                    pe.wait_ge(w_staged, W_CONV + 14 * o + 7 + s + 1)
                    cls = (s + 1) // 2
                    for n, tiles, rows, idx in transform_groups(s, True):
                        pe.wait_ge(cr_lo, 16 * o + 8 + 2 * cls + n + 1)
                        pe.wait_ge(ci_free, 32 * o + idx + 1)
                        products(ps[:, idx % 8, :], [(*w((7 + s) % 2, a), rg_hi[n][:, b, :], rg_lo[n][:, b, :], None) for a, b in zip(tiles, rows)], ci_done)
            for g in range(16):
                pe.wait_ge(z_made, 2)
                if g == 0:
                    pe.wait_ge(ci_free, 8 + 32 * ORDERS)
                if g >= 4:
                    pe.wait_ge(z_lo, g - 3)
                for j in range(4):
                    tt = 4 * (g % 2) + j
                    last = nc.tensor.transpose(ps[:, g % 4, j * P:(j + 1) * P], src[:, tt // 2, tt % 2, (g // 2) * P:(g // 2 + 1) * P], idm[:, :])
                last.then_inc(zt_done, 1)
            project(W_OUT, zh, zl, ho_done, ho_free, lambda k, n: (z_lo, 2 * k + n + 1))
            norms(N_POSTH, mssum)
            mlp(1, A_MLP1)
            for c in range(N_POSTM, N_POSTM + 2):
                pe.wait_ge(std_made, c)
                mean_square(c, mssum, HALF, 6 + c % 2)
            for g in range(16):
                if g < 2:
                    pe.wait_ge(post_x, B_MLP1 + 16)
                if g >= 4:
                    pe.wait_ge(out_made, g - 3)
                for j in range(4):
                    last = nc.tensor.transpose(ps[:, g % 4, j * P:(j + 1) * P], xm[:, 4 * (g % 2) + j, (g // 2) * P:(g // 2 + 1) * P], idm[:, :])
                last.then_inc(out_done, 1)

        @blk.scalar
        def _(act):
            ac = Chain(act, act_chain)

            def square(c, sq, source, ready):
                if ready:
                    act.wait_ge(*ready)
                if c:
                    act.wait_ge(sum_made, c)
                nc.scalar.activation(sq, source, ACT.Square).then_inc(sq_made, 1)

            def root(c, std, bank, width, count):
                act.wait_ge(ms_made, c + 1)
                if c:
                    act.wait_ge(rstd_made, c)
                nc.scalar.activation(std[:, 0:width], ps[:, bank, 0:width], ACT.Sqrt, bias=eps[:, 0:1], scale=1.0 / count).then_inc(std_made, 1)

            def pre_high(it, dst, tmp, shift):
                act.wait_ge(pre_t, it + 1)
                nc.scalar.activation(dst, tmp, ACT.Identity, bias=shift).then_inc(pre_hi, 1)

            act.wait_ge(vec_made, 1)
            nc.scalar.activation(sile[:, :], vec[:, V_C:V_C + 16], ACT.Exp, scale=-1.0).then_inc(sil_exp, 1)
            for l in range(2):
                act.wait_ge(hd_arg, l + 1)
                nc.scalar.activation((hd1, hd2)[l][:, :], hda[:, :], ACT.Sin).then_inc(hd_sin, 1)
            act.sem_inc(fs_free, 4)
            with act.Fori(0, ORDERS) as o:
                sent = [0] * 4

                def high(r):
                    act.wait_ge(fr_val, 16 * o + r + 1)
                    if r >= 2:
                        act.wait_ge(fs_done, FS_PER * o + RING_END[r - 2])
                    nc.scalar.activation(rg_hi[r % 2][:, :, :], val[r % 2][:, :, :], ACT.Copy).then_inc(fr_hi, 1)

                high(0)
                high(1)
                idx = 0
                for r in range(16):
                    c, n = RING[r % 8]
                    for _, _, f, plane in (s_groups if r < 8 else d_groups)(c):
                        q = idx % 4
                        act.wait_ge(fs_done, FS_PER * o + idx + 1)
                        if sent[q]:
                            act.wait_ge(ko_out[q], 16 * (KO_USES[q] * o + sent[q]))
                        if (f, plane) == (0, 1):
                            inst = nc.scalar.activation(ko[q][:, :], ps[:, q, :], ACT.Copy, scale=notop[:, 0:1])
                        else:
                            inst = nc.scalar.activation(ko[q][:, :], ps[:, q, :], ACT.Copy)
                        inst.then_inc(fs_free, 1)
                        act.wait_ge(fs_free, 4 + FS_PER * o + idx + 1)
                        if plane == 2:
                            act.wait_ge(ko_out[before], 16 * (KO_USES[before] * o + sent[before]))
                            act.dma_start(spec[bass.ds(((8 * o + f) * 3 + 2) * P, 1), half(n)], ko[q][0:1, :]).then_inc(ko_out[q], 16)
                            sent[q] += 1
                        else:
                            for pl in ((0, 2) if (f, plane) == (0, 0) else (plane,)):
                                act.dma_start(spec[bass.ds(((8 * o + f) * 3 + pl) * P, P), half(n)], ko[q][:, :]).then_inc(ko_out[q], 16)
                                sent[q] += 1
                        before = q
                        idx += 1
                    if r + 2 < 16:
                        high(r + 2)
                assert sent == KO_USES
                for q in range(4):
                    act.wait_ge(ko_out[q], 16 * (KO_USES[q] * o + KO_USES[q]))
            for n in range(2):
                square(N_LAT + n, asq[:, :, :], xa[:, :, half(n)], (xt_free, 15 + n))
                root(N_LAT + n, astd, 6 + n, HALF, D)
                for k in range(KT):
                    it = A_LAT + 8 * n + k
                    pre_high(it, hh[:, k, half(n)], atmp[it % 2][:, :], mod[:, k:k + 1])
            square(N_CTX, asq[:, :, 0:C], xc[:, :, :], (xt_free, 20))
            root(N_CTX, astd, 6, C, D)
            for k in range(KT):
                it = A_CTX + k
                pre_high(it, hch[:, k, :], atmp[it % 2][:, 0:C], mod[:, 48 + k:49 + k])
            for n in range(2):
                square(N_CQ + n, csq[:, :, :], cq[:, :, half(n)], (dn_free, 4))
                root(N_CQ + n, cstd, 6 + (n + 1) % 2, HALF, QR)
            for n in range(3):
                width = HALF if n < 2 else C
                cols = slice(n * HALF, n * HALF + width)
                square(N_CKV + n, csq[:, 0, 0:width], ckv[:, cols], (dn_free, 7))
                root(N_CKV + n, cstd, 6 + (n + 1) % 2, width, KVR)
            for k in range(2):
                act.wait_ge(cn_val, k + 1)
                nc.scalar.activation(cqh[:, k, :], cq[:, k, :], ACT.Copy).then_inc(cn_hi, 1)
            act.wait_ge(cn_val, 3)
            nc.scalar.activation(ckvh[:, :], ckv[:, :], ACT.Copy).then_inc(cn_hi, 1)
            for c in range(3):
                width = HALF if c < 2 else C
                cols = slice(c * HALF, c * HALF + width)
                act.wait_ge(kr_done, c + 1)
                for hd in range(2):
                    nc.scalar.activation(kh[NOPE:P, hd, cols], ps[NOPE:P, 3 + c, 0:width], ACT.Copy).then_inc(kr_hi, 1)
            with act.Fori(0, HEADS // 4) as i:
                for gg in range(2):
                    G8 = 16 * i + 8 * gg
                    for j in range(10):
                        bank = j % 4
                        if j < 4:
                            act.wait_ge(q_val, 8 * i + 4 * gg + j + 1)
                            nc.scalar.activation(qh[:, j // 2, half(j % 2)], qf[j % 2][:, :], ACT.Copy).then_inc(pp_hi, 1)
                            continue
                        act.wait_ge(pp_done, 20 * i + 10 * gg + j + 1)
                        if j < 7:
                            width = HALF if j < 6 else C
                            cols = slice((j - 4) * HALF, (j - 4) * HALF + width)
                            for hd in range(2):
                                nc.scalar.activation(kh[0:NOPE, hd, cols], ps[NOPE * hd:NOPE * hd + NOPE, bank, 0:width], ACT.Copy).then_inc(pp_hi, 1)
                        else:
                            t0 = 4 * (j - 7)
                            nt = min(10, t0 + 4) - t0
                            nc.scalar.activation(vh[:, t0:t0 + nt, :, 0:VD].rearrange("p t h v -> p (t h) v"),
                                                 ps[:, bank, 0:nt * P].rearrange("p (g v) -> p g v", v=VD), ACT.Copy).then_inc(pp_hi, 1)

                    def weights_of(u, j):
                        act.wait_ge(max_made, 2 * G8 + 2 * u + j + 1)
                        if u >= 2:
                            act.wait_ge(t_done, 5 * G8 + 5 * (u - 1))
                        a = 2 * (u % 2) + j
                        nc.scalar.activation(pr[:, u % 2, j, :], psf[:, j * KEYS:(j + 1) * KEYS], ACT.Exp, bias=mx[:, a:a + 1], scale=SCALE).then_inc(p_made, 1)

                    def turned_high(u, jj):
                        idx = 5 * u + jj
                        act.wait_ge(t_done, 5 * G8 + idx + 1)
                        if idx >= 4:
                            act.wait_ge(pv_done, 5 * G8 + idx - 3)
                        nc.scalar.activation(pth[idx % 4][:, :, :], ps[:, 5 + idx % 2, :].rearrange("p (k q) -> p k q", k=2), ACT.Copy).then_inc(t_hi, 1)

                    weights_of(0, 0)
                    weights_of(0, 1)
                    for u in range(8):
                        turned_high(u, 0)
                        turned_high(u, 1)
                        if u < 7:
                            weights_of(u + 1, 0)
                        turned_high(u, 2)
                        if u < 7:
                            weights_of(u + 1, 1)
                        turned_high(u, 3)
                        turned_high(u, 4)
            act.wait_ge(o_made, 64)
            for k in range(KT):
                nc.scalar.activation(hh[:, k, :], ao[:, k, :], ACT.Copy).then_inc(oh_made, 1)

            def post_then_pre(post, pre, items, shift, ready):
                for n in range(2):
                    square(post + n, msq[:, :, :], y[:, :, half(n)], ready)
                    root(post + n, mstd, 6 + (post + n) % 2, HALF, D)
                if pre is None:
                    return
                for n in range(2):
                    square(pre + n, msq[:, :, :], xm[:, :, half(n)], (post_x, {N_PRE2: B_ATT, N_PREH: B_MLP0, N_PREM: B_HY}[pre] + 8 * n + 8))
                    root(pre + n, mstd, 6 + (pre + n) % 2, HALF, D)
                    for k in range(KT):
                        it = items + 8 * n + k
                        pre_high(it, hh[:, k, half(n)], mtmp[it % 2][:, :], mod[:, shift + k:shift + k + 1])

            def mlp(l):
                with act.Fori(0, NCHUNK) as j:
                    for g in range(8):
                        act.wait_ge(hid_free[l], 4 + 8 * j + g + 1)
                        if g >= 2:
                            act.wait_ge(hid_lo[l], 8 * j + g - 1)
                        nc.scalar.activation(ms2[g % 2][:, :], mr[g % 2][:, :], ACT.Square).then_inc(hid_sq[l], 1)
                        act.wait_ge(hid_sq[l], 8 * j + g + 1)
                        nc.scalar.activation(hidh[:, g // 2, half(g % 2)], ms2[g % 2][:, :], ACT.Copy).then_inc(hid_hi[l], 1)
                    act.wait_ge(acc_done[l], 16 * j + 16)

            post_then_pre(N_POST1, N_PRE2, A_MLP0, 24, (wo_free, 4 + 16))
            mlp(0)
            post_then_pre(N_POST2, N_PREH, A_HY, 64, (acc_free[0], 4 + 16 * NCHUNK))

            def send_u(i, s):
                act.wait_ge(ut_made, 4 + 4 * i + 2 * s + 2)
                act.dma_start(u_tm[bass.ds(2 * i + s, 1)].rearrange("m (a p) c -> (m p) a c", p=P), ut[s][:, :, :]).then_inc(ut_out[s], 16)

            def middle(i, s, first):
                act.wait_ge(wi_free, 4 + 4 * i + 2 * s + 2)
                if not first:
                    act.wait_ge(ut_done, 4 * i + 2 * s - 2)
                nc.scalar.activation(uc[s][:, :], ub[s][:, 1:T + 1], ACT.Identity, bias=vec[:, bass.ds(V_BSH + 2 * i + s, 1)],
                                     scale=vec[:, bass.ds(V_WSH + 24 + 2 * i + s, 1)]).then_inc(uc_mid, 1)

            middle(0, 0, True)
            middle(0, 1, True)
            send_u(0, 0)
            with act.Fori(1, 12) as i:
                middle(i, 0, False)
                send_u(i - 1, 1)
                middle(i, 1, False)
                send_u(i, 0)
            send_u(11, 1)
            act.sem_inc(ci_free, 8)
            with act.Fori(0, ORDERS) as o:
                def high(r, *read):
                    act.wait_ge(cr_val, 8 * o + r + 1)
                    if read:
                        act.wait_ge(*read)
                    nc.scalar.activation(rg_hi[r % 2][:, :, :], val[r % 2][:, :, :], ACT.Copy).then_inc(cr_hi, 1)

                for r, (c, n) in enumerate(RING):
                    high(r, *((cf_done, 32 * o + ring_read(c - 1, n)) if c else ()))

                def high_inverse(c, n):
                    if c == 0:
                        act.wait_ge(cf_done, 32 * o + ring_read(3, n))
                    else:
                        act.wait_ge(ci_done, 32 * o + ring_read(c - 1, n))
                    act.wait_ge(pz_made, 16 * o + 4 * c + 2 * n + 2)
                    nc.scalar.activation(rg_hi[n][:, :, :], pz[:, c, :, half(n)], ACT.Copy).then_inc(cr_hi, 1)

                high_inverse(0, 0)
                high_inverse(0, 1)
                for s in range(7):
                    c = (s + 1) // 2
                    for n, _, _, idx in transform_groups(s, True):
                        plane = idx % 4 if c == 0 else 2 * (1 - s % 2) + idx % 2
                        act.wait_ge(ci_done, 32 * o + idx + 1)
                        nc.scalar.activation(pz[:, c, plane, half(n)], ps[:, idx % 8, :], ACT.Copy).then_inc(ci_free, 1)
                        if c < 3 and idx + 1 == ring_read(c, n):
                            high_inverse(c + 1, n)
            for g in range(16):
                act.wait_ge(zt_done, g + 1)
                nc.scalar.activation(zh[:, g // 2, half(g % 2)], ps[:, g % 4, :], ACT.Copy).then_inc(z_hi, 1)
            post_then_pre(N_POSTH, N_PREM, A_MLP1, 64 + 24, (ho_free, 4 + 16))
            mlp(1)
            post_then_pre(N_POSTM, None, None, None, (acc_free[1], 4 + 16 * NCHUNK))

        @blk.vector
        def _(dve):
            dv = Chain(dve, dve_chain)
            tt, ts, stt = nc.vector.tensor_tensor, nc.vector.tensor_scalar, nc.vector.scalar_tensor_tensor

            def root_mean(c, sq, ssum, std, rstd, width):
                dve.wait_ge(sq_made, c + 1)
                if c:
                    dve.wait_ge(ms_made, c)
                nc.vector.tensor_reduce(ssum[:, 0:width], sq.rearrange("p k t -> p t k"), AXX, ALU.add).then_inc(sum_made, 1)
                dve.wait_ge(std_made, c + 1)
                nc.vector.reciprocal(rstd, std[:, 0:width]).then_inc(rstd_made, 1)
                dve.wait_ge(rstd_made, c + 1)

            def pre_apply(items, src_of, tmp_of, hi_of, lo_of, factor, rstd, shift):
                def low(it, k):
                    dve.wait_ge(pre_hi, it + 1)
                    stt(lo_of(k), tmp_of(it), shift(k), hi_of(k), ALU.add, ALU.subtract).then_inc(pre_lo, 1)

                for k in range(KT):
                    it = items + k
                    if it >= 2:
                        dve.wait_ge(pre_lo, it - 1)
                    stt(tmp_of(it), src_of(k), factor(k), rstd, ALU.mult, ALU.mult).then_inc(pre_t, 1)
                    if k:
                        low(it - 1, k - 1)
                low(items + KT - 1, KT - 1)

            nc.vector.memset(ones[:, :], 1.0).then_inc(ones_made, 1)
            dv.did(nc.vector.memset(eps[:, :], EPS))
            dv.did(nc.vector.memset(notop[:, :], 1.0))
            dv.wait()
            dv.did(nc.vector.memset(notop[0:1, :], 0.0))
            dve.wait_ge(vec_t, 1)
            nc.vector.tensor_copy(vec[:, :], ps[:, 0, 0:NVEC]).then_inc(vec_made, 1)
            dve.wait_ge(vec_made, 1)
            dve.wait_ge(sil_exp, 1)
            dv.did(ts(sile[:, :], sile[:, :], 1.0, None, ALU.add))
            dv.wait()
            dv.did(nc.vector.reciprocal(sile[:, :], sile[:, :]))
            dv.wait()
            dv.did(tt(sil[:, :], sile[:, :], vec[:, V_C:V_C + 16], ALU.mult))
            dv.wait()
            n = 0
            for l in range(2):
                if l:
                    dve.wait_ge(ada_sum, 1)
                for k in range(KT):
                    for h in range(2):
                        dve.wait_ge(ada_in[n % 2], 16 * (n // 2 + 1))
                        if k:
                            dve.wait_ge(ada_acc, n - 1)
                        if l == 0 and h == 0:
                            if k == 0:
                                dv.did(ts(aaccc[:, :], araw[n % 2][:, 0:2 * D], sil[:, 8 + k:9 + k], None, ALU.mult))
                            else:
                                dv.wait()
                                dv.did(stt(aaccc[:, :], araw[n % 2][:, 0:2 * D], sil[:, 8 + k:9 + k], aaccc[:, :], ALU.mult, ALU.add))
                        acc = aacc[:, h * 3 * D:(h + 1) * 3 * D]
                        if k == 0:
                            ts(acc, araw[n % 2][:, :], sil[:, k:k + 1], None, ALU.mult).then_inc(ada_acc, 1)
                        else:
                            stt(acc, araw[n % 2][:, :], sil[:, k:k + 1], acc, ALU.mult, ALU.add).then_inc(ada_acc, 1)
                        n += 1
                dve.wait_ge(ada_sum, l + 1)
                lo, hi = (0, 48) if l == 0 else (64, 112)
                dv.did(tt(mod[:, lo:hi], ps[:, 1, lo:hi], vec[:, V_ADAB + 48 * l:V_ADAB + 48 * l + 48], ALU.add))
                if l == 0:
                    dv.did(tt(mod[:, 48:64], ps[:, 1, 48:64], vec[:, V_ADAB:V_ADAB + 16], ALU.add))
                dv.wait()
                m, g = 64 * l, V_NORMG + 32 * l
                for j, col in ((0, 8), (2, 32)):
                    dv.did(stt(fac[:, 32 * l + 8 * j:32 * l + 8 * j + 8], mod[:, m + col:m + col + 8], 1.0, vec[:, g + 8 * j:g + 8 * j + 8], ALU.add, ALU.mult))
                for j, col in ((1, 16), (3, 40)):
                    dv.did(tt(fac[:, 32 * l + 8 * j:32 * l + 8 * j + 8], mod[:, m + col:m + col + 8], vec[:, g + 8 * j:g + 8 * j + 8], ALU.mult))
                if l == 0:
                    dv.did(stt(fac[:, 64:72], mod[:, 56:64], 1.0, vec[:, g:g + 8], ALU.add, ALU.mult))
            dv.wait()
            MAGIC = 12582912.0
            C1 = 6.28125
            C2 = float(np.float32(2 * math.pi - C1))
            C3 = 2 * math.pi - C1 - C2
            PI = float(np.nextafter(np.float32(math.pi), np.float32(0)))
            for l in range(2):
                dve.wait_ge(hd_done, l + 1)
                if l:
                    dve.wait_ge(hd_sin, 1)
                dv.did(ts(hda[:, :], ps[0:FH, 2:4, :].rearrange("p b n -> p (b n)"), vec[0:FH, V_FB1 + l:V_FB1 + l + 1], vec[0:FH, V_FREQ:V_FREQ + 1], ALU.add, ALU.mult))
                dv.wait()
                dv.did(ts(hdn[:, :], hda[:, :], 1 / (2 * math.pi), MAGIC, ALU.mult, ALU.add))
                dv.wait()
                dv.did(ts(hdn[:, :], hdn[:, :], MAGIC, None, ALU.subtract))
                for part in (C1, C2, C3):
                    dv.wait()
                    dv.did(stt(hda[:, :], hdn[:, :], -part, hda[:, :], ALU.mult, ALU.add))
                dv.wait()
                ts(hda[:, :], hda[:, :], PI, -PI, ALU.min, ALU.max).then_inc(hd_arg, 1)
            dve.sem_inc(hf_free, 4)

            def operand(c, n, x4, v, made):
                q, s, x0, x2 = bq[:, :, half(n)], bs[:, :, half(n)], x4[:, 0, :, half(n)], x4[:, 2, :, half(n)]
                re, im = v[:, 0:2, :], v[:, 2:4, :]
                if c == 0:
                    dv.did(tt(re, x0, x2, ALU.add))
                    dv.wait()
                    dv.did(tt(im, re, q, ALU.subtract))
                    dv.wait()
                    tt(re, re, q, ALU.add).then_inc(made, 1)
                elif c == 2:
                    dv.did(tt(re, x0, x2, ALU.subtract))
                    nc.vector.tensor_copy(im, s).then_inc(made, 1)
                else:
                    r4 = R4 if c == 1 else -R4
                    dv.did(stt(re, s, r4, x0, ALU.mult, ALU.add))
                    stt(im, q, R4, x2, ALU.mult, ALU.add if c == 1 else ALU.subtract).then_inc(made, 1)

            def butterflies(x4, ready):
                if ready:
                    dve.wait_ge(*ready)
                dv.did(tt(bq[:, :, :], x4[:, 1, :, :], x4[:, 3, :, :], ALU.add))
                dv.did(tt(bs[:, :, :], x4[:, 1, :, :], x4[:, 3, :, :], ALU.subtract))
                dv.wait()

            with dve.Fori(0, ORDERS) as o:
                dv.enter(o, 2 + 16 + 2 * (2 + 10))
                for t in range(TT):
                    dve.wait_ge(dec_in[t % 2], 16 * (4 * o + t // 2 + 1))
                    for j in range(4):
                        dve.wait_ge(hf_done, 32 * o + 4 * t + j + 1)
                        tt(fb[:, j // 2, half(j % 2)], ps[:, 4 + j, :], dec[t % 2][:, half(j % 2)], ALU.mult).then_inc(hf_free, 1)
                    dve.wait_ge(hf_free, 4 + 32 * o + 4 * t + 4)
                    if t == 0:
                        dv.did(nc.vector.memset(fb[0:1, 1, :], 0.0))
                        dv.did(tt(fb[0:1, 0, :], fb[0:1, 0, :], fbias[0:1, bass.ds(o * D, D)], ALU.add))
                        dv.wait()
                    dv.did(tt(f_s[:, t // 2, t % 2, :], fb[:, 0, :], fb[:, 1, :], ALU.add))
                    dv.did(tt(f_d[:, t // 2, t % 2, :], fb[:, 0, :], fb[:, 1, :], ALU.subtract))
                    dv.wait()
                for rnd, x4 in ((0, f_s), (1, f_d)):
                    butterflies(x4, (fr_lo, 16 * o + 8) if rnd else None)

                    def low(r):
                        dve.wait_ge(fr_hi, 16 * o + 8 * rnd + r + 1)
                        tt(rg_lo[r % 2][:, :, :], val[r % 2][:, :, :], rg_hi[r % 2][:, :, :], ALU.subtract).then_inc(fr_lo, 1)

                    operand(*RING[0], x4, val[0], fr_val)
                    operand(*RING[1], x4, val[1], fr_val)
                    for r in range(8):
                        low(r)
                        if r + 2 < 8:
                            dve.wait_ge(fr_lo, 16 * o + 8 * rnd + r + 1)
                            operand(*RING[r + 2], x4, val[r % 2], fr_val)
                dve.wait_ge(fr_lo, 16 * o + 16)
                dv.leave(ORDERS)
            for g in range(20):
                dve.wait_ge(xt_done, g + 1)
                if g < 16:
                    nc.vector.tensor_copy(xa[:, g // 2, half(g % 2)], ps[:, g % 4, :]).then_inc(xt_free, 1)
                else:
                    nc.vector.tensor_copy(xc[:, 2 * (g - 16):2 * (g - 16) + 2, :], ps[:, g % 4, :].rearrange("p (k t) -> p k t", k=2)).then_inc(xt_free, 1)
            for n in range(2):
                rs = arstd[:, half(n)]
                root_mean(N_LAT + n, asq[:, :, :], assum, astd, rs, HALF)
                pre_apply(A_LAT + 8 * n, lambda k: xa[:, k, half(n)], lambda it: atmp[it % 2][:, :], lambda k: hh[:, k, half(n)],
                          lambda k: hl[:, k, half(n)], lambda k: fac[:, k:k + 1], rs, lambda k: mod[:, k:k + 1])
            rs = arstd[:, T:KEYS]
            root_mean(N_CTX, asq[:, :, 0:C], assum, astd, rs, C)
            pre_apply(A_CTX, lambda k: xc[:, k, :], lambda it: atmp[it % 2][:, 0:C], lambda k: hch[:, k, :], lambda k: hcl[:, k, :],
                      lambda k: fac[:, 64 + k:65 + k], rs, lambda k: mod[:, 48 + k:49 + k])
            g = 0
            dve.wait_ge(tab_in, 32)
            for s in range(4):
                for n in range(3 if s >= 2 else 2):
                    width = HALF if n < 2 else C
                    cols = slice(n * HALF, n * HALF + width)
                    dve.wait_ge(dn_done, g + 1)
                    bank = ps[:, g % 6, 0:width]
                    if s < 2:
                        nc.vector.tensor_copy(cq[:, s, cols], bank).then_inc(dn_free, 1)
                    elif s == 2:
                        nc.vector.tensor_copy(ckv[:, cols], bank).then_inc(dn_free, 1)
                    else:
                        tt(krt[:, cols], bank, rtab[:, cols], ALU.mult).then_inc(dn_free, 1)
                    g += 1
            dve.wait_ge(dn_free, 10)
            dve.sem_inc(kr_made, 3)
            for n in range(2):
                root_mean(N_CQ + n, csq[:, :, :], cssum, cstd, crstd[:, half(n)], HALF)
            for k in range(2):
                stt(cq[:, k, :], cq[:, k, :], vec[:, V_GQ + k:V_GQ + k + 1], crstd[:, 0:T], ALU.mult, ALU.mult).then_inc(cn_val, 1)
            dve.wait_ge(cn_val, 2)
            for n in range(3):
                width = HALF if n < 2 else C
                root_mean(N_CKV + n, csq[:, 0:1, 0:width], cssum, cstd, crstd[:, n * HALF:n * HALF + width], width)
            stt(ckv[:, :], ckv[:, :], vec[:, V_GKV:V_GKV + 1], crstd[:, :], ALU.mult, ALU.mult).then_inc(cn_val, 1)
            for k in range(2):
                dve.wait_ge(cn_hi, k + 1)
                tt(cql[:, k, :], cq[:, k, :], cqh[:, k, :], ALU.subtract).then_inc(cn_lo, 1)
            dve.wait_ge(cn_hi, 3)
            dve.wait_ge(cn_val, 3)
            tt(ckvl[:, :], ckv[:, :], ckvh[:, :], ALU.subtract).then_inc(cn_lo, 1)
            nc.vector.memset(vh[:, :, :, VD:P].bitcast(F32), 1.0).then_inc(cn_lo, 1)
            nc.vector.memset(vl[:, :, :, VD:P].bitcast(F32), 0.0).then_inc(cn_lo, 1)
            for c in range(3):
                width = HALF if c < 2 else C
                cols = slice(c * HALF, c * HALF + width)
                for hd in range(2):
                    dve.wait_ge(kr_hi, 2 * c + 2)
                    tt(kl[NOPE:P, hd, cols], ps[NOPE:P, 3 + c, 0:width], kh[NOPE:P, hd, cols], ALU.subtract).then_inc(kr_lo, 1)
            dve.wait_ge(kr_lo, 6)
            dve.wait_ge(x_saved, 16)
            dve.sem_inc(pp_free, 4)
            with dve.Fori(0, HEADS // 4) as i:
                for gg in range(2):
                    G8 = 16 * i + 8 * gg
                    pp = 20 * i + 10 * gg

                    def query_low(j):
                        dve.wait_ge(pp_hi, 26 * i + 13 * gg + j + 1)
                        tt(ql[:, j // 2, half(j % 2)], qf[j % 2][:, :], qh[:, j // 2, half(j % 2)], ALU.subtract).then_inc(q_lo, 1)

                    for j in range(4):
                        dve.wait_ge(pp_done, pp + j + 1)
                        if j >= 2:
                            dve.wait_ge(q_lo, 8 * i + 4 * gg + j - 1)
                        tt(qf[j % 2][:, :], ps[:, j % 4, :], rtab[:, half(j % 2)], ALU.mult).then_inc(q_val, 1)
                        dve.wait_ge(q_val, 8 * i + 4 * gg + j + 1)
                        dve.sem_inc(pp_free, 1)
                        if j:
                            query_low(j - 1)
                    query_low(3)
                    for j in range(4, 7):
                        width = HALF if j < 6 else C
                        cols = slice((j - 4) * HALF, (j - 4) * HALF + width)
                        for hd in range(2):
                            dve.wait_ge(pp_hi, 26 * i + 13 * gg + 4 + 2 * (j - 4) + 2)
                            inst = tt(kl[0:NOPE, hd, cols], ps[NOPE * hd:NOPE * hd + NOPE, j % 4, 0:width], kh[0:NOPE, hd, cols], ALU.subtract)
                            inst.then_inc(pp_free if hd else k_lo, 1)
                    for j in range(7, 10):
                        t0 = 4 * (j - 7)
                        nt = min(10, t0 + 4) - t0
                        dve.wait_ge(pp_hi, 26 * i + 13 * gg + 10 + (j - 7) + 1)
                        tt(vl[:, t0:t0 + nt, :, 0:VD].rearrange("p t h v -> p (t h) v"), ps[:, j % 4, 0:nt * P].rearrange("p (g v) -> p g v", v=VD),
                           vh[:, t0:t0 + nt, :, 0:VD].rearrange("p t h v -> p (t h) v"), ALU.subtract).then_inc(pp_free, 1)

                    def maximum(u, j):
                        a = 2 * (u % 2) + j
                        dve.wait_ge(s_done, 2 * G8 + 2 * u + j + 1)
                        if u >= 2:
                            dve.wait_ge(p_made, 2 * G8 + 2 * u + j - 3)
                        nc.vector.reduce_max(mxr[:, a:a + 1], psf[:, j * KEYS:(j + 1) * KEYS], AXX).then_inc(raw_max, 1)
                        dve.wait_ge(raw_max, 2 * G8 + 2 * u + j + 1)
                        ts(mx[:, a:a + 1], mxr[:, a:a + 1], -SCALE, None, ALU.mult).then_inc(max_made, 1)

                    def turned_low(u, jj):
                        idx = 5 * u + jj
                        dve.wait_ge(t_hi, 5 * G8 + idx + 1)
                        tt(ptl[idx % 4][:, :, :], ps[:, 5 + idx % 2, :].rearrange("p (k q) -> p k q", k=2), pth[idx % 4][:, :, :], ALU.subtract).then_inc(t_free, 1)

                    def result(u):
                        dve.wait_ge(pv_done, 5 * G8 + 5 * u + 5)
                        nc.vector.reciprocal(rc[0:VD, :], ps[VD:P, 7, 0:256]).then_inc(rc_made, 1)
                        dve.wait_ge(rc_made, G8 + u + 1)
                        hd, q = u // 4, u % 4
                        tt(ao[VD * hd:VD * hd + VD, bass.ds(2 * i + gg, 1), q * 256:(q + 1) * 256], ps[0:VD, 7:8, 0:256],
                           rc[0:VD, :].rearrange("p (a q) -> p a q", a=1), ALU.mult).then_inc(o_made, 1)

                    maximum(0, 0)
                    maximum(0, 1)
                    for u in range(8):
                        if u < 7:
                            maximum(u + 1, 0)
                        turned_low(u, 0)
                        turned_low(u, 1)
                        turned_low(u, 2)
                        if u < 7:
                            maximum(u + 1, 1)
                        turned_low(u, 3)
                        turned_low(u, 4)
                        result(u)
            dve.wait_ge(o_made, 64)
            for k in range(KT):
                dve.wait_ge(oh_made, k + 1)
                tt(hl[:, k, :], ao[:, k, :], hh[:, k, :], ALU.subtract).then_inc(ol_made, 1)

            def post_apply(items, factor, rstd, n):
                for k in range(KT):
                    stt(y[:, k, half(n)], y[:, k, half(n)], factor(k), rstd, ALU.mult, ALU.mult).then_inc(post_y, 1)
                    if k:
                        dve.wait_ge(post_y, items + k)
                        tt(xm[:, k - 1, half(n)], xm[:, k - 1, half(n)], y[:, k - 1, half(n)], ALU.add).then_inc(post_x, 1)
                dve.wait_ge(post_y, items + KT)
                tt(xm[:, KT - 1, half(n)], xm[:, KT - 1, half(n)], y[:, KT - 1, half(n)], ALU.add).then_inc(post_x, 1)

            def post_then_pre(post, pre, b_items, a_items, f_post, f_pre, shift):
                for n in range(2):
                    rs = mrstd[:, half(n)]
                    root_mean(post + n, msq[:, :, :], mssum, mstd, rs, HALF)
                    post_apply(b_items + 8 * n, lambda k: fac[:, f_post + k:f_post + k + 1], rs, n)
                if pre is None:
                    return
                dve.wait_ge(post_x, b_items + 16)
                for n in range(2):
                    rs = mrstd[:, half(n)]
                    root_mean(pre + n, msq[:, :, :], mssum, mstd, rs, HALF)
                    pre_apply(a_items + 8 * n, lambda k: xm[:, k, half(n)], lambda it: mtmp[it % 2][:, :], lambda k: hh[:, k, half(n)],
                              lambda k: hl[:, k, half(n)], lambda k: fac[:, f_pre + k:f_pre + k + 1], rs, lambda k: mod[:, shift + k:shift + k + 1])

            def mlp(l):
                dv.did(nc.vector.memset(y[:, :, :], 0.0))
                dv.wait()
                dve.sem_inc(hid_free[l], 4)
                dve.sem_inc(acc_free[l], 4)
                with dve.Fori(0, NCHUNK) as j:
                    def low(g):
                        dve.wait_ge(hid_hi[l], 8 * j + g + 1)
                        tt(hidl[:, g // 2, half(g % 2)], ms2[g % 2][:, :], hidh[:, g // 2, half(g % 2)], ALU.subtract).then_inc(hid_lo[l], 1)

                    for g in range(8):
                        dve.wait_ge(hid_done[l], 8 * j + g + 1)
                        ts(mr[g % 2][:, :], ps[:, g % 4, :], 0.0, None, ALU.max).then_inc(hid_free[l], 1)
                        if g:
                            low(g - 1)
                    low(7)
                    dve.wait_ge(acc_free[l], 4 + 16 * j)
                    for q in range(16):
                        s, n, m = q // 4, q // 2 % 2, q % 2
                        dve.wait_ge(acc_done[l], 16 * j + q + 1)
                        dst = y[:, 2 * s + m, half(n)]
                        tt(dst, ps[:, 4 + 2 * n + m, :], dst, ALU.add).then_inc(acc_free[l], 1)
                dve.wait_ge(acc_free[l], 4 + 16 * NCHUNK)

            dve.sem_inc(wo_free, 4)
            with dve.Fori(0, 4) as i:
                for g in range(4):
                    dve.wait_ge(wo_done, 4 * i + g + 1)
                    nc.vector.tensor_copy(y[:, bass.ds(2 * i + g // 2, 1), half(g % 2)], ps[:, g:g + 1, :]).then_inc(wo_free, 1)
            dve.wait_ge(x_back, 16)
            post_then_pre(N_POST1, N_PRE2, B_ATT, A_MLP0, 8, 16, 24)
            mlp(0)
            post_then_pre(N_POST2, N_PREH, B_MLP0, A_HY, 24, 32, 64)
            for s in range(2):
                dv.did(nc.vector.memset(ub[s][:, 0:1], 0.0))
                dv.did(nc.vector.memset(ub[s][:, T + 1:T + 2], 0.0))
            dv.wait()
            dve.sem_inc(wi_free, 4)
            dve.sem_inc(ut_made, 4)

            def outer(i, s):
                dve.wait_ge(uc_mid, 2 * i + s + 1)
                stt(uc[s][:, :], ub[s][:, 0:T], vec[:, bass.ds(V_WSH + 2 * i + s, 1)], uc[s][:, :], ALU.mult, ALU.add).then_inc(uc_left, 1)
                dve.wait_ge(uc_left, 2 * i + s + 1)
                stt(uc[s][:, :], ub[s][:, 2:T + 2], vec[:, bass.ds(V_WSH + 48 + 2 * i + s, 1)], uc[s][:, :], ALU.mult, ALU.add).then_inc(uc_made, 1)

            def take(i, s, first):
                for n in range(2):
                    dve.wait_ge(ut_done, 4 * i + 2 * s + n + 1)
                    if not first:
                        dve.wait_ge(ut_out[s], 16 * i)
                    nc.vector.tensor_copy(ut[s][:, 4 * n:4 * n + 4, :], ps[:, 4 + 2 * s + n, :].rearrange("p (q c) -> p q c", q=4)).then_inc(ut_made, 1)

            def biased(i, s, first):
                for n in range(2):
                    dve.wait_ge(wi_done, 4 * i + 2 * s + n + 1)
                    if not first:
                        dve.wait_ge(uc_made, 2 * i + s - 1)
                    ts(ub[s][:, 1 + n * HALF:1 + (n + 1) * HALF], ps[:, 2 * s + n, :], vec[:, bass.ds(V_BIN + 2 * i + s, 1)], None, ALU.add).then_inc(wi_free, 1)

            biased(0, 0, True)
            outer(0, 0)
            biased(0, 1, True)
            take(0, 0, True)
            outer(0, 1)
            biased(1, 0, False)
            take(0, 1, True)
            outer(1, 0)
            with dve.Fori(1, 11) as i:
                biased(i, 1, False)
                take(i, 0, False)
                outer(i, 1)
                biased(i + 1, 0, False)
                take(i, 1, False)
                outer(i + 1, 0)
            biased(11, 1, False)
            take(11, 0, False)
            outer(11, 1)
            take(11, 1, False)
            dve.wait_ge(src_in, 16 * KT)
            with dve.Fori(0, ORDERS) as o:
                dv.enter(o, 2 + 10 + 16 * 4 + 14 + 4)

                def low(c, n):
                    dve.wait_ge(cr_hi, 16 * o + 2 * c + n + 1)
                    tt(rg_lo[n][:, :, :], val[n][:, :, :], rg_hi[n][:, :, :], ALU.subtract).then_inc(cr_lo, 1)

                def value(c, n):
                    if c:
                        dve.wait_ge(cr_lo, 16 * o + 2 * (c - 1) + n + 1)
                    operand(c, n, src, val[n], cr_val)

                def product(p):
                    f, n = pair_tile(p)
                    gr, gi = pair_groups(p)
                    c, m = f // 2, f % 2
                    re, im = (2 * m, 2 * m + 1) if c == 0 else (m, 2 + m)
                    k = ks[p % 2]
                    ur, ui = ps[:, gr % 8, :], ps[:, gi % 8, :]
                    pr_, pi_ = pz[:, c, re, half(n)], pz[:, c, im, half(n)]
                    dve.wait_ge(k_in[p % 2], 16 * (8 * o + p // 2 + 1))
                    if f == 0:
                        dve.wait_ge(k_ny_in, 16 * (2 * o + n + 1))
                    dve.wait_ge(cf_done, 32 * o + gi + 1)
                    dv.did(tt(pr_, ur, k[:, 0, :], ALU.mult))
                    dv.did(tt(pi_, ur, k[:, 1, :], ALU.mult))
                    dv.did(tt(pt[0][:, :], ui, k[:, 1, :], ALU.mult))
                    tt(pt[1][:, :], ui, k[:, 2 if f == 0 else 0, :], ALU.mult).then_inc(cf_free, 1)
                    dv.wait()
                    dv.did(tt(pr_, pr_, pt[0][:, :], ALU.subtract))
                    dve.wait_ge(cf_free, 16 * o + p + 1)
                    tt(pi_, pi_, pt[1][:, :], ALU.add).then_inc(pz_made, 1)
                    dve.wait_ge(pz_made, 16 * o + p + 1)
                    dv.wait()

                butterflies(src, None)
                value(0, 0)
                value(0, 1)
                low(0, 0)
                low(0, 1)
                value(1, 0)
                value(1, 1)
                for c in range(4):
                    for n in range(2):
                        product(4 * c + 2 * n)
                        if c < 3:
                            low(c + 1, n)
                        if c < 2:
                            value(c + 2, n)
                        product(4 * c + 2 * n + 1)
                for c in range(4):
                    for n in range(2):
                        dve.wait_ge(cr_hi, 16 * o + 8 + 2 * c + n + 1)
                        tt(rg_lo[n][:, :, :], pz[:, c, :, half(n)], rg_hi[n][:, :, :], ALU.subtract).then_inc(cr_lo, 1)
                dve.wait_ge(ci_free, 8 + 32 * o + 32)
                y0, y1, y2, y3 = (src[:, a, :, :] for a in range(4))
                z0, z4 = pz[:, 0, 0:2, :], pz[:, 0, 2:4, :]
                (r1, i1), (r2, i2), (r3, i3) = ((pz[:, c, 0:2, :], pz[:, c, 2:4, :]) for c in (1, 2, 3))
                dv.did(tt(y0, z0, z4, ALU.add))
                dv.did(tt(y1, z0, z4, ALU.subtract))
                dv.wait()
                dv.did(tt(z0, r1, r3, ALU.add))
                dv.did(tt(z4, r1, r3, ALU.subtract))
                dv.wait()
                dv.did(tt(r1, i1, i3, ALU.add))
                dv.did(tt(r3, i3, i1, ALU.subtract))
                dv.did(tt(y2, y0, r2, ALU.subtract))
                dv.wait()
                dv.did(tt(y0, y0, r2, ALU.add))
                dv.did(stt(i1, z4, R4, i2, ALU.mult, ALU.subtract))
                dv.wait()
                dv.did(stt(y1, r1, -R4, y1, ALU.mult, ALU.add))
                dv.did(tt(y0, y0, z0, ALU.add))
                dv.did(tt(y2, y2, r3, ALU.add))
                dv.wait()
                dv.did(tt(y3, y1, i1, ALU.subtract))
                dv.wait()
                dv.did(tt(y1, y1, i1, ALU.add))
                dv.wait()
                dve.wait_ge(gate_in, 16 * KT * (o + 1))
                for a in range(4):
                    dv.did(tt(src[:, a, :, :], src[:, a, :, :], gate[:, a, :, :], ALU.mult))
                dv.wait()
                dve.sem_inc(z_made, 1)
                dv.leave(ORDERS)
            for g in range(16):
                dve.wait_ge(z_hi, g + 1)
                tt(zl[:, g // 2, half(g % 2)], ps[:, g % 4, :], zh[:, g // 2, half(g % 2)], ALU.subtract).then_inc(z_lo, 1)
            dve.wait_ge(z_lo, 16)
            dve.sem_inc(ho_free, 4)
            with dve.Fori(0, 4) as i:
                for g in range(4):
                    dve.wait_ge(ho_done, 4 * i + g + 1)
                    ts(y[:, bass.ds(2 * i + g // 2, 1), half(g % 2)], ps[:, g:g + 1, :], vec[:, bass.ds(V_BOUT + 2 * i + g // 2, 1)], None, ALU.add).then_inc(ho_free, 1)
            dve.wait_ge(x_back, 32)
            post_then_pre(N_POSTH, N_PREM, B_HY, A_MLP1, 40, 48, 64 + 24)
            mlp(1)
            post_then_pre(N_POSTM, None, B_MLP1, None, 56, None, None)
            for g in range(16):
                t = g // 2
                dve.wait_ge(out_done, g + 1)
                if t >= 2:
                    dve.wait_ge(out_sent[t % 2], 16 * (t // 2))
                nc.vector.tensor_copy(ot[t % 2][:, half(g % 2)], ps[:, g % 4, :]).then_inc(out_made, 1)


def kernel(x, c, ctx, c_ctx, ada_w, ada_b, norm_g, mla_w_dq, mla_g_q, mla_w_uq, mla_w_dkv,
           mla_g_kv, mla_w_ukv, mla_w_o, hy_w_in, hy_b_in, hy_w_short, hy_b_short, hy_f_w1,
           hy_f_b1, hy_f_w2, hy_f_b2, hy_f_w3, hy_f_freq, hy_bias, hy_w_out, hy_b_out,
           mlp_w1, mlp_w2):
    import concourse.bacc as bacc
    from concourse.bass_utils import run_bass_kernel_spmd

    def arr(a):
        return np.ascontiguousarray(np.asarray(a))

    (x, c, ctx, c_ctx, ada_w, ada_b, norm_g, w_dq, g_q, w_uq, w_dkv, g_kv, w_ukv, w_o, w_in, b_in, w_sh, b_sh,
     f_w1, f_b1, f_w2, f_b2, f_w3, freq, hbias, w_out, b_out, w1, w2) = map(arr, (
         x, c, ctx, c_ctx, ada_w, ada_b, norm_g, mla_w_dq, mla_g_q, mla_w_uq, mla_w_dkv, mla_g_kv, mla_w_ukv,
         mla_w_o, hy_w_in, hy_b_in, hy_w_short, hy_b_short, hy_f_w1, hy_f_b1, hy_f_w2, hy_f_b2, hy_f_w3,
         hy_f_freq, hy_bias, hy_w_out, hy_b_out, mlp_w1, mlp_w2))

    def row(v):
        return np.concatenate([v.reshape(1, FH), np.zeros((1, P - FH), v.dtype)], axis=1)

    rows = [v.reshape(-1, P) for v in (ada_b, norm_g, b_in, w_sh, b_sh, b_out, g_q, g_kv, c, c_ctx)]
    rows += [row(f_b1), row(f_b2), row(freq)]
    used = sum(r.shape[0] for r in rows)
    vecs = np.concatenate(rows + [np.zeros((NVEC - used, P), x.dtype)], axis=0)

    kr = w_dkv[0][:, KVR:]
    swap = np.concatenate([kr[:, 16:], kr[:, :16]], axis=1)
    w_down = np.concatenate([w_dq[0], w_dkv[0][:, :KVR], w_dkv[0][:, :64], kr, swap], axis=1)

    uq = w_uq[0].reshape(2, P, HEADS, NOPE + ROPE)
    uq = np.concatenate([uq, uq[..., NOPE + 16:], uq[..., NOPE:NOPE + 16]], axis=3)
    ukv = w_ukv[0].reshape(P, HEADS, NOPE + VD)
    w_head = np.zeros((HEADS // 2, P, 8, P), x.dtype)
    for g in range(HEADS // 2):
        for k in range(2):
            for h in range(2):
                w_head[g, :, 2 * k + h] = uq[k, :, 2 * g + h]
        w_head[g, :, 4] = ukv[:, 2 * g:2 * g + 2, :NOPE].reshape(P, P)
        w_head[g, :, 5] = ukv[:, 2 * g:2 * g + 2, NOPE:].reshape(P, P)

    fwd, inv = dft_steps()
    ins = dict(x=x[0], ctx=ctx[0], vecs=vecs, ada_w=ada_w, w_down=w_down, w_head=w_head.reshape(HEADS // 2, P, 8 * P),
               w_o=w_o[0], w_in=w_in[0], w_out=w_out[0], mlp_w1=w1, mlp_w2=w2, f_w1=f_w1[0], f_w2=f_w2[0], f_w3=f_w3[0],
               hy_bias=hbias[0], rope=rope_table(), ropesum=rope_sum(), ident=np.eye(P, dtype=np.float32),
               zpos=filter_positions(), decay=filter_decay(), dft_fwd=fwd, dft_inv=inv)
    nc = bacc.Bacc("TRN2", target_bir_lowering=False, num_devices=1)
    arrays, aps = {}, {}
    for name, a in ins.items():
        a = np.ascontiguousarray(a)
        arrays[f"in_{name}"] = a
        aps[name] = nc.dram_tensor(f"in_{name}", a.shape, mybir.dt.from_np(a.dtype), kind="ExternalInput").ap()
    aps["out"] = nc.dram_tensor("out_y", (T, D), F32, kind="ExternalOutput").ap()
    build_program(nc, **aps)
    res = run_bass_kernel_spmd(nc, [arrays], core_ids=[0])
    return res.results[0]["out_y"].reshape(1, T, D)
```

```python
import math

import numpy as np

import concourse.bass as bass
import concourse.mybir as mybir

F32 = mybir.dt.float32
F32R = mybir.dt.float32r
ALU = mybir.AluOpType
ACT = mybir.ActivationFunctionType
AXX = mybir.AxisListType.X

P = 128
D = 1024
T = 1024
C = 256
KEYS = T + C
KT = D // P
TT = T // P
HALF = 512
HEADS = 16
NOPE, ROPE, VD = 64, 32, 64
QR, KVR = 256, 128
FF = 4 * D
CHUNK = 512
NCHUNK = FF // CHUNK
HIDT = CHUNK // P
EMB, FH = 33, 64
EPS = 1e-6
GRID_W, ROPE_BASE = 64, 10000.0
SCALE = 1.0 / math.sqrt(NOPE + ROPE)
ORDERS = 2
NFFT = 2 * T
R4 = math.sqrt(0.5)

V_ADAB = 0
V_NORMG = 96
V_BIN = 160
V_WSH = 184
V_BSH = 256
V_BOUT = 280
V_GQ = 288
V_GKV = 290
V_C = 291
V_CCTX = 299
V_FB1, V_FB2, V_FREQ = 307, 308, 309
NVEC = 384



def rope_table():
    t = np.arange(T)
    inv = ROPE_BASE ** (-np.arange(ROPE // 4) / (ROPE // 4))
    ang = np.concatenate([(t // GRID_W)[:, None] * inv, (t % GRID_W)[:, None] * inv], axis=1).T
    out = np.zeros((P, KEYS))
    out[:NOPE] = 1.0
    out[NOPE:NOPE + 16, :T] = out[NOPE + 16:NOPE + 32, :T] = np.cos(ang)
    out[NOPE + 32:NOPE + 48, :T] = -np.sin(ang)
    out[NOPE + 48:, :T] = np.sin(ang)
    out[NOPE:NOPE + 32, T:] = 1.0
    return out.astype(np.float32)


def rope_sum():
    m = np.zeros((P, P), np.float32)
    for j in range(ROPE):
        for o in (NOPE + j, NOPE + ROPE + j):
            m[NOPE + j, o] = m[NOPE + ROPE + j, o] = 1.0
    return m


def filter_positions():
    t = np.linspace(0.0, 1.0, T, dtype=np.float32).astype(np.float64)[:, None]
    w = (2.0 * math.pi) * np.arange(T)[:, None] / T
    f = np.linspace(1e-4, (EMB - 1) // 2 - 1, (EMB - 1) // 2)[None, :]
    return np.concatenate([t, np.cos(f * w), -np.sin(f * w)], axis=1).T.astype(np.float32).copy()


def filter_decay():
    t = np.linspace(0.0, 1.0, T)[:, None]
    deltas = np.linspace(math.log(1e-2) / 1.5, math.log(1e-2) / 0.3, D)
    return np.exp(-t * np.abs(deltas)[None, :]).astype(np.float32)


def dft_steps():
    b = np.arange(256)[:, None]
    fwd = np.zeros((7, P, 8, P))
    inv = np.zeros((7, P, 8, P))

    def cut(m, i, j):
        return m[i * P:(i + 1) * P, j * P:(j + 1) * P]

    f0 = 8 * np.arange(P)[None, :]
    f4 = f0 + 4
    ang0, ang4 = 2 * np.pi * b * f0 / NFFT, 2 * np.pi * b * f4 / NFFT
    c0, s0, c4, s4 = np.cos(ang0), -np.sin(ang0), np.cos(ang4), -np.sin(ang4)
    s0[:, 0] = (-1.0) ** b[:, 0]
    for k in range(2):
        for n, m in enumerate((c0, s0, c4, s4)):
            fwd[0, :, 2 * n + k] = cut(m, k, 0)
    i0, j0 = 2 * c0.T / NFFT, 2 * s0.T / NFFT
    i0[0] /= 2
    j0[0] /= 2
    i4, j4 = 2 * c4.T / NFFT, 2 * s4.T / NFFT
    for m in range(2):
        for n, (re, im) in enumerate(((i0, j0), (i4, j4))):
            inv[0, :, 4 * n + 2 * m] = cut(re, 0, m)
            inv[0, :, 4 * n + 2 * m + 1] = cut(im, 0, m)
    for c in (1, 2, 3):
        f = c + 8 * np.arange(256)[None, :]
        ang = 2 * np.pi * b * f / NFFT
        co, si = np.cos(ang), np.sin(ang)
        ic, isn = 2 * co.T / NFFT, 2 * si.T / NFFT
        for m in range(2):
            for k in range(2):
                fwd[2 * c - 1, :, 4 * m + k] = cut(co, k, m)
                fwd[2 * c - 1, :, 4 * m + 2 + k] = cut(-si, k, m)
                fwd[2 * c, :, 4 * m + k] = cut(-si, k, m)
                fwd[2 * c, :, 4 * m + 2 + k] = cut(-co, k, m)
                inv[2 * c - 1, :, 4 * m + k] = cut(ic, k, m)
                inv[2 * c - 1, :, 4 * m + 2 + k] = cut(-isn, k, m)
                inv[2 * c, :, 4 * m + k] = cut(isn, k, m)
                inv[2 * c, :, 4 * m + 2 + k] = cut(ic, k, m)
    return (fwd.reshape(7, P, 8 * P).astype(np.float32), inv.reshape(7, P, 8 * P).astype(np.float32))



FIXED = 16512
KB = 1024

N_LAT, N_CTX, N_CQ, N_CKV, N_POST1, N_PRE2, N_POST2, N_PREH, N_POSTH, N_PREM, N_POSTM = 0, 2, 3, 5, 8, 10, 12, 14, 16, 18, 20
A_LAT, A_CTX, A_MLP0, A_HY, A_MLP1 = 0, 16, 24, 40, 56
B_ATT, B_MLP0, B_HY, B_MLP1 = 0, 16, 32, 48
W_FILT = 0
W_DOWN = W_FILT + 16
W_HEAD = W_DOWN + 4
W_O = W_HEAD + 8
W_MLP0 = W_O + 8
W_IN = W_MLP0 + 8 * NCHUNK
W_CONV = W_IN + 24
W_OUT = W_CONV + 28
W_MLP1 = W_OUT + 8
W_END = W_MLP1 + 8 * NCHUNK

ABLOCKS = 3
ACOLS = 6 * D // (ABLOCKS * NCHUNK)


class Chain:

    def __init__(self, eng, sem):
        self.eng, self.sem, self.base, self.n = eng, sem, 0, 0

    def did(self, inst):
        inst.then_inc(self.sem, 1)
        self.n += 1

    def wait(self):
        self.eng.wait_ge(self.sem, self.base + self.n)

    def enter(self, i, per):
        self.before, self.per = self.base + self.n, per
        self.base, self.n = self.before + i * per, 0

    def leave(self, rounds):
        assert self.n == self.per, (self.n, self.per)
        self.base, self.n = self.before + rounds * self.per, 0


def build_program(nc, x, ctx, vecs, ada_w, w_down, w_head, w_o, w_in, w_out, mlp_w1, mlp_w2,
                  f_w1, f_w2, f_w3, hy_bias, rope, ropesum, ident, zpos, decay, dft_fwd, dft_inv, out):
    at = [FIXED]

    def fixed(name, shape, dt=F32):
        off = at[0]
        at[0] += -(-int(np.prod(shape[1:])) * 4 // 32) * 32
        return nc.alloc_sbuf_tensor_at(name, list(shape), dt, offset=off)

    raw = [fixed(f"w_raw{s}", [P, 1024]) for s in range(2)]
    whi = [fixed(f"w_hi{s}", [P, 8, P], F32R) for s in range(2)]
    wlo = [fixed(f"w_lo{s}", [P, 8, P], F32R) for s in range(2)]
    idm = fixed("idm", [P, P])
    ones = fixed("ones", [P, P])
    vec = fixed("vec", [P, NVEC])
    mod = fixed("mod", [P, 112])
    fac = fixed("fac", [P, 72])
    sil = fixed("sil", [P, 16])
    sile = fixed("sile", [P, 16])
    eps = fixed("eps", [P, 1])
    mx = fixed("mx", [P, 4])
    mxr = fixed("mxr", [P, 4])
    sm = fixed("sm", [P, 4])
    inv_sum = fixed("inv_sum", [P, 2])
    zero = fixed("zero", [P, 1])
    notop = fixed("notop", [P, 1])
    ARENA = -(-at[0] // 64) * 64

    def arena(name, kb, shape, dt=F32):
        return nc.alloc_sbuf_tensor_at(name, list(shape), dt, offset=ARENA + int(kb * KB))

    f_s = arena("f_s", 0, [P, 4, 2, D])
    f_d = arena("f_d", 32, [P, 4, 2, D])
    rg_hi = [arena(f"rg_hi{s}", 64 + 16 * s, [P, 4, HALF], F32R) for s in range(2)]
    rg_lo = [arena(f"rg_lo{s}", 72 + 16 * s, [P, 4, HALF], F32R) for s in range(2)]
    bq = arena("bq", 96, [P, 2, D])
    bs = arena("bs", 104, [P, 2, D])
    val = [arena(f"val{s}", 112 + 8 * s, [P, 4, HALF]) for s in range(2)]
    fb = arena("fb", 128, [P, 2, D])
    dec = [arena(f"dec{s}", 136 + 4 * s, [P, D]) for s in range(2)]
    fw3 = arena("fw3", 144, [FH, 2 * D])
    fbias = arena("fbias", 152, [1, 2 * D])
    ko = [arena(f"ko{s}", 160 + 2 * s, [P, HALF]) for s in range(4)]
    hda = arena("hda", 168, [FH, T])
    hdn = arena("hdn", 172, [FH, T])
    hd2 = arena("hd2", 176, [FH, T])
    zp = arena("zp", 128, [EMB, T])
    hd1 = arena("hd1", 132, [FH, T])
    fw12 = arena("fw12", 136, [FH, 2, FH])
    vrow = arena("vrow", 64, [P, NVEC // P, P])
    aacc = arena("aacc", 0, [P, 6 * D])
    aaccc = arena("aaccc", 24, [P, 2 * D])
    araw = [arena(f"araw{s}", off, [P, 3 * D]) for s, off in enumerate((32, 44, 66, 78))]
    xa = arena("xa", 0, [P, KT, T])
    xtm = arena("xtm", 112, [P, TT, D])
    xctm = arena("xctm", 152, [P, 2, D])
    xc = arena("xc", 144, [P, KT, C])
    hh = arena("hh", 32, [P, KT, T], F32R)
    hl = arena("hl", 64, [P, KT, T], F32R)
    hch = arena("hch", 96, [P, KT, C], F32R)
    hcl = arena("hcl", 104, [P, KT, C], F32R)
    asq = arena("asq", 112, [P, KT, HALF])
    arstd = arena("arstd", 128, [P, KEYS])
    atmp = [arena(f"atmp{s}", 136 + 2 * s, [P, HALF]) for s in range(2)]
    assum = arena("assum", 140, [P, HALF])
    astd = arena("astd", 142, [P, HALF])
    cq = arena("cq", 144, [P, 2, T])
    ckv = arena("ckv", 152, [P, KEYS])
    krt = arena("krt", 112, [P, KEYS])
    cqh = arena("cqh", 118, [P, 2, T], F32R)
    cql = arena("cql", 126, [P, 2, T], F32R)
    ckvh = arena("ckvh", 134, [P, KEYS], F32R)
    ckvl = arena("ckvl", 139, [P, KEYS], F32R)
    rtab = arena("rtab", 160, [P, KEYS])
    rsm = arena("rsm", 117, [P, P])
    csq = arena("csq", 165, [P, 2, HALF])
    crstd = arena("crstd", 169, [P, KEYS])
    cssum = arena("cssum", 174, [P, HALF])
    cstd = arena("cstd", 176, [P, HALF])
    ao = arena("ao", 0, [P, KT, T])
    qh = arena("qh", 32, [P, 2, T], F32R)
    ql = arena("ql", 40, [P, 2, T], F32R)
    kh = arena("kh", 48, [P, 2, KEYS], F32R)
    kl = arena("kl", 58, [P, 2, KEYS], F32R)
    vh = arena("vh", 68, [P, 10, 2, VD], F32R)
    vl = arena("vl", 78, [P, 10, 2, VD], F32R)
    pr = arena("pr", 88, [P, 2, 2, KEYS])
    pth = [arena(f"pth{s}", 144 + 2 * s, [P, 2, 256], F32R) for s in range(4)]
    ptl = [arena(f"ptl{s}", 152 + 2 * s, [P, 2, 256], F32R) for s in range(4)]
    qf = [arena(f"qf{s}", 165 + 2 * s, [P, HALF]) for s in range(2)]
    rc = arena("rc", 169, [VD, 256])
    rb = arena("rb", 170, [P, 2, VD])
    xm = arena("xm", 128, [P, KT, T])
    y = arena("y", 96, [P, KT, T])
    hidh = arena("hidh", 0, [P, HIDT, T], F32R)
    hidl = arena("hidl", 16, [P, HIDT, T], F32R)
    msq = arena("msq", 0, [P, KT, HALF])
    mr = [arena(f"mr{s}", 160 + 2 * s, [P, HALF]) for s in range(2)]
    ms2 = [arena(f"ms2{s}", 164 + 2 * s, [P, HALF]) for s in range(2)]
    mrstd = arena("mrstd", 168, [P, T])
    mtmp = [arena(f"mtmp{s}", 172 + 2 * s, [P, HALF]) for s in range(2)]
    mssum = arena("mssum", 176, [P, HALF])
    mstd = arena("mstd", 178, [P, HALF])
    bacc = arena("bacc", 176, [P, ABLOCKS, ACOLS])
    braw = arena("braw", 168, [P, KT, ACOLS])
    ub = [arena(f"ub{s}", 96 + 5 * s, [P, T + 2]) for s in range(2)]
    uc = [arena(f"uc{s}", 106 + 4 * s, [P, T]) for s in range(2)]
    ut = [arena(f"ut{s}", 114 + 4 * s, [P, TT, P]) for s in range(2)]
    src = arena("src", 128, [P, 4, 2, D])
    pz = arena("pz", 0, [P, 4, 4, D])
    ks = [arena(f"ks{s}", 160 + 6 * s, [P, 3, HALF]) for s in range(2)]
    pt = [arena(f"pt{s}", 172 + 2 * s, [P, HALF]) for s in range(2)]
    gate = arena("gate", 64, [P, 4, 2, D])
    zh = arena("zh", 0, [P, KT, T], F32R)
    zl = arena("zl", 32, [P, KT, T], F32R)
    ot = [arena(f"ot{s}", 4 * s, [P, D]) for s in range(2)]

    ps = nc.alloc_psum_tensor("ps", [P, 8, HALF], F32)
    psf = ps[:, :, :].rearrange("p b n -> p (b n)")

    x_spill = nc.dram_tensor("x_spill", [KT, P, T], F32, kind="Internal").ap()
    spec = nc.dram_tensor("spec", [ORDERS * 8 * 3 * P, D], F32, kind="Internal").ap()
    u_tm = nc.dram_tensor("u_tm", [3 * KT, T, P], F32, kind="Internal").ap()

    names = set()

    def sem(name):
        assert name not in names
        names.add(name)
        return nc.alloc_semaphore(name)

    w_arrived = [sem(f"w_arrived{s}") for s in range(2)]
    w_hi_made, w_staged = sem("w_hi_made"), sem("w_staged")
    const_in, filt_in, filt_w3_in = sem("const_in"), sem("filt_in"), sem("filt_w3_in")
    dec_in = [sem(f"dec_in{s}") for s in range(2)]
    vec_t, vec_made, sil_exp = sem("vec_t"), sem("vec_made"), sem("sil_exp")
    ones_made, zero_made = sem("ones_made"), sem("zero_made")
    dve_chain, act_chain = sem("dve_chain"), sem("act_chain")
    ada_in = [sem(f"ada_in{s}") for s in range(4)]
    ada1_in, ada1_acc, ada1_sum, ada1_mod = sem("ada1_in"), sem("ada1_acc"), sem("ada1_sum"), sem("ada1_mod")
    ada_acc, ada_sum, mods_made = sem("ada_acc"), sem("ada_sum"), sem("mods_made")
    hd_done, hd_arg, hd_sin = sem("hd_done"), sem("hd_arg"), sem("hd_sin")
    hf_done, hf_free = sem("hf_done"), sem("hf_free")
    fs_done, fs_free = sem("fs_done"), sem("fs_free")
    fr_val, fr_hi, fr_lo = sem("fr_val"), sem("fr_hi"), sem("fr_lo")
    ko_out = [sem(f"ko_out{s}") for s in range(4)]
    x_in, xt_done, xt_free = sem("x_in"), sem("xt_done"), sem("xt_free")
    sq_made, sum_made, ms_made, std_made, rstd_made = sem("sq_made"), sem("sum_made"), sem("ms_made"), sem("std_made"), sem("rstd_made")
    pre_t, pre_hi, pre_lo, post_y, post_x = sem("pre_t"), sem("pre_hi"), sem("pre_lo"), sem("post_y"), sem("post_x")
    x_saved, x_back = sem("x_saved"), sem("x_back")
    dn_done, dn_free = sem("dn_done"), sem("dn_free")
    cn_hi, cn_val, cn_lo = sem("cn_hi"), sem("cn_val"), sem("cn_lo")
    kr_made, kr_done, kr_hi, kr_lo = sem("kr_made"), sem("kr_done"), sem("kr_hi"), sem("kr_lo")
    tab_in, v_ones = sem("tab_in"), sem("v_ones")
    pp_done, pp_free, q_val, pp_hi = sem("pp_done"), sem("pp_free"), sem("q_val"), sem("pp_hi")
    q_lo, k_lo, raw_max, uc_left = sem("q_lo"), sem("k_lo"), sem("raw_max"), sem("uc_left")
    s_done, max_made, p_made = sem("s_done"), sem("max_made"), sem("p_made")
    t_done, t_hi, t_free = sem("t_done"), sem("t_hi"), sem("t_free")
    pv_done, rc_made, o_made = sem("pv_done"), sem("rc_made"), sem("o_made")
    rs_made, rb_made, rt_done = sem("rs_made"), sem("rb_made"), sem("rt_done")
    oh_made, ol_made = sem("oh_made"), sem("ol_made")
    wo_done, wo_free = sem("wo_done"), sem("wo_free")
    hid_done, hid_free = [sem(f"hid_done{i}") for i in range(2)], [sem(f"hid_free{i}") for i in range(2)]
    hid_sq, hid_hi, hid_lo = [sem(f"hid_sq{i}") for i in range(2)], [sem(f"hid_hi{i}") for i in range(2)], [sem(f"hid_lo{i}") for i in range(2)]
    acc_done, acc_free = [sem(f"acc_done{i}") for i in range(2)], [sem(f"acc_free{i}") for i in range(2)]
    y_zero = sem("y_zero")
    wi_done, wi_free, uc_mid, uc_made, ut_done, ut_made = (sem("wi_done"), sem("wi_free"), sem("uc_mid"), sem("uc_made"), sem("ut_done"), sem("ut_made"))
    ut_out = [sem(f"ut_out{s}") for s in range(2)]
    src_in, k_ny_in, gate_in = sem("src_in"), sem("k_ny_in"), sem("gate_in")
    k_in = [sem(f"k_in{s}") for s in range(2)]
    cf_done, cf_free = sem("cf_done"), sem("cf_free")
    ci_done, ci_free = sem("ci_done"), sem("ci_free")
    cr_val, cr_hi, cr_lo = sem("cr_val"), sem("cr_hi"), sem("cr_lo")
    pz_made, z_made = sem("pz_made"), sem("z_made")
    zt_done, z_hi, z_lo = sem("zt_done"), sem("z_hi"), sem("z_lo")
    out_done, out_made = sem("out_done"), sem("out_made")
    out_sent = [sem(f"out_sent{s}") for s in range(2)]
    ho_done, ho_free = sem("ho_done"), sem("ho_free")

    def w_tiles(ap):
        return ap.rearrange("(k p) m -> p k m", p=P)

    RING = [(c, n) for c in range(4) for n in range(2)]
    def s_groups(c):
        if c == 0:
            return [((0, 1), (0, 1), 0, 0), ((2, 3), (0, 1), 0, 2), ((4, 5), (2, 3), 1, 0)]
        return [((4 * m, 4 * m + 1, 4 * m + 2, 4 * m + 3), (0, 1, 2, 3), 2 * c + m, 0) for m in range(2)]

    def d_groups(c):
        if c == 0:
            return [((2, 3), (0, 1), 0, 1), ((6, 7), (2, 3), 1, 1)]
        return [((4 * m, 4 * m + 1, 4 * m + 2, 4 * m + 3), (0, 1, 2, 3), 2 * c + m, 1) for m in range(2)]

    S_CNT = [len(s_groups(c)) for c, _ in RING]
    D_CNT = [len(d_groups(c)) for c, _ in RING]
    FS_PER = sum(S_CNT) + sum(D_CNT)
    S_END = [sum(S_CNT[:i + 1]) for i in range(8)]
    D_END = [sum(S_CNT) + sum(D_CNT[:i + 1]) for i in range(8)]
    RING_END = S_END + D_END

    FS_GROUPS = [(c, n, *g) for groups in (s_groups, d_groups) for c, n in RING for g in groups(c)]
    KO_USES = [sum(2 if g[4:] == (0, 0) else 1 for g in FS_GROUPS[q::4]) for q in range(4)]
    STEP_END = [8 + 4 * s for s in range(7)]
    FWD_END = INV_END = STEP_END

    PIECE_BANK = (0, 1, 2, 3, 0, 1, 2, 3, 4, 3)

    def half(n):
        return slice(n * HALF, (n + 1) * HALF)

    def transform_groups(s, inverse):
        out = []
        for n in range(2):
            if s == 0:
                for q in range(4):
                    out.append((n, (2 * q, 2 * q + 1), (2 * (q // 2), 2 * (q // 2) + 1), 4 * n + q))
            else:
                for m in range(2):
                    out.append((n, tuple(range(4 * m, 4 * m + 4)), (0, 1, 2, 3), STEP_END[s - 1] + 2 * n + m))
        return out

    def pair_tile(p):
        return (p % 2, p // 2) if p < 4 else (2 * (p // 4) + p % 2, p % 4 // 2)

    def pair_groups(p):
        if p < 4:
            return 2 * p, 2 * p + 1
        return 8 * (p // 4) + p % 4, 8 * (p // 4) + 4 + p % 4

    def ring_read(c, n):
        return 4 * (n + 1) if c == 0 else 8 * c + 6 + 2 * n

    def filter_step_src(o8):
        return (0, 1, 3, 5, 0, 2, 4, 6)[o8]

    block = nc.Block()
    with block as blk:

        @blk.sync
        def _(sp):
            def weights(s, source):
                if not (isinstance(s, int) and s < 2):
                    sp.wait_ge(w_staged, s - 1)
                return source

            def load(slot, s, source, shape=None):
                weights(s, source)
                dst = raw[slot][:, :]
                if shape:
                    dst = dst.rearrange("p (k m) -> p k m", k=shape)
                sp.dma_start(dst, source).then_inc(w_arrived[slot], 16)

            sp.dma_start(vrow[:, :, :], vecs.rearrange("(a p) c -> p a c", p=P)).then_inc(const_in, 16)
            sp.dma_start(idm[:, :], ident).then_inc(const_in, 16)
            sp.dma_start(zp[:, :], zpos).then_inc(filt_in, 16)
            sp.dma_start(fw12[0:EMB, 0, :], f_w1).then_inc(filt_in, 16)
            sp.dma_start(fw12[:, 1, :], f_w2).then_inc(filt_in, 16)
            sp.dma_start(fbias[:, :], hy_bias.rearrange("(a o) d -> a (o d)", a=1)).then_inc(filt_in, 16)
            for n in range(2 * KT):
                k, h = n // 2, n % 2
                if n >= 4:
                    sp.wait_ge(ada_acc, n - 3)
                sp.dma_start(araw[n % 4][:, :], ada_w[0, k * P:(k + 1) * P, h * 3 * D:(h + 1) * 3 * D]).then_inc(ada_in[n % 4], 16)
            sp.wait_ge(hd_sin, 2)
            for o in range(ORDERS):
                if o:
                    sp.wait_ge(hf_done, 32 * o)
                sp.dma_start(fw3[:, :], f_w3[:, o * 2 * D:(o + 1) * 2 * D]).then_inc(filt_w3_in, 16)
                for t in range(TT):
                    if 8 * o + t >= 2:
                        sp.wait_ge(hf_free, 4 + 4 * (8 * o + t - 1))
                    sp.dma_start(dec[t % 2][:, :], decay[t * P:(t + 1) * P, :]).then_inc(dec_in[t % 2], 16)
                    if t < 2:
                        load(t % 2, W_FILT + 8 * o + t, dft_fwd[filter_step_src(t)])
                for s in range(2, 8):
                    load(s % 2, W_FILT + 8 * o + s, dft_fwd[filter_step_src(s)])
            sp.wait_ge(fs_done, 2 * FS_PER)
            for q in range(4):
                sp.wait_ge(ko_out[q], 16 * ORDERS * KO_USES[q])
            sp.dma_start(xtm[:, :, :], x.rearrange("(a p) d -> p a d", p=P)).then_inc(x_in, 16)
            sp.dma_start(xctm[:, :, :], ctx.rearrange("(a p) d -> p a d", p=P)).then_inc(x_in, 16)
            for s in range(4):
                load(s % 2, W_DOWN + s, w_tiles(w_down)[:, :, s * P:(s + 1) * P], 8)
            sp.wait_ge(xt_free, 20)
            sp.dma_start(rtab[:, :], rope).then_inc(tab_in, 16)
            sp.wait_ge(pre_t, A_LAT + 16)
            sp.dma_start(x_spill.rearrange("k p t -> p k t"), xa[:, :, :]).then_inc(x_saved, 16)
            sp.wait_ge(pre_lo, A_CTX + 8)
            sp.dma_start(rsm[:, :], ropesum).then_inc(tab_in, 16)
            for s in range(2):
                load(s % 2, W_HEAD + s, w_head[s])
            with sp.Fori(1, HEADS // 4) as i:
                for s in range(2):
                    load(s, W_HEAD + 2 * i + s, w_head[bass.ds(2 * i + s, 1)].rearrange("a p n -> (a p) n"))
            for s in range(2):
                load(s, W_O + s, w_tiles(w_o)[:, :, s * P:(s + 1) * P], 8)
            with sp.Fori(1, 4) as i:
                for s in range(2):
                    load(s, W_O + 2 * i + s, w_tiles(w_o)[:, :, bass.ds((2 * i + s) * P, P)], 8)
            sp.wait_ge(ol_made, 8)
            sp.wait_ge(x_saved, 16)
            sp.dma_start(xm[:, :, :], x_spill.rearrange("k p t -> p k t")).then_inc(x_back, 16)

            def mlp(layer, base):
                w1 = w_tiles(mlp_w1[layer])
                w2 = mlp_w2[layer].rearrange("(c k p) m -> c p k m", k=HIDT, p=P)

                def step(j, s):
                    if s < 4:
                        load(s % 2, base + 8 * j + s, w1[:, :, bass.ds((4 * j + s) * P, P)], 8)
                    else:
                        load(s % 2, base + 8 * j + s, w2[bass.ds(j, 1), :, :, (s - 4) * 256:(s - 3) * 256].rearrange("c p k m -> (c p) k m"), 4)

                with sp.Fori(0, NCHUNK) as j:
                    for s in range(8):
                        if layer == 0 and s in (2, 5, 7):
                            b = (2, 5, 7).index(s)
                            sp.wait_ge(ada1_acc, 1 + KT * (ABLOCKS * j + b))
                            sp.dma_start(braw[:, :, :], ada_w[1].rearrange("(k p) n -> p k n", p=P)[:, :, bass.ds((ABLOCKS * j + b) * ACOLS, ACOLS)]).then_inc(ada1_in, 16)
                        step(j, s)

            mlp(0, W_MLP0)
            for s in range(2):
                load(s, W_IN + s, w_tiles(w_in)[:, :, s * P:(s + 1) * P], 8)
            sp.wait_ge(pre_t, A_HY + 16)
            sp.dma_start(x_spill.rearrange("k p t -> p k t"), xm[:, :, :]).then_inc(x_saved, 16)
            with sp.Fori(1, 12) as i:
                for s in range(2):
                    load(s, W_IN + 2 * i + s, w_tiles(w_in)[:, :, bass.ds((2 * i + s) * P, P)], 8)
            sp.wait_ge(x_saved, 32)
            for s in range(2):
                sp.wait_ge(ut_out[s], 16 * 12)

            def token_major(dst, first, arrived):
                for k in range(KT):
                    sp.dma_start(dst[:, :, :, k * P:(k + 1) * P].rearrange("p a b c -> p (a b) c"),
                                 u_tm[bass.ds(first + k, 1)].rearrange("m (a p) c -> (m p) a c", p=P)).then_inc(arrived, 16)

            token_major(src, 2 * KT, src_in)
            with sp.Fori(0, ORDERS) as o:
                def conv_weights(s):
                    load(s % 2, W_CONV + 14 * o + s, dft_fwd[s])

                def spectrum(p):
                    f, n = pair_tile(p)
                    if p >= 2:
                        sp.wait_ge(cf_free, 16 * o + p - 1)
                    rows = spec[bass.ds((8 * o + f) * 3 * P, 2 * P), half(n)]
                    sp.dma_start(ks[p % 2][:, 0:2, :], rows.rearrange("(a p) d -> p a d", p=P)).then_inc(k_in[p % 2], 16)
                    if f == 0:
                        sp.dma_start(ks[p % 2][:, 2, :], spec[bass.ds(((8 * o + f) * 3 + 2) * P, P), half(n)]).then_inc(k_ny_in, 16)

                conv_weights(0)
                spectrum(0)
                spectrum(1)
                conv_weights(1)
                spectrum(2)
                spectrum(3)
                for c in (1, 2, 3):
                    conv_weights(2 * c)
                    spectrum(4 * c)
                    spectrum(4 * c + 1)
                    if c < 3:
                        conv_weights(2 * c + 1)
                    spectrum(4 * c + 2)
                    spectrum(4 * c + 3)
                for s in range(7):
                    load((7 + s) % 2, W_CONV + 14 * o + 7 + s, dft_inv[s])
                sp.wait_ge(ci_done, 32 * o + 32)
                token_major(gate, KT * o, gate_in)
            for s in range(2):
                load(s, W_OUT + s, w_tiles(w_out)[:, :, s * P:(s + 1) * P], 8)
            sp.wait_ge(z_lo, 16)
            sp.dma_start(xm[:, :, :], x_spill.rearrange("k p t -> p k t")).then_inc(x_back, 16)
            with sp.Fori(1, 4) as i:
                for s in range(2):
                    load(s, W_OUT + 2 * i + s, w_tiles(w_out)[:, :, bass.ds((2 * i + s) * P, P)], 8)
            mlp(1, W_MLP1)
            for t in range(TT):
                sp.wait_ge(out_made, 2 * t + 2)
                sp.dma_start(out[t * P:(t + 1) * P, :], ot[t % 2][:, :]).then_inc(out_sent[t % 2], 16)
            for s in range(2):
                sp.wait_ge(out_sent[s], 16 * 4)

        @blk.gpsimd
        def _(pool):
            nc.gpsimd.memset(zero[:, :], 0.0).then_inc(zero_made, 1)
            pool.wait_ge(zero_made, 1)

            def stage(slot, s, uses, read=None):
                pool.wait_ge(w_arrived[slot], 16 * uses)
                if read:
                    pool.wait_ge(*read)
                hi, lo = (w[slot][:, :, :].rearrange("p k m -> p (k m)") for w in (whi, wlo))
                nc.gpsimd.tensor_tensor(hi, raw[slot][:, :], zero[:, 0:1].to_broadcast([P, 1024]), ALU.add).then_inc(w_hi_made, 1)
                pool.wait_ge(w_hi_made, s + 1)
                nc.gpsimd.tensor_tensor(lo, raw[slot][:, :], hi, ALU.subtract).then_inc(w_staged, 1)

            def uses(s):
                return s // 2 + 1

            done = {}
            for o in range(ORDERS):
                for s in range(8):
                    r = 2 * s + 1
                    done[W_FILT + 8 * o + s] = (fs_done, FS_PER * o + RING_END[r])
            for s, n in enumerate((2, 4, 7, 10)):
                done[W_DOWN + s] = (dn_done, n)
            for g in range(8):
                done[W_HEAD + g] = (pp_done, 10 * g + 10)
            for s in range(8):
                done[W_O + s] = (wo_done, 2 * s + 2)
                done[W_OUT + s] = (ho_done, 2 * s + 2)
            for l, base in enumerate((W_MLP0, W_MLP1)):
                for s in (6, 7):
                    done[base + 8 * (NCHUNK - 1) + s] = (acc_done[l], 16 * (NCHUNK - 1) + 4 * (s - 3))
            for s in range(24):
                done[W_IN + s] = (wi_done, 2 * s + 2)
            for s in (12, 13):
                done[W_CONV + 14 + s] = (ci_done, 32 + INV_END[s - 7])
            for s in range(W_FILT, W_HEAD + 2):
                stage(s % 2, s, uses(s), done.get(s - 2))
            with pool.Fori(1, 4) as i:
                for s in range(2):
                    stage(s, W_HEAD + 2 * i + s, W_HEAD // 2 + i + 1, (pp_done, 20 * i + 10 * s - 10))
            for s in range(W_O, W_O + 2):
                stage(s % 2, s, uses(s), done[s - 2])
            with pool.Fori(1, 4) as i:
                for s in range(2):
                    stage(s, W_O + 2 * i + s, W_O // 2 + i + 1, (wo_done, 4 * i + 2 * s - 2))

            def mlp(l, base):
                def step(j, s):
                    if s < 6:
                        read = (hid_done[l], 8 * j + 2 * (s - 1))
                    else:
                        read = (acc_done[l], 16 * j + 4 * (s - 5))
                    stage(s % 2, base + 8 * j + s, base // 2 + 4 * j + s // 2 + 1, read)

                for s in range(2):
                    stage(s, base + s, uses(base + s), done[base + s - 2])
                with pool.Fori(0, NCHUNK - 1) as j:
                    for s in range(2, 10):
                        step(j, s)
                for s in range(2, 8):
                    step(NCHUNK - 1, s)

            mlp(0, W_MLP0)
            for s in range(W_IN, W_IN + 2):
                stage(s % 2, s, uses(s), done[s - 2])
            with pool.Fori(1, 12) as i:
                for s in range(2):
                    stage(s, W_IN + 2 * i + s, W_IN // 2 + i + 1, (wi_done, 4 * i + 2 * s - 2))
            for s in range(W_CONV, W_CONV + 2):
                stage(s % 2, s, uses(s), done[s - 2])
            with pool.Fori(0, ORDERS - 1) as o:
                for s in range(2, 16):
                    read = (cf_done, 32 * o + FWD_END[s - 2]) if s < 9 else (ci_done, 32 * o + INV_END[s - 9])
                    stage(s % 2, W_CONV + 14 * o + s, W_CONV // 2 + 7 * o + s // 2 + 1, read)
            for s in range(2, 14):
                read = (cf_done, 32 * (ORDERS - 1) + FWD_END[s - 2]) if s < 9 else (ci_done, 32 * (ORDERS - 1) + INV_END[s - 9])
                stage(s % 2, W_CONV + 14 + s, uses(W_CONV + 14 + s), read)
            for s in range(W_OUT, W_OUT + 2):
                stage(s % 2, s, uses(s), done[s - 2])
            with pool.Fori(1, 4) as i:
                for s in range(2):
                    stage(s, W_OUT + 2 * i + s, W_OUT // 2 + i + 1, (ho_done, 4 * i + 2 * s - 2))
            mlp(1, W_MLP1)

        @blk.tensor
        def _(pe):
            def products(dst, terms, done):
                n = len(terms)
                for i, (wh, wl, rh, rl, ready) in enumerate(terms):
                    if ready:
                        pe.wait_ge(*ready)
                    nc.tensor.matmul(dst, wh, rh, start=(i == 0), stop=False)
                    nc.tensor.matmul(dst, wh, rl, start=False, stop=False)
                    last = nc.tensor.matmul(dst, wl, rh, start=False, stop=(i == n - 1))
                last.then_inc(done, 1)

            def w(slot, k):
                return whi[slot][:, k, :], wlo[slot][:, k, :]

            def mean_square(c, ssum, width, bank):
                pe.wait_ge(sum_made, c + 1)
                nc.tensor.matmul(ps[:, bank, 0:width], ones[:, :], ssum[:, 0:width], start=True, stop=True).then_inc(ms_made, 1)

            pe.wait_ge(const_in, 32)
            pe.wait_ge(ones_made, 1)
            for a in range(3):
                last = nc.tensor.transpose(ps[:, 0, a * P:(a + 1) * P], vrow[:, a, :], idm[:, :])
            last.then_inc(vec_t, 1)
            pe.wait_ge(filt_in, 64)
            for n in range(2):
                last = nc.tensor.matmul(ps[0:FH, 2 + n, :], fw12[0:EMB, 0, :], zp[0:EMB, half(n)], start=True, stop=True)
            last.then_inc(hd_done, 1)
            pe.wait_ge(hd_sin, 1)
            for n in range(2):
                last = nc.tensor.matmul(ps[0:FH, 2 + n, :], fw12[:, 1, :], hd1[:, half(n)], start=True, stop=True)
            last.then_inc(hd_done, 1)
            pe.wait_ge(hd_sin, 2)
            pe.wait_ge(ada_acc, 2 * KT)
            for m in range(48):
                last = nc.tensor.matmul(ps[:, 1, m:m + 1], aacc[:, m * P:(m + 1) * P], ones[:, 0:1], start=True, stop=True)
            for m in range(16):
                last = nc.tensor.matmul(ps[:, 1, 48 + m:49 + m], aaccc[:, m * P:(m + 1) * P], ones[:, 0:1], start=True, stop=True)
            last.then_inc(ada_sum, 1)
            with pe.Fori(0, ORDERS) as o:
                pe.wait_ge(filt_w3_in, 16 * o + 16)
                for t in range(TT):
                    for j in range(4):
                        pe.wait_ge(hf_free, 32 * o + 4 * t + j + 1)
                        nc.tensor.matmul(ps[:, 4 + j, :], hd2[:, t * P:(t + 1) * P], fw3[:, half(j)], start=True, stop=True).then_inc(hf_done, 1)
                idx = 0
                for rnd, groups in ((0, s_groups), (1, d_groups)):
                    for r, (c, n) in enumerate(RING):
                        slot = r % 2
                        pe.wait_ge(fr_lo, 16 * o + 8 * rnd + r + 1)
                        if n == 0:
                            pe.wait_ge(w_staged, W_FILT + 8 * o + 4 * rnd + c + 1)
                        for tiles, rows, _, _ in groups(c):
                            pe.wait_ge(fs_free, FS_PER * o + max(idx + 1, 4))
                            products(ps[:, idx % 4, :],
                                     [(*w(c % 2, a), rg_hi[slot][:, b, :], rg_lo[slot][:, b, :], None) for a, b in zip(tiles, rows)], fs_done)
                            idx += 1
            pe.wait_ge(x_in, 32)
            for g in range(20):
                bank = g % 4
                if g == 0:
                    pe.wait_ge(fs_free, 4 + 2 * FS_PER)
                if g >= 4:
                    pe.wait_ge(xt_free, g - 3)
                for j in range(4):
                    if g < 16:
                        blk_in = xtm[:, 4 * (g % 2) + j, (g // 2) * P:(g // 2 + 1) * P]
                    else:
                        dt = 2 * (g - 16) + j // 2
                        blk_in = xctm[:, j % 2, dt * P:(dt + 1) * P]
                    last = nc.tensor.transpose(ps[:, bank, j * P:(j + 1) * P], blk_in, idm[:, :])
                last.then_inc(xt_done, 1)
            for c in range(2):
                mean_square(N_LAT + c, assum, HALF, 6 + c)
            pe.wait_ge(std_made, 1)
            mean_square(N_CTX, assum, C, 6)
            g = 0
            for s in range(4):
                pe.wait_ge(w_staged, W_DOWN + s + 1)
                for n in range(3 if s >= 2 else 2):
                    if g >= 6:
                        pe.wait_ge(dn_free, g - 5)
                    width = HALF if n < 2 else C
                    rh, rl = (hh, hl) if n < 2 else (hch, hcl)
                    cols = half(n) if n < 2 else slice(0, C)
                    base = A_LAT + 8 * n if n < 2 else A_CTX
                    products(ps[:, g % 6, 0:width],
                             [(*w(s % 2, k), rh[:, k, cols], rl[:, k, cols], (pre_lo, base + k + 1)) for k in range(KT)], dn_done)
                    g += 1
            for c in range(2):
                pe.wait_ge(std_made, N_CQ + c - 1)
                mean_square(N_CQ + c, cssum, HALF, 6 + (c + 1) % 2)
            for c in range(3):
                pe.wait_ge(std_made, N_CKV + c - 1)
                mean_square(N_CKV + c, cssum, HALF if c < 2 else C, 6 + (c + 1) % 2)
            pe.wait_ge(tab_in, 32)
            for c in range(3):
                width = HALF if c < 2 else C
                pe.wait_ge(kr_made, c + 1)
                nc.tensor.matmul(ps[:, 3 + c, 0:width], rsm[:, :], krt[:, c * HALF:c * HALF + width], start=True, stop=True).then_inc(kr_done, 1)
            def project_piece(g, gg, j):
                if j == 0:
                    pe.wait_ge(w_staged, W_HEAD + g + 1)
                pe.wait_ge(pp_free, 10 * g + (12 if j == 9 else max(j + 1, 4)))
                bank = PIECE_BANK[j]
                if j < 4:
                    hd, n = j // 2, j % 2
                    products(ps[:, bank, :], [(*w(gg, 2 * k + hd), cqh[:, k, half(n)], cql[:, k, half(n)], None) for k in range(2)], pp_done)
                elif j < 7:
                    n = j - 4
                    width = HALF if n < 2 else C
                    cols = slice(n * HALF, n * HALF + width)
                    products(ps[:, bank, 0:width], [(*w(gg, 4), ckvh[:, cols], ckvl[:, cols], None)], pp_done)
                else:
                    for q, t in enumerate(range(4 * (j - 7), min(10, 4 * (j - 7) + 4))):
                        dst = ps[:, bank, q * P:(q + 1) * P]
                        a, b = ckvh[:, t * P:(t + 1) * P], ckvl[:, t * P:(t + 1) * P]
                        vw_h, vw_l = w(gg, 5)
                        nc.tensor.matmul(dst, a, vw_h, start=True, stop=False)
                        nc.tensor.matmul(dst, a, vw_l, start=False, stop=False)
                        last = nc.tensor.matmul(dst, b, vw_h, start=False, stop=True)
                    last.then_inc(pp_done, 1)

            def scores(u, j, cuts):
                hd, q = u // 4, 2 * (u % 4) + j
                qs = slice(q * P, (q + 1) * P)
                for a, b in cuts:
                    dst = psf[:, j * KEYS + a:j * KEYS + b]
                    nc.tensor.matmul(dst, qh[:, hd, qs], kh[:, hd, a:b], start=True, stop=False)
                    nc.tensor.matmul(dst, qh[:, hd, qs], kl[:, hd, a:b], start=False, stop=False)
                    last = nc.tensor.matmul(dst, ql[:, hd, qs], kh[:, hd, a:b], start=False, stop=True)
                return last

            def scores_first(g, u):
                if u >= 1:
                    pe.wait_ge(p_made, 16 * g + 2 * u - 1)
                scores(u, 0, ((0, 512), (512, 1024)))

            def scores_first_end(g, u):
                if u >= 1:
                    pe.wait_ge(p_made, 16 * g + 2 * u)
                scores(u, 0, ((1024, 1280),)).then_inc(s_done, 1)

            def scores_shared(g, u):
                pe.wait_ge(p_made, 16 * g + 2 * u + 1)
                scores(u, 1, ((0, 256),)).then_inc(s_done, 1)

            def turn(g, u, jj):
                if jj == 0:
                    pe.wait_ge(p_made, 16 * g + 2 * u + 2)
                if 5 * u + jj >= 2:
                    pe.wait_ge(t_free, 40 * g + 5 * u + jj - 1)
                for k in range(2):
                    for j in range(2):
                        last = nc.tensor.transpose(ps[:, 5 + (5 * u + jj) % 2, k * 256 + j * P:k * 256 + (j + 1) * P],
                                                   pr[:, u % 2, j, (2 * jj + k) * P:(2 * jj + k + 1) * P], idm[:, :])
                last.then_inc(t_done, 1)

            def weigh(g, u, jj):
                pe.wait_ge(t_free, 40 * g + 5 * u + jj + 1)
                if jj == 0 and u >= 1:
                    pe.wait_ge(o_made, 8 * g + u)
                if jj == 4:
                    pe.wait_ge(rb_made, 16 * g + 2 * u + 2)
                slot = (5 * u + jj) % 4
                for k in range(2):
                    t = 2 * jj + k
                    a, b = vh[:, t, u // 4, :], vl[:, t, u // 4, :]
                    nc.tensor.matmul(ps[0:VD, 7, 0:256], a, pth[slot][:, k, :], start=(t == 0), stop=False)
                    nc.tensor.matmul(ps[0:VD, 7, 0:256], a, ptl[slot][:, k, :], start=False, stop=False)
                    last = nc.tensor.matmul(ps[0:VD, 7, 0:256], b, pth[slot][:, k, :], start=False, stop=(t == 9))
                last.then_inc(pv_done, 1)
                if jj == 4:
                    for j in range(2):
                        last = nc.tensor.transpose(ps[0:VD, 7, 256 + j * P:256 + (j + 1) * P], rb[:, j, :], idm[:, :])
                    last.then_inc(rt_done, 1)

            def group(g, gg, more):
                pe.wait_ge(pp_free, 4 + 10 * g + 7)
                scores_first(g, 0)
                scores_first_end(g, 0)
                project_piece(g, gg, 9)
                pe.wait_ge(pp_free, 4 + 10 * g + 10)
                scores(0, 1, ((256, 768), (768, 1280)))
                scores_shared(g, 0)
                scores_first(g, 1)
                for u in range(7):
                    scores_first_end(g, u + 1)
                    turn(g, u, 0)
                    turn(g, u, 1)
                    scores(u + 1, 1, ((256, 768), (768, 1280)))
                    weigh(g, u, 0)
                    turn(g, u, 2)
                    weigh(g, u, 1)
                    scores_shared(g, u + 1)
                    turn(g, u, 3)
                    weigh(g, u, 2)
                    turn(g, u, 4)
                    if u < 6:
                        scores_first(g, u + 2)
                    weigh(g, u, 3)
                    weigh(g, u, 4)
                turn(g, 7, 0)
                turn(g, 7, 1)
                if not more:
                    for jj in range(3):
                        weigh(g, 7, jj)
                        turn(g, 7, jj + 2)
                    weigh(g, 7, 3)
                    weigh(g, 7, 4)
                    return
                project_piece(g + 1, 1 - gg, 0)
                project_piece(g + 1, 1 - gg, 1)
                for jj in range(3):
                    weigh(g, 7, jj)
                    turn(g, 7, jj + 2)
                    project_piece(g + 1, 1 - gg, 2 + jj)
                weigh(g, 7, 3)
                project_piece(g + 1, 1 - gg, 5)
                weigh(g, 7, 4)
                for j in range(6, 9):
                    project_piece(g + 1, 1 - gg, j)

            pe.wait_ge(cn_lo, 3)
            pe.wait_ge(kr_lo, 6)
            for j in range(9):
                project_piece(0, 0, j)
            with pe.Fori(0, HEADS // 4 - 1) as i:
                group(2 * i, 0, True)
                group(2 * i + 1, 1, True)
            group(HEADS // 2 - 2, 0, True)
            group(HEADS // 2 - 1, 1, False)

            def project(base, rows_hi, rows_lo, done, free, first):
                with pe.Fori(0, 4) as i:
                    for s in range(2):
                        pe.wait_ge(w_staged, base + 2 * i + s + 1)
                        for n in range(2):
                            pe.wait_ge(free, 4 * i + 2 * s + n + 1)
                            products(ps[:, 2 * s + n, :],
                                     [(*w(s, k), rows_hi[:, k, half(n)], rows_lo[:, k, half(n)], first(k, n) if s == 0 else None) for k in range(KT)], done)

            def norms(first, ssum):
                for c in range(first, first + 4):
                    pe.wait_ge(std_made, c)
                    mean_square(c, ssum, HALF, 6 + c % 2)

            def mlp(l, pre):
                with pe.Fori(0, NCHUNK) as j:
                    if l == 0:
                        pe.wait_ge(ada1_mod, j + 1)
                    for s in range(4):
                        pe.wait_ge(w_staged, (W_MLP0, W_MLP1)[l] + 8 * j + s + 1)
                        for n in range(2):
                            pe.wait_ge(hid_free[l], 8 * j + 2 * s + n + 1)
                            products(ps[:, (2 * s + n) % 4, :],
                                     [(*w(s % 2, k), hh[:, k, half(n)], hl[:, k, half(n)], (pre_lo, pre + 8 * n + k + 1) if s == 0 else None)
                                      for k in range(KT)], hid_done[l])
                    for s in range(4):
                        if l == 0 and s == 3:
                            pe.wait_ge(ada1_acc, 1 + KT * ABLOCKS * (j + 1))
                            for b in range(ABLOCKS):
                                for m in range(ACOLS // P):
                                    col = b * (ACOLS // P) + m
                                    last = nc.tensor.matmul(ps[:, 0, col:col + 1], bacc[:, b, m * P:(m + 1) * P], ones[:, 0:1], start=True, stop=True)
                            last.then_inc(ada1_sum, 1)
                        pe.wait_ge(w_staged, (W_MLP0, W_MLP1)[l] + 8 * j + 4 + s + 1)
                        for n in range(2):
                            for m in range(2):
                                pe.wait_ge(acc_free[l], 16 * j + 4 * s + 2 * n + m + 1)
                                products(ps[:, 4 + 2 * n + m, :],
                                         [(*w(s % 2, 2 * k + m), hidh[:, k, half(n)], hidl[:, k, half(n)],
                                           (hid_lo[l], 8 * j + 2 * k + n + 1) if s == 0 and m == 0 else None) for k in range(HIDT)], acc_done[l])

            project(W_O, hh, hl, wo_done, wo_free, lambda k, n: (ol_made, k + 1))
            norms(N_POST1, mssum)
            mlp(0, A_MLP0)
            norms(N_POST2, mssum)
            def project_u(i, s, first):
                pe.wait_ge(w_staged, W_IN + 2 * i + s + 1)
                for n in range(2):
                    pe.wait_ge(wi_free, 4 * i + 2 * s + n + 1)
                    products(ps[:, 2 * (s % 2) + n, :],
                             [(*w(s % 2, k), hh[:, k, half(n)], hl[:, k, half(n)], (pre_lo, A_HY + 8 * n + k + 1) if first else None) for k in range(KT)], wi_done)

            def turn_u(i, s):
                pe.wait_ge(uc_made, 2 * i + s + 1)
                for n in range(2):
                    pe.wait_ge(ut_made, 4 * i + 2 * s + n + 1)
                    for q in range(4):
                        last = nc.tensor.transpose(ps[:, 4 + 2 * s + n, q * P:(q + 1) * P], uc[s][:, (4 * n + q) * P:(4 * n + q + 1) * P], idm[:, :])
                    last.then_inc(ut_done, 1)

            project_u(0, 0, True)
            with pe.Fori(0, 11) as i:
                project_u(i, 1, False)
                turn_u(i, 0)
                project_u(i, 2, False)
                turn_u(i, 1)
            project_u(11, 1, False)
            turn_u(11, 0)
            turn_u(11, 1)
            with pe.Fori(0, ORDERS) as o:
                for s in range(7):
                    pe.wait_ge(w_staged, W_CONV + 14 * o + s + 1)
                    cls = (s + 1) // 2
                    for n, tiles, rows, idx in transform_groups(s, False):
                        pe.wait_ge(cr_lo, 16 * o + 2 * cls + n + 1)
                        if cls == 1:
                            pe.wait_ge(cf_free, 16 * o + idx % 8 // 2 + 1)
                        elif cls > 1:
                            pe.wait_ge(cf_free, 16 * o + 4 * (cls - 1) + idx % 4 + 1)
                        products(ps[:, idx % 8, :], [(*w(s % 2, a), rg_hi[n][:, b, :], rg_lo[n][:, b, :], None) for a, b in zip(tiles, rows)], cf_done)
                pe.wait_ge(cf_free, 16 * o + 16)
                for s in range(7):
                    pe.wait_ge(w_staged, W_CONV + 14 * o + 7 + s + 1)
                    cls = (s + 1) // 2
                    for n, tiles, rows, idx in transform_groups(s, True):
                        pe.wait_ge(cr_lo, 16 * o + 8 + 2 * cls + n + 1)
                        pe.wait_ge(ci_free, 32 * o + idx + 1)
                        products(ps[:, idx % 8, :], [(*w((7 + s) % 2, a), rg_hi[n][:, b, :], rg_lo[n][:, b, :], None) for a, b in zip(tiles, rows)], ci_done)
            for g in range(16):
                pe.wait_ge(z_made, 2)
                if g == 0:
                    pe.wait_ge(ci_free, 8 + 32 * ORDERS)
                if g >= 4:
                    pe.wait_ge(z_lo, g - 3)
                for j in range(4):
                    tt = 4 * (g % 2) + j
                    last = nc.tensor.transpose(ps[:, g % 4, j * P:(j + 1) * P], src[:, tt // 2, tt % 2, (g // 2) * P:(g // 2 + 1) * P], idm[:, :])
                last.then_inc(zt_done, 1)
            project(W_OUT, zh, zl, ho_done, ho_free, lambda k, n: (z_lo, 2 * k + n + 1))
            norms(N_POSTH, mssum)
            mlp(1, A_MLP1)
            for c in range(N_POSTM, N_POSTM + 2):
                pe.wait_ge(std_made, c)
                mean_square(c, mssum, HALF, 6 + c % 2)
            for g in range(16):
                if g < 2:
                    pe.wait_ge(post_x, B_MLP1 + 16)
                if g >= 4:
                    pe.wait_ge(out_made, g - 3)
                for j in range(4):
                    last = nc.tensor.transpose(ps[:, g % 4, j * P:(j + 1) * P], xm[:, 4 * (g % 2) + j, (g // 2) * P:(g // 2 + 1) * P], idm[:, :])
                last.then_inc(out_done, 1)

        @blk.scalar
        def _(act):
            ac = Chain(act, act_chain)

            def square(c, sq, source, ready):
                if ready:
                    act.wait_ge(*ready)
                if c:
                    act.wait_ge(sum_made, c)
                nc.scalar.activation(sq, source, ACT.Square).then_inc(sq_made, 1)

            def root(c, std, bank, width, count):
                act.wait_ge(ms_made, c + 1)
                if c:
                    act.wait_ge(rstd_made, c)
                nc.scalar.activation(std[:, 0:width], ps[:, bank, 0:width], ACT.Sqrt, bias=eps[:, 0:1], scale=1.0 / count).then_inc(std_made, 1)

            def pre_high(it, dst, tmp, shift):
                act.wait_ge(pre_t, it + 1)
                nc.scalar.activation(dst, tmp, ACT.Identity, bias=shift).then_inc(pre_hi, 1)

            act.wait_ge(vec_made, 1)
            nc.scalar.activation(sile[:, :], vec[:, V_C:V_C + 16], ACT.Exp, scale=-1.0).then_inc(sil_exp, 1)
            for l in range(2):
                act.wait_ge(hd_arg, l + 1)
                nc.scalar.activation((hd1, hd2)[l][:, :], hda[:, :], ACT.Sin).then_inc(hd_sin, 1)
            act.sem_inc(fs_free, 4)
            with act.Fori(0, ORDERS) as o:
                sent = [0] * 4

                def high(r):
                    act.wait_ge(fr_val, 16 * o + r + 1)
                    if r >= 2:
                        act.wait_ge(fs_done, FS_PER * o + RING_END[r - 2])
                    nc.scalar.activation(rg_hi[r % 2][:, :, :], val[r % 2][:, :, :], ACT.Copy).then_inc(fr_hi, 1)

                high(0)
                high(1)
                idx = 0
                for r in range(16):
                    c, n = RING[r % 8]
                    for _, _, f, plane in (s_groups if r < 8 else d_groups)(c):
                        q = idx % 4
                        act.wait_ge(fs_done, FS_PER * o + idx + 1)
                        if sent[q]:
                            act.wait_ge(ko_out[q], 16 * (KO_USES[q] * o + sent[q]))
                        if (f, plane) == (0, 1):
                            inst = nc.scalar.activation(ko[q][:, :], ps[:, q, :], ACT.Copy, scale=notop[:, 0:1])
                        else:
                            inst = nc.scalar.activation(ko[q][:, :], ps[:, q, :], ACT.Copy)
                        inst.then_inc(fs_free, 1)
                        act.wait_ge(fs_free, 4 + FS_PER * o + idx + 1)
                        if plane == 2:
                            act.wait_ge(ko_out[before], 16 * (KO_USES[before] * o + sent[before]))
                            act.dma_start(spec[bass.ds(((8 * o + f) * 3 + 2) * P, 1), half(n)], ko[q][0:1, :]).then_inc(ko_out[q], 16)
                            sent[q] += 1
                        else:
                            for pl in ((0, 2) if (f, plane) == (0, 0) else (plane,)):
                                act.dma_start(spec[bass.ds(((8 * o + f) * 3 + pl) * P, P), half(n)], ko[q][:, :]).then_inc(ko_out[q], 16)
                                sent[q] += 1
                        before = q
                        idx += 1
                    if r + 2 < 16:
                        high(r + 2)
                assert sent == KO_USES
                for q in range(4):
                    act.wait_ge(ko_out[q], 16 * (KO_USES[q] * o + KO_USES[q]))
            for n in range(2):
                square(N_LAT + n, asq[:, :, :], xa[:, :, half(n)], (xt_free, 15 + n))
                root(N_LAT + n, astd, 6 + n, HALF, D)
                for k in range(KT):
                    it = A_LAT + 8 * n + k
                    pre_high(it, hh[:, k, half(n)], atmp[it % 2][:, :], mod[:, k:k + 1])
            square(N_CTX, asq[:, :, 0:C], xc[:, :, :], (xt_free, 20))
            root(N_CTX, astd, 6, C, D)
            for k in range(KT):
                it = A_CTX + k
                pre_high(it, hch[:, k, :], atmp[it % 2][:, 0:C], mod[:, 48 + k:49 + k])
            for n in range(2):
                square(N_CQ + n, csq[:, :, :], cq[:, :, half(n)], (dn_free, 4))
                root(N_CQ + n, cstd, 6 + (n + 1) % 2, HALF, QR)
            for n in range(3):
                width = HALF if n < 2 else C
                cols = slice(n * HALF, n * HALF + width)
                square(N_CKV + n, csq[:, 0, 0:width], ckv[:, cols], (dn_free, 7))
                root(N_CKV + n, cstd, 6 + (n + 1) % 2, width, KVR)
            for k in range(2):
                act.wait_ge(cn_val, k + 1)
                nc.scalar.activation(cqh[:, k, :], cq[:, k, :], ACT.Copy).then_inc(cn_hi, 1)
            act.wait_ge(cn_val, 3)
            nc.scalar.activation(ckvh[:, :], ckv[:, :], ACT.Copy).then_inc(cn_hi, 1)
            for c in range(3):
                width = HALF if c < 2 else C
                cols = slice(c * HALF, c * HALF + width)
                act.wait_ge(kr_done, c + 1)
                for hd in range(2):
                    nc.scalar.activation(kh[NOPE:P, hd, cols], ps[NOPE:P, 3 + c, 0:width], ACT.Copy).then_inc(kr_hi, 1)
            def piece_high(g, j):
                bank = PIECE_BANK[j]
                if j < 4:
                    act.wait_ge(q_val, 4 * g + j + 1)
                    nc.scalar.activation(qh[:, j // 2, half(j % 2)], qf[j % 2][:, :], ACT.Copy).then_inc(pp_hi, 1)
                    return
                act.wait_ge(pp_done, 10 * g + j + 1)
                if j < 7:
                    width = HALF if j < 6 else C
                    cols = slice((j - 4) * HALF, (j - 4) * HALF + width)
                    for hd in range(2):
                        nc.scalar.activation(kh[0:NOPE, hd, cols], ps[NOPE * hd:NOPE * hd + NOPE, bank, 0:width], ACT.Copy).then_inc(pp_hi, 1)
                else:
                    t0 = 4 * (j - 7)
                    nt = min(10, t0 + 4) - t0
                    nc.scalar.activation(vh[:, t0:t0 + nt, :, :].rearrange("p t h v -> p (t h) v"),
                                         ps[:, bank, 0:nt * P].rearrange("p (g v) -> p g v", v=VD), ACT.Copy).then_inc(pp_hi, 1)

            def weights_of(g, u, j):
                act.wait_ge(max_made, 16 * g + 2 * u + j + 1)
                if u >= 2:
                    act.wait_ge(t_done, 40 * g + 5 * (u - 1))
                a = 2 * (u % 2) + j
                nc.scalar.activation(pr[:, u % 2, j, :], psf[:, j * KEYS:(j + 1) * KEYS], ACT.Exp, bias=mx[:, a:a + 1], scale=SCALE, accum_out=sm[:, a:a + 1]).then_inc(p_made, 1)

            def turned_high(g, u, jj):
                idx = 5 * u + jj
                act.wait_ge(t_done, 40 * g + idx + 1)
                if idx >= 4:
                    act.wait_ge(pv_done, 40 * g + idx - 3)
                nc.scalar.activation(pth[idx % 4][:, :, :], ps[:, 5 + idx % 2, :].rearrange("p (k q) -> p k q", k=2), ACT.Copy).then_inc(t_hi, 1)

            def inverse_sums(g, u):
                act.wait_ge(rt_done, 8 * g + u + 1)
                if u >= 1:
                    act.wait_ge(o_made, 8 * g + u)
                nc.scalar.activation(rc[:, :], ps[0:VD, 7, 256:512], ACT.Copy).then_inc(rc_made, 1)

            def group(g, more):
                weights_of(g, 0, 0)
                weights_of(g, 0, 1)
                for u in range(7):
                    turned_high(g, u, 0)
                    turned_high(g, u, 1)
                    weights_of(g, u + 1, 0)
                    turned_high(g, u, 2)
                    turned_high(g, u, 3)
                    turned_high(g, u, 4)
                    weights_of(g, u + 1, 1)
                    inverse_sums(g, u)
                turned_high(g, 7, 0)
                turned_high(g, 7, 1)
                if more:
                    piece_high(g + 1, 0)
                    piece_high(g + 1, 1)
                for jj in range(2, 5):
                    turned_high(g, 7, jj)
                    if more:
                        piece_high(g + 1, jj)
                if more:
                    piece_high(g + 1, 5)
                inverse_sums(g, 7)
                if more:
                    piece_high(g + 1, 6)
                    act.wait_ge(pv_done, 40 * g + 40)
                    for j in range(7, 10):
                        piece_high(g + 1, j)

            for j in range(10):
                piece_high(0, j)
            with act.Fori(0, HEADS // 4 - 1) as i:
                group(2 * i, True)
                group(2 * i + 1, True)
            group(HEADS // 2 - 2, True)
            group(HEADS // 2 - 1, False)
            act.wait_ge(o_made, 64)
            for k in range(KT):
                nc.scalar.activation(hh[:, k, :], ao[:, k, :], ACT.Copy).then_inc(oh_made, 1)

            def post_then_pre(post, pre, items, shift, ready):
                for n in range(2):
                    square(post + n, msq[:, :, :], y[:, :, half(n)], ready)
                    root(post + n, mstd, 6 + (post + n) % 2, HALF, D)
                if pre is None:
                    return
                for n in range(2):
                    square(pre + n, msq[:, :, :], xm[:, :, half(n)], (post_x, {N_PRE2: B_ATT, N_PREH: B_MLP0, N_PREM: B_HY}[pre] + 8 * n + 8))
                    root(pre + n, mstd, 6 + (pre + n) % 2, HALF, D)
                    for k in range(KT):
                        it = items + 8 * n + k
                        pre_high(it, hh[:, k, half(n)], mtmp[it % 2][:, :], mod[:, shift + k:shift + k + 1])

            def mlp(l):
                with act.Fori(0, NCHUNK) as j:
                    for g in range(8):
                        act.wait_ge(hid_free[l], 4 + 8 * j + g + 1)
                        if g >= 2:
                            act.wait_ge(hid_lo[l], 8 * j + g - 1)
                        nc.scalar.activation(ms2[g % 2][:, :], mr[g % 2][:, :], ACT.Square).then_inc(hid_sq[l], 1)
                        act.wait_ge(hid_sq[l], 8 * j + g + 1)
                        nc.scalar.activation(hidh[:, g // 2, half(g % 2)], ms2[g % 2][:, :], ACT.Copy).then_inc(hid_hi[l], 1)
                    act.wait_ge(acc_done[l], 16 * j + 16)

            post_then_pre(N_POST1, N_PRE2, A_MLP0, 24, (wo_free, 4 + 16))
            mlp(0)
            post_then_pre(N_POST2, N_PREH, A_HY, 64, (acc_free[0], 4 + 16 * NCHUNK))

            def send_u(i, s):
                act.wait_ge(ut_made, 4 + 4 * i + 2 * s + 2)
                act.dma_start(u_tm[bass.ds(2 * i + s, 1)].rearrange("m (a p) c -> (m p) a c", p=P), ut[s][:, :, :]).then_inc(ut_out[s], 16)

            def middle(i, s, first):
                act.wait_ge(wi_free, 4 + 4 * i + 2 * s + 2)
                if not first:
                    act.wait_ge(ut_done, 4 * i + 2 * s - 2)
                nc.scalar.activation(uc[s][:, :], ub[s][:, 1:T + 1], ACT.Identity, bias=vec[:, bass.ds(V_BSH + 2 * i + s, 1)],
                                     scale=vec[:, bass.ds(V_WSH + 24 + 2 * i + s, 1)]).then_inc(uc_mid, 1)

            middle(0, 0, True)
            middle(0, 1, True)
            send_u(0, 0)
            with act.Fori(1, 12) as i:
                middle(i, 0, False)
                send_u(i - 1, 1)
                middle(i, 1, False)
                send_u(i, 0)
            send_u(11, 1)
            act.sem_inc(ci_free, 8)
            with act.Fori(0, ORDERS) as o:
                def high(r, *read):
                    act.wait_ge(cr_val, 8 * o + r + 1)
                    if read:
                        act.wait_ge(*read)
                    nc.scalar.activation(rg_hi[r % 2][:, :, :], val[r % 2][:, :, :], ACT.Copy).then_inc(cr_hi, 1)

                for r, (c, n) in enumerate(RING):
                    high(r, *((cf_done, 32 * o + ring_read(c - 1, n)) if c else ()))

                def high_inverse(c, n):
                    if c == 0:
                        act.wait_ge(cf_done, 32 * o + ring_read(3, n))
                    else:
                        act.wait_ge(ci_done, 32 * o + ring_read(c - 1, n))
                    act.wait_ge(pz_made, 16 * o + 4 * c + 2 * n + 2)
                    nc.scalar.activation(rg_hi[n][:, :, :], pz[:, c, :, half(n)], ACT.Copy).then_inc(cr_hi, 1)

                high_inverse(0, 0)
                high_inverse(0, 1)
                for s in range(7):
                    c = (s + 1) // 2
                    for n, _, _, idx in transform_groups(s, True):
                        plane = idx % 4 if c == 0 else 2 * (1 - s % 2) + idx % 2
                        act.wait_ge(ci_done, 32 * o + idx + 1)
                        nc.scalar.activation(pz[:, c, plane, half(n)], ps[:, idx % 8, :], ACT.Copy).then_inc(ci_free, 1)
                        if c < 3 and idx + 1 == ring_read(c, n):
                            high_inverse(c + 1, n)
            for g in range(16):
                act.wait_ge(zt_done, g + 1)
                nc.scalar.activation(zh[:, g // 2, half(g % 2)], ps[:, g % 4, :], ACT.Copy).then_inc(z_hi, 1)
            post_then_pre(N_POSTH, N_PREM, A_MLP1, 64 + 24, (ho_free, 4 + 16))
            mlp(1)
            post_then_pre(N_POSTM, None, None, None, (acc_free[1], 4 + 16 * NCHUNK))

        @blk.vector
        def _(dve):
            dv = Chain(dve, dve_chain)
            tt, ts, stt = nc.vector.tensor_tensor, nc.vector.tensor_scalar, nc.vector.scalar_tensor_tensor

            def root_mean(c, sq, ssum, std, rstd, width):
                dve.wait_ge(sq_made, c + 1)
                if c:
                    dve.wait_ge(ms_made, c)
                nc.vector.tensor_reduce(ssum[:, 0:width], sq.rearrange("p k t -> p t k"), AXX, ALU.add).then_inc(sum_made, 1)
                dve.wait_ge(std_made, c + 1)
                nc.vector.reciprocal(rstd, std[:, 0:width]).then_inc(rstd_made, 1)
                dve.wait_ge(rstd_made, c + 1)

            def pre_apply(items, src_of, tmp_of, hi_of, lo_of, factor, rstd, shift):
                def low(it, k):
                    dve.wait_ge(pre_hi, it + 1)
                    stt(lo_of(k), tmp_of(it), shift(k), hi_of(k), ALU.add, ALU.subtract).then_inc(pre_lo, 1)

                for k in range(KT):
                    it = items + k
                    if it >= 2:
                        dve.wait_ge(pre_lo, it - 1)
                    stt(tmp_of(it), src_of(k), factor(k), rstd, ALU.mult, ALU.mult).then_inc(pre_t, 1)
                    if k:
                        low(it - 1, k - 1)
                low(items + KT - 1, KT - 1)

            nc.vector.memset(ones[:, :], 1.0).then_inc(ones_made, 1)
            dv.did(nc.vector.memset(eps[:, :], EPS))
            dv.did(nc.vector.memset(notop[:, :], 1.0))
            dv.wait()
            dv.did(nc.vector.memset(notop[0:1, :], 0.0))
            dve.wait_ge(vec_t, 1)
            nc.vector.tensor_copy(vec[:, :], ps[:, 0, 0:NVEC]).then_inc(vec_made, 1)
            dve.wait_ge(vec_made, 1)
            dve.wait_ge(sil_exp, 1)
            dv.did(ts(sile[:, :], sile[:, :], 1.0, None, ALU.add))
            dv.wait()
            dv.did(nc.vector.reciprocal(sile[:, :], sile[:, :]))
            dv.wait()
            dv.did(tt(sil[:, :], sile[:, :], vec[:, V_C:V_C + 16], ALU.mult))
            dv.wait()
            MAGIC = 12582912.0
            C1 = 6.28125
            C2 = float(np.float32(2 * math.pi - C1))
            C3 = 2 * math.pi - C1 - C2
            PI = float(np.nextafter(np.float32(math.pi), np.float32(0)))
            for l in range(2):
                dve.wait_ge(hd_done, l + 1)
                if l:
                    dve.wait_ge(hd_sin, 1)
                dv.did(ts(hda[:, :], ps[0:FH, 2:4, :].rearrange("p b n -> p (b n)"), vec[0:FH, V_FB1 + l:V_FB1 + l + 1], vec[0:FH, V_FREQ:V_FREQ + 1], ALU.add, ALU.mult))
                dv.wait()
                dv.did(ts(hdn[:, :], hda[:, :], 1 / (2 * math.pi), MAGIC, ALU.mult, ALU.add))
                dv.wait()
                dv.did(ts(hdn[:, :], hdn[:, :], MAGIC, None, ALU.subtract))
                for part in (C1, C2, C3):
                    dv.wait()
                    dv.did(stt(hda[:, :], hdn[:, :], -part, hda[:, :], ALU.mult, ALU.add))
                dv.wait()
                ts(hda[:, :], hda[:, :], PI, -PI, ALU.min, ALU.max).then_inc(hd_arg, 1)
            def factors(l):
                m, g = 64 * l, V_NORMG + 32 * l
                for j, col in ((0, 8), (2, 32)):
                    dv.did(stt(fac[:, 32 * l + 8 * j:32 * l + 8 * j + 8], mod[:, m + col:m + col + 8], 1.0, vec[:, g + 8 * j:g + 8 * j + 8], ALU.add, ALU.mult))
                for j, col in ((1, 16), (3, 40)):
                    dv.did(tt(fac[:, 32 * l + 8 * j:32 * l + 8 * j + 8], mod[:, m + col:m + col + 8], vec[:, g + 8 * j:g + 8 * j + 8], ALU.mult))
                if l == 0:
                    dv.did(stt(fac[:, 64:72], mod[:, 56:64], 1.0, vec[:, g:g + 8], ALU.add, ALU.mult))
                dv.wait()

            for n in range(2 * KT):
                k, h = n // 2, n % 2
                dve.wait_ge(ada_in[n % 4], 16 * (n // 4 + 1))
                if k:
                    dve.wait_ge(ada_acc, n - 1)
                if h == 0:
                    if k == 0:
                        dv.did(ts(aaccc[:, :], araw[n % 4][:, 0:2 * D], sil[:, 8 + k:9 + k], None, ALU.mult))
                    else:
                        dv.wait()
                        dv.did(stt(aaccc[:, :], araw[n % 4][:, 0:2 * D], sil[:, 8 + k:9 + k], aaccc[:, :], ALU.mult, ALU.add))
                acc = aacc[:, h * 3 * D:(h + 1) * 3 * D]
                if k == 0:
                    ts(acc, araw[n % 4][:, :], sil[:, k:k + 1], None, ALU.mult).then_inc(ada_acc, 1)
                else:
                    stt(acc, araw[n % 4][:, :], sil[:, k:k + 1], acc, ALU.mult, ALU.add).then_inc(ada_acc, 1)
            dve.wait_ge(ada_sum, 1)
            dv.did(tt(mod[:, 0:48], ps[:, 1, 0:48], vec[:, V_ADAB:V_ADAB + 48], ALU.add))
            dv.did(tt(mod[:, 48:64], ps[:, 1, 48:64], vec[:, V_ADAB:V_ADAB + 16], ALU.add))
            dv.wait()
            factors(0)
            dve.sem_inc(hf_free, 4)

            def operand(c, n, x4, v, made):
                q, s, x0, x2 = bq[:, :, half(n)], bs[:, :, half(n)], x4[:, 0, :, half(n)], x4[:, 2, :, half(n)]
                re, im = v[:, 0:2, :], v[:, 2:4, :]
                if c == 0:
                    dv.did(tt(re, x0, x2, ALU.add))
                    dv.wait()
                    dv.did(tt(im, re, q, ALU.subtract))
                    dv.wait()
                    tt(re, re, q, ALU.add).then_inc(made, 1)
                elif c == 2:
                    dv.did(tt(re, x0, x2, ALU.subtract))
                    nc.vector.tensor_copy(im, s).then_inc(made, 1)
                else:
                    r4 = R4 if c == 1 else -R4
                    dv.did(stt(re, s, r4, x0, ALU.mult, ALU.add))
                    stt(im, q, R4, x2, ALU.mult, ALU.add if c == 1 else ALU.subtract).then_inc(made, 1)

            def butterflies(x4, ready):
                if ready:
                    dve.wait_ge(*ready)
                dv.did(tt(bq[:, :, :], x4[:, 1, :, :], x4[:, 3, :, :], ALU.add))
                dv.did(tt(bs[:, :, :], x4[:, 1, :, :], x4[:, 3, :, :], ALU.subtract))
                dv.wait()

            with dve.Fori(0, ORDERS) as o:
                dv.enter(o, 2 + 16 + 2 * (2 + 10))
                for t in range(TT):
                    dve.wait_ge(dec_in[t % 2], 16 * (4 * o + t // 2 + 1))
                    for j in range(4):
                        dve.wait_ge(hf_done, 32 * o + 4 * t + j + 1)
                        tt(fb[:, j // 2, half(j % 2)], ps[:, 4 + j, :], dec[t % 2][:, half(j % 2)], ALU.mult).then_inc(hf_free, 1)
                    dve.wait_ge(hf_free, 4 + 32 * o + 4 * t + 4)
                    if t == 0:
                        dv.did(nc.vector.memset(fb[0:1, 1, :], 0.0))
                        dv.did(tt(fb[0:1, 0, :], fb[0:1, 0, :], fbias[0:1, bass.ds(o * D, D)], ALU.add))
                        dv.wait()
                    dv.did(tt(f_s[:, t // 2, t % 2, :], fb[:, 0, :], fb[:, 1, :], ALU.add))
                    dv.did(tt(f_d[:, t // 2, t % 2, :], fb[:, 0, :], fb[:, 1, :], ALU.subtract))
                    dv.wait()
                for rnd, x4 in ((0, f_s), (1, f_d)):
                    butterflies(x4, (fr_lo, 16 * o + 8) if rnd else None)

                    def low(r):
                        dve.wait_ge(fr_hi, 16 * o + 8 * rnd + r + 1)
                        tt(rg_lo[r % 2][:, :, :], val[r % 2][:, :, :], rg_hi[r % 2][:, :, :], ALU.subtract).then_inc(fr_lo, 1)

                    operand(*RING[0], x4, val[0], fr_val)
                    operand(*RING[1], x4, val[1], fr_val)
                    for r in range(8):
                        low(r)
                        if r + 2 < 8:
                            dve.wait_ge(fr_lo, 16 * o + 8 * rnd + r + 1)
                            operand(*RING[r + 2], x4, val[r % 2], fr_val)
                dve.wait_ge(fr_lo, 16 * o + 16)
                dv.leave(ORDERS)
            for g in range(20):
                dve.wait_ge(xt_done, g + 1)
                if g < 16:
                    nc.vector.tensor_copy(xa[:, g // 2, half(g % 2)], ps[:, g % 4, :]).then_inc(xt_free, 1)
                else:
                    nc.vector.tensor_copy(xc[:, 2 * (g - 16):2 * (g - 16) + 2, :], ps[:, g % 4, :].rearrange("p (k t) -> p k t", k=2)).then_inc(xt_free, 1)
            for n in range(2):
                rs = arstd[:, half(n)]
                root_mean(N_LAT + n, asq[:, :, :], assum, astd, rs, HALF)
                pre_apply(A_LAT + 8 * n, lambda k: xa[:, k, half(n)], lambda it: atmp[it % 2][:, :], lambda k: hh[:, k, half(n)],
                          lambda k: hl[:, k, half(n)], lambda k: fac[:, k:k + 1], rs, lambda k: mod[:, k:k + 1])
            rs = arstd[:, T:KEYS]
            root_mean(N_CTX, asq[:, :, 0:C], assum, astd, rs, C)
            pre_apply(A_CTX, lambda k: xc[:, k, :], lambda it: atmp[it % 2][:, 0:C], lambda k: hch[:, k, :], lambda k: hcl[:, k, :],
                      lambda k: fac[:, 64 + k:65 + k], rs, lambda k: mod[:, 48 + k:49 + k])
            g = 0
            dve.wait_ge(tab_in, 32)
            for s in range(4):
                for n in range(3 if s >= 2 else 2):
                    width = HALF if n < 2 else C
                    cols = slice(n * HALF, n * HALF + width)
                    dve.wait_ge(dn_done, g + 1)
                    bank = ps[:, g % 6, 0:width]
                    if s < 2:
                        nc.vector.tensor_copy(cq[:, s, cols], bank).then_inc(dn_free, 1)
                    elif s == 2:
                        nc.vector.tensor_copy(ckv[:, cols], bank).then_inc(dn_free, 1)
                    else:
                        tt(krt[:, cols], bank, rtab[:, cols], ALU.mult).then_inc(dn_free, 1)
                    g += 1
            dve.wait_ge(dn_free, 10)
            dve.sem_inc(kr_made, 3)
            for n in range(2):
                root_mean(N_CQ + n, csq[:, :, :], cssum, cstd, crstd[:, half(n)], HALF)
            for k in range(2):
                stt(cq[:, k, :], cq[:, k, :], vec[:, V_GQ + k:V_GQ + k + 1], crstd[:, 0:T], ALU.mult, ALU.mult).then_inc(cn_val, 1)
            dve.wait_ge(cn_val, 2)
            for n in range(3):
                width = HALF if n < 2 else C
                root_mean(N_CKV + n, csq[:, 0:1, 0:width], cssum, cstd, crstd[:, n * HALF:n * HALF + width], width)
            stt(ckv[:, :], ckv[:, :], vec[:, V_GKV:V_GKV + 1], crstd[:, :], ALU.mult, ALU.mult).then_inc(cn_val, 1)
            for k in range(2):
                dve.wait_ge(cn_hi, k + 1)
                tt(cql[:, k, :], cq[:, k, :], cqh[:, k, :], ALU.subtract).then_inc(cn_lo, 1)
            dve.wait_ge(cn_hi, 3)
            dve.wait_ge(cn_val, 3)
            tt(ckvl[:, :], ckv[:, :], ckvh[:, :], ALU.subtract).then_inc(cn_lo, 1)
            for c in range(3):
                width = HALF if c < 2 else C
                cols = slice(c * HALF, c * HALF + width)
                for hd in range(2):
                    dve.wait_ge(kr_hi, 2 * c + 2)
                    tt(kl[NOPE:P, hd, cols], ps[NOPE:P, 3 + c, 0:width], kh[NOPE:P, hd, cols], ALU.subtract).then_inc(kr_lo, 1)
            dve.wait_ge(kr_lo, 6)
            dve.wait_ge(x_saved, 16)
            dve.sem_inc(pp_free, 4)

            def query_value(g, j):
                dve.wait_ge(pp_done, 10 * g + j + 1)
                if j >= 2:
                    dve.wait_ge(q_lo, 4 * g + j - 1)
                tt(qf[j % 2][:, :], ps[:, j % 4, :], rtab[:, half(j % 2)], ALU.mult).then_inc(q_val, 1)
                dve.wait_ge(q_val, 4 * g + j + 1)
                dve.sem_inc(pp_free, 1)

            def query_low(g, j):
                dve.wait_ge(pp_hi, 13 * g + j + 1)
                tt(ql[:, j // 2, half(j % 2)], qf[j % 2][:, :], qh[:, j // 2, half(j % 2)], ALU.subtract).then_inc(q_lo, 1)

            def key_low(g, j):
                width = HALF if j < 6 else C
                cols = slice((j - 4) * HALF, (j - 4) * HALF + width)
                for hd in range(2):
                    dve.wait_ge(pp_hi, 13 * g + 4 + 2 * (j - 4) + 2)
                    inst = tt(kl[0:NOPE, hd, cols], ps[NOPE * hd:NOPE * hd + NOPE, j % 4, 0:width], kh[0:NOPE, hd, cols], ALU.subtract)
                    inst.then_inc(pp_free if hd else k_lo, 1)

            def value_low(g, j):
                t0 = 4 * (j - 7)
                nt = min(10, t0 + 4) - t0
                dve.wait_ge(pp_hi, 13 * g + 10 + (j - 7) + 1)
                tt(vl[:, t0:t0 + nt, :, :].rearrange("p t h v -> p (t h) v"), ps[:, PIECE_BANK[j], 0:nt * P].rearrange("p (g v) -> p g v", v=VD),
                   vh[:, t0:t0 + nt, :, :].rearrange("p t h v -> p (t h) v"), ALU.subtract).then_inc(pp_free, 1)

            def maximum(g, u, j):
                a = 2 * (u % 2) + j
                dve.wait_ge(s_done, 16 * g + 2 * u + j + 1)
                if u >= 2:
                    dve.wait_ge(p_made, 16 * g + 2 * u + j - 3)
                nc.vector.reduce_max(mxr[:, a:a + 1], psf[:, j * KEYS:(j + 1) * KEYS], AXX).then_inc(raw_max, 1)
                dve.wait_ge(raw_max, 16 * g + 2 * u + j + 1)
                ts(mx[:, a:a + 1], mxr[:, a:a + 1], -SCALE, None, ALU.mult).then_inc(max_made, 1)

            def turned_low(g, u, jj):
                idx = 5 * u + jj
                dve.wait_ge(t_hi, 40 * g + idx + 1)
                tt(ptl[idx % 4][:, :, :], ps[:, 5 + idx % 2, :].rearrange("p (k q) -> p k q", k=2), pth[idx % 4][:, :, :], ALU.subtract).then_inc(t_free, 1)

            def inverse_sum(g, u):
                a = 2 * (u % 2)
                if u >= 1:
                    dve.wait_ge(rb_made, 16 * g + 2 * u)
                nc.vector.reciprocal(inv_sum[:, :], sm[:, a:a + 2]).then_inc(rs_made, 1)
                dve.wait_ge(rs_made, 8 * g + u + 1)
                for j in range(2):
                    ts(rb[:, j, :], ones[:, 0:VD], inv_sum[:, j:j + 1], None, ALU.mult).then_inc(rb_made, 1)

            def result(g, u):
                dve.wait_ge(rc_made, 8 * g + u + 1)
                hd, q = u // 4, u % 4
                feature = slice(g, g + 1) if isinstance(g, int) else bass.ds(g, 1)
                tt(ao[VD * hd:VD * hd + VD, feature, q * 256:(q + 1) * 256], ps[0:VD, 7:8, 0:256],
                   rc[:, :].rearrange("p (a q) -> p a q", a=1), ALU.mult).then_inc(o_made, 1)

            def group(g, more):
                maximum(g, 0, 0)
                maximum(g, 0, 1)
                for u in range(7):
                    maximum(g, u + 1, 0)
                    turned_low(g, u, 0)
                    turned_low(g, u, 1)
                    inverse_sum(g, u)
                    turned_low(g, u, 2)
                    maximum(g, u + 1, 1)
                    turned_low(g, u, 3)
                    turned_low(g, u, 4)
                    result(g, u)
                turned_low(g, 7, 0)
                turned_low(g, 7, 1)
                inverse_sum(g, 7)
                if not more:
                    for jj in range(2, 5):
                        turned_low(g, 7, jj)
                    result(g, 7)
                    return
                query_value(g + 1, 0)
                query_value(g + 1, 1)
                turned_low(g, 7, 2)
                query_low(g + 1, 0)
                query_value(g + 1, 2)
                turned_low(g, 7, 3)
                query_low(g + 1, 1)
                query_value(g + 1, 3)
                turned_low(g, 7, 4)
                query_low(g + 1, 2)
                query_low(g + 1, 3)
                key_low(g + 1, 4)
                key_low(g + 1, 5)
                result(g, 7)
                key_low(g + 1, 6)
                for j in range(7, 10):
                    value_low(g + 1, j)

            for j in range(4):
                query_value(0, j)
                if j:
                    query_low(0, j - 1)
            query_low(0, 3)
            for j in range(4, 7):
                key_low(0, j)
            for j in range(7, 10):
                value_low(0, j)
            with dve.Fori(0, HEADS // 4 - 1) as i:
                group(2 * i, True)
                group(2 * i + 1, True)
            group(HEADS // 2 - 2, True)
            group(HEADS // 2 - 1, False)
            dve.wait_ge(o_made, 64)
            for k in range(KT):
                dve.wait_ge(oh_made, k + 1)
                tt(hl[:, k, :], ao[:, k, :], hh[:, k, :], ALU.subtract).then_inc(ol_made, 1)

            def post_apply(items, factor, rstd, n):
                for k in range(KT):
                    stt(y[:, k, half(n)], y[:, k, half(n)], factor(k), rstd, ALU.mult, ALU.mult).then_inc(post_y, 1)
                    if k:
                        dve.wait_ge(post_y, items + k)
                        tt(xm[:, k - 1, half(n)], xm[:, k - 1, half(n)], y[:, k - 1, half(n)], ALU.add).then_inc(post_x, 1)
                dve.wait_ge(post_y, items + KT)
                tt(xm[:, KT - 1, half(n)], xm[:, KT - 1, half(n)], y[:, KT - 1, half(n)], ALU.add).then_inc(post_x, 1)

            def post_then_pre(post, pre, b_items, a_items, f_post, f_pre, shift):
                for n in range(2):
                    rs = mrstd[:, half(n)]
                    root_mean(post + n, msq[:, :, :], mssum, mstd, rs, HALF)
                    post_apply(b_items + 8 * n, lambda k: fac[:, f_post + k:f_post + k + 1], rs, n)
                if pre is None:
                    return
                dve.wait_ge(post_x, b_items + 16)
                for n in range(2):
                    rs = mrstd[:, half(n)]
                    root_mean(pre + n, msq[:, :, :], mssum, mstd, rs, HALF)
                    pre_apply(a_items + 8 * n, lambda k: xm[:, k, half(n)], lambda it: mtmp[it % 2][:, :], lambda k: hh[:, k, half(n)],
                              lambda k: hl[:, k, half(n)], lambda k: fac[:, f_pre + k:f_pre + k + 1], rs, lambda k: mod[:, shift + k:shift + k + 1])

            def mlp(l):
                dv.did(nc.vector.memset(y[:, :, :], 0.0))
                dv.wait()
                dve.sem_inc(hid_free[l], 4)
                dve.sem_inc(acc_free[l], 4)
                if l == 0:
                    dve.wait_ge(pre_lo, A_MLP0 + 16)
                    dve.sem_inc(ada1_acc, 1)
                    dve.sem_inc(ada1_mod, 1)
                with dve.Fori(0, NCHUNK) as j:
                    def modulation(b):
                        dve.wait_ge(ada1_in, 16 * (ABLOCKS * j + b + 1))
                        for k in range(KT):
                            dve.wait_ge(ada1_acc, 1 + KT * (ABLOCKS * j + b) + k)
                            if k == 0:
                                if b == 0:
                                    dve.wait_ge(ada1_mod, j + 1)
                                ts(bacc[:, b, :], braw[:, k, :], sil[:, k:k + 1], None, ALU.mult).then_inc(ada1_acc, 1)
                            else:
                                stt(bacc[:, b, :], braw[:, k, :], sil[:, k:k + 1], bacc[:, b, :], ALU.mult, ALU.add).then_inc(ada1_acc, 1)

                    def low(g):
                        dve.wait_ge(hid_hi[l], 8 * j + g + 1)
                        tt(hidl[:, g // 2, half(g % 2)], ms2[g % 2][:, :], hidh[:, g // 2, half(g % 2)], ALU.subtract).then_inc(hid_lo[l], 1)

                    for g in range(8):
                        dve.wait_ge(hid_done[l], 8 * j + g + 1)
                        ts(mr[g % 2][:, :], ps[:, g % 4, :], 0.0, None, ALU.max).then_inc(hid_free[l], 1)
                        if g:
                            low(g - 1)
                        if l == 0 and g == 4:
                            modulation(0)
                    low(7)
                    if l == 0:
                        modulation(1)
                    dve.wait_ge(acc_free[l], 4 + 16 * j)
                    for q in range(16):
                        s, n, m = q // 4, q // 2 % 2, q % 2
                        dve.wait_ge(acc_done[l], 16 * j + q + 1)
                        dst = y[:, 2 * s + m, half(n)]
                        tt(dst, ps[:, 4 + 2 * n + m, :], dst, ALU.add).then_inc(acc_free[l], 1)
                        if l == 0 and q == 5:
                            modulation(2)
                        if l == 0 and q == 12:
                            dve.wait_ge(ada1_sum, j + 1)
                            cols = ABLOCKS * ACOLS // P
                            tt(mod[:, bass.ds(64 + cols * j, cols)], ps[:, 0, 0:cols], vec[:, bass.ds(V_ADAB + 48 + cols * j, cols)], ALU.add).then_inc(ada1_mod, 1)
                dve.wait_ge(acc_free[l], 4 + 16 * NCHUNK)
                if l == 0:
                    dve.wait_ge(ada1_mod, 1 + NCHUNK)
                    factors(1)

            dve.sem_inc(wo_free, 4)
            with dve.Fori(0, 4) as i:
                for g in range(4):
                    dve.wait_ge(wo_done, 4 * i + g + 1)
                    nc.vector.tensor_copy(y[:, bass.ds(2 * i + g // 2, 1), half(g % 2)], ps[:, g:g + 1, :]).then_inc(wo_free, 1)
            dve.wait_ge(x_back, 16)
            post_then_pre(N_POST1, N_PRE2, B_ATT, A_MLP0, 8, 16, 24)
            mlp(0)
            post_then_pre(N_POST2, N_PREH, B_MLP0, A_HY, 24, 32, 64)
            for s in range(2):
                dv.did(nc.vector.memset(ub[s][:, 0:1], 0.0))
                dv.did(nc.vector.memset(ub[s][:, T + 1:T + 2], 0.0))
            dv.wait()
            dve.sem_inc(wi_free, 4)
            dve.sem_inc(ut_made, 4)

            def outer(i, s):
                dve.wait_ge(uc_mid, 2 * i + s + 1)
                stt(uc[s][:, :], ub[s][:, 0:T], vec[:, bass.ds(V_WSH + 2 * i + s, 1)], uc[s][:, :], ALU.mult, ALU.add).then_inc(uc_left, 1)
                dve.wait_ge(uc_left, 2 * i + s + 1)
                stt(uc[s][:, :], ub[s][:, 2:T + 2], vec[:, bass.ds(V_WSH + 48 + 2 * i + s, 1)], uc[s][:, :], ALU.mult, ALU.add).then_inc(uc_made, 1)

            def take(i, s, first):
                for n in range(2):
                    dve.wait_ge(ut_done, 4 * i + 2 * s + n + 1)
                    if not first:
                        dve.wait_ge(ut_out[s], 16 * i)
                    nc.vector.tensor_copy(ut[s][:, 4 * n:4 * n + 4, :], ps[:, 4 + 2 * s + n, :].rearrange("p (q c) -> p q c", q=4)).then_inc(ut_made, 1)

            def biased(i, s, first):
                for n in range(2):
                    dve.wait_ge(wi_done, 4 * i + 2 * s + n + 1)
                    if not first:
                        dve.wait_ge(uc_made, 2 * i + s - 1)
                    ts(ub[s][:, 1 + n * HALF:1 + (n + 1) * HALF], ps[:, 2 * s + n, :], vec[:, bass.ds(V_BIN + 2 * i + s, 1)], None, ALU.add).then_inc(wi_free, 1)

            biased(0, 0, True)
            outer(0, 0)
            biased(0, 1, True)
            take(0, 0, True)
            outer(0, 1)
            biased(1, 0, False)
            take(0, 1, True)
            outer(1, 0)
            with dve.Fori(1, 11) as i:
                biased(i, 1, False)
                take(i, 0, False)
                outer(i, 1)
                biased(i + 1, 0, False)
                take(i, 1, False)
                outer(i + 1, 0)
            biased(11, 1, False)
            take(11, 0, False)
            outer(11, 1)
            take(11, 1, False)
            dve.wait_ge(src_in, 16 * KT)
            with dve.Fori(0, ORDERS) as o:
                dv.enter(o, 2 + 10 + 16 * 4 + 14 + 4)

                def low(c, n):
                    dve.wait_ge(cr_hi, 16 * o + 2 * c + n + 1)
                    tt(rg_lo[n][:, :, :], val[n][:, :, :], rg_hi[n][:, :, :], ALU.subtract).then_inc(cr_lo, 1)

                def value(c, n):
                    if c:
                        dve.wait_ge(cr_lo, 16 * o + 2 * (c - 1) + n + 1)
                    operand(c, n, src, val[n], cr_val)

                def product(p):
                    f, n = pair_tile(p)
                    gr, gi = pair_groups(p)
                    c, m = f // 2, f % 2
                    re, im = (2 * m, 2 * m + 1) if c == 0 else (m, 2 + m)
                    k = ks[p % 2]
                    ur, ui = ps[:, gr % 8, :], ps[:, gi % 8, :]
                    pr_, pi_ = pz[:, c, re, half(n)], pz[:, c, im, half(n)]
                    dve.wait_ge(k_in[p % 2], 16 * (8 * o + p // 2 + 1))
                    if f == 0:
                        dve.wait_ge(k_ny_in, 16 * (2 * o + n + 1))
                    dve.wait_ge(cf_done, 32 * o + gi + 1)
                    dv.did(tt(pr_, ur, k[:, 0, :], ALU.mult))
                    dv.did(tt(pi_, ur, k[:, 1, :], ALU.mult))
                    dv.did(tt(pt[0][:, :], ui, k[:, 1, :], ALU.mult))
                    tt(pt[1][:, :], ui, k[:, 2 if f == 0 else 0, :], ALU.mult).then_inc(cf_free, 1)
                    dv.wait()
                    dv.did(tt(pr_, pr_, pt[0][:, :], ALU.subtract))
                    dve.wait_ge(cf_free, 16 * o + p + 1)
                    tt(pi_, pi_, pt[1][:, :], ALU.add).then_inc(pz_made, 1)
                    dve.wait_ge(pz_made, 16 * o + p + 1)
                    dv.wait()

                butterflies(src, None)
                value(0, 0)
                value(0, 1)
                low(0, 0)
                low(0, 1)
                value(1, 0)
                value(1, 1)
                for c in range(4):
                    for n in range(2):
                        product(4 * c + 2 * n)
                        if c < 3:
                            low(c + 1, n)
                        if c < 2:
                            value(c + 2, n)
                        product(4 * c + 2 * n + 1)
                for c in range(4):
                    for n in range(2):
                        dve.wait_ge(cr_hi, 16 * o + 8 + 2 * c + n + 1)
                        tt(rg_lo[n][:, :, :], pz[:, c, :, half(n)], rg_hi[n][:, :, :], ALU.subtract).then_inc(cr_lo, 1)
                dve.wait_ge(ci_free, 8 + 32 * o + 32)
                y0, y1, y2, y3 = (src[:, a, :, :] for a in range(4))
                z0, z4 = pz[:, 0, 0:2, :], pz[:, 0, 2:4, :]
                (r1, i1), (r2, i2), (r3, i3) = ((pz[:, c, 0:2, :], pz[:, c, 2:4, :]) for c in (1, 2, 3))
                dv.did(tt(y0, z0, z4, ALU.add))
                dv.did(tt(y1, z0, z4, ALU.subtract))
                dv.wait()
                dv.did(tt(z0, r1, r3, ALU.add))
                dv.did(tt(z4, r1, r3, ALU.subtract))
                dv.wait()
                dv.did(tt(r1, i1, i3, ALU.add))
                dv.did(tt(r3, i3, i1, ALU.subtract))
                dv.did(tt(y2, y0, r2, ALU.subtract))
                dv.wait()
                dv.did(tt(y0, y0, r2, ALU.add))
                dv.did(stt(i1, z4, R4, i2, ALU.mult, ALU.subtract))
                dv.wait()
                dv.did(stt(y1, r1, -R4, y1, ALU.mult, ALU.add))
                dv.did(tt(y0, y0, z0, ALU.add))
                dv.did(tt(y2, y2, r3, ALU.add))
                dv.wait()
                dv.did(tt(y3, y1, i1, ALU.subtract))
                dv.wait()
                dv.did(tt(y1, y1, i1, ALU.add))
                dv.wait()
                dve.wait_ge(gate_in, 16 * KT * (o + 1))
                for a in range(4):
                    dv.did(tt(src[:, a, :, :], src[:, a, :, :], gate[:, a, :, :], ALU.mult))
                dv.wait()
                dve.sem_inc(z_made, 1)
                dv.leave(ORDERS)
            for g in range(16):
                dve.wait_ge(z_hi, g + 1)
                tt(zl[:, g // 2, half(g % 2)], ps[:, g % 4, :], zh[:, g // 2, half(g % 2)], ALU.subtract).then_inc(z_lo, 1)
            dve.wait_ge(z_lo, 16)
            dve.sem_inc(ho_free, 4)
            with dve.Fori(0, 4) as i:
                for g in range(4):
                    dve.wait_ge(ho_done, 4 * i + g + 1)
                    ts(y[:, bass.ds(2 * i + g // 2, 1), half(g % 2)], ps[:, g:g + 1, :], vec[:, bass.ds(V_BOUT + 2 * i + g // 2, 1)], None, ALU.add).then_inc(ho_free, 1)
            dve.wait_ge(x_back, 32)
            post_then_pre(N_POSTH, N_PREM, B_HY, A_MLP1, 40, 48, 64 + 24)
            mlp(1)
            post_then_pre(N_POSTM, None, B_MLP1, None, 56, None, None)
            for g in range(16):
                t = g // 2
                dve.wait_ge(out_done, g + 1)
                if t >= 2:
                    dve.wait_ge(out_sent[t % 2], 16 * (t // 2))
                nc.vector.tensor_copy(ot[t % 2][:, half(g % 2)], ps[:, g % 4, :]).then_inc(out_made, 1)


def kernel(x, c, ctx, c_ctx, ada_w, ada_b, norm_g, mla_w_dq, mla_g_q, mla_w_uq, mla_w_dkv,
           mla_g_kv, mla_w_ukv, mla_w_o, hy_w_in, hy_b_in, hy_w_short, hy_b_short, hy_f_w1,
           hy_f_b1, hy_f_w2, hy_f_b2, hy_f_w3, hy_f_freq, hy_bias, hy_w_out, hy_b_out,
           mlp_w1, mlp_w2):
    import concourse.bacc as bacc
    from concourse.bass_utils import run_bass_kernel_spmd

    def arr(a):
        return np.ascontiguousarray(np.asarray(a))

    (x, c, ctx, c_ctx, ada_w, ada_b, norm_g, w_dq, g_q, w_uq, w_dkv, g_kv, w_ukv, w_o, w_in, b_in, w_sh, b_sh,
     f_w1, f_b1, f_w2, f_b2, f_w3, freq, hbias, w_out, b_out, w1, w2) = map(arr, (
         x, c, ctx, c_ctx, ada_w, ada_b, norm_g, mla_w_dq, mla_g_q, mla_w_uq, mla_w_dkv, mla_g_kv, mla_w_ukv,
         mla_w_o, hy_w_in, hy_b_in, hy_w_short, hy_b_short, hy_f_w1, hy_f_b1, hy_f_w2, hy_f_b2, hy_f_w3,
         hy_f_freq, hy_bias, hy_w_out, hy_b_out, mlp_w1, mlp_w2))

    def row(v):
        return np.concatenate([v.reshape(1, FH), np.zeros((1, P - FH), v.dtype)], axis=1)

    rows = [v.reshape(-1, P) for v in (ada_b, norm_g, b_in, w_sh, b_sh, b_out, g_q, g_kv, c, c_ctx)]
    rows += [row(f_b1), row(f_b2), row(freq)]
    used = sum(r.shape[0] for r in rows)
    vecs = np.concatenate(rows + [np.zeros((NVEC - used, P), x.dtype)], axis=0)

    kr = w_dkv[0][:, KVR:]
    swap = np.concatenate([kr[:, 16:], kr[:, :16]], axis=1)
    w_down = np.concatenate([w_dq[0], w_dkv[0][:, :KVR], w_dkv[0][:, :64], kr, swap], axis=1)

    uq = w_uq[0].reshape(2, P, HEADS, NOPE + ROPE)
    uq = np.concatenate([uq, uq[..., NOPE + 16:], uq[..., NOPE:NOPE + 16]], axis=3)
    ukv = w_ukv[0].reshape(P, HEADS, NOPE + VD)
    w_head = np.zeros((HEADS // 2, P, 8, P), x.dtype)
    for g in range(HEADS // 2):
        for k in range(2):
            for h in range(2):
                w_head[g, :, 2 * k + h] = uq[k, :, 2 * g + h]
        w_head[g, :, 4] = ukv[:, 2 * g:2 * g + 2, :NOPE].reshape(P, P)
        w_head[g, :, 5] = ukv[:, 2 * g:2 * g + 2, NOPE:].reshape(P, P)

    fwd, inv = dft_steps()
    ins = dict(x=x[0], ctx=ctx[0], vecs=vecs, ada_w=ada_w, w_down=w_down, w_head=w_head.reshape(HEADS // 2, P, 8 * P),
               w_o=w_o[0], w_in=w_in[0], w_out=w_out[0], mlp_w1=w1, mlp_w2=w2, f_w1=f_w1[0], f_w2=f_w2[0], f_w3=f_w3[0],
               hy_bias=hbias[0], rope=rope_table(), ropesum=rope_sum(), ident=np.eye(P, dtype=np.float32),
               zpos=filter_positions(), decay=filter_decay(), dft_fwd=fwd, dft_inv=inv)
    nc = bacc.Bacc("TRN2", target_bir_lowering=False, num_devices=1)
    arrays, aps = {}, {}
    for name, a in ins.items():
        a = np.ascontiguousarray(a)
        arrays[f"in_{name}"] = a
        aps[name] = nc.dram_tensor(f"in_{name}", a.shape, mybir.dt.from_np(a.dtype), kind="ExternalInput").ap()
    aps["out"] = nc.dram_tensor("out_y", (T, D), F32, kind="ExternalOutput").ap()
    build_program(nc, **aps)
    res = run_bass_kernel_spmd(nc, [arrays], core_ids=[0])
    return res.results[0]["out_y"].reshape(1, T, D)
```

```python
import math

import numpy as np

import concourse.bass as bass
import concourse.mybir as mybir

F32 = mybir.dt.float32
F32R = mybir.dt.float32r
ALU = mybir.AluOpType
ACT = mybir.ActivationFunctionType
AXX = mybir.AxisListType.X

P = 128
D = 1024
T = 1024
C = 256
KEYS = T + C
KT = D // P
TT = T // P
HALF = 512
HEADS = 16
NOPE, ROPE, VD = 64, 32, 64
QR, KVR = 256, 128
FF = 4 * D
CHUNK = 512
NCHUNK = FF // CHUNK
HIDT = CHUNK // P
EMB, FH = 33, 64
EPS = 1e-6
GRID_W, ROPE_BASE = 64, 10000.0
SCALE = 1.0 / math.sqrt(NOPE + ROPE)
ORDERS = 2
NFFT = 2 * T
R4 = math.sqrt(0.5)

V_ADAB = 0
V_NORMG = 96
V_BIN = 160
V_WSH = 184
V_BSH = 256
V_BOUT = 280
V_GQ = 288
V_GKV = 290
V_C = 291
V_FB1, V_FB2, V_FREQ = 307, 308, 309
NVEC = 384



def rope_table():
    t = np.arange(T)
    inv = ROPE_BASE ** (-np.arange(ROPE // 4) / (ROPE // 4))
    ang = np.concatenate([(t // GRID_W)[:, None] * inv, (t % GRID_W)[:, None] * inv], axis=1).T
    out = np.zeros((P, KEYS))
    out[:NOPE] = 1.0
    out[NOPE:NOPE + 16, :T] = out[NOPE + 16:NOPE + 32, :T] = np.cos(ang)
    out[NOPE + 32:NOPE + 48, :T] = -np.sin(ang)
    out[NOPE + 48:, :T] = np.sin(ang)
    out[NOPE:NOPE + 32, T:] = 1.0
    return out.astype(np.float32)


def rope_sum():
    m = np.zeros((P, P), np.float32)
    for j in range(ROPE):
        for o in (NOPE + j, NOPE + ROPE + j):
            m[NOPE + j, o] = m[NOPE + ROPE + j, o] = 1.0
    return m


def filter_positions():
    t = np.linspace(0.0, 1.0, T, dtype=np.float32).astype(np.float64)[:, None]
    w = (2.0 * math.pi) * np.arange(T)[:, None] / T
    f = np.linspace(1e-4, (EMB - 1) // 2 - 1, (EMB - 1) // 2)[None, :]
    return np.concatenate([t, np.cos(f * w), -np.sin(f * w)], axis=1).T.astype(np.float32).copy()


def filter_decay():
    t = np.linspace(0.0, 1.0, T)[:, None]
    deltas = np.linspace(math.log(1e-2) / 1.5, math.log(1e-2) / 0.3, D)
    return np.exp(-t * np.abs(deltas)[None, :]).astype(np.float32)


def dft_steps():
    b = np.arange(256)[:, None]
    fwd = np.zeros((7, P, 8, P))
    inv = np.zeros((7, P, 8, P))

    def cut(m, i, j):
        return m[i * P:(i + 1) * P, j * P:(j + 1) * P]

    f0 = 8 * np.arange(P)[None, :]
    f4 = f0 + 4
    ang0, ang4 = 2 * np.pi * b * f0 / NFFT, 2 * np.pi * b * f4 / NFFT
    c0, s0, c4, s4 = np.cos(ang0), -np.sin(ang0), np.cos(ang4), -np.sin(ang4)
    s0[:, 0] = (-1.0) ** b[:, 0]
    for k in range(2):
        for n, m in enumerate((c0, s0, c4, s4)):
            fwd[0, :, 2 * n + k] = cut(m, k, 0)
    i0, j0 = 2 * c0.T / NFFT, 2 * s0.T / NFFT
    i0[0] /= 2
    j0[0] /= 2
    i4, j4 = 2 * c4.T / NFFT, 2 * s4.T / NFFT
    for m in range(2):
        for n, (re, im) in enumerate(((i0, j0), (i4, j4))):
            inv[0, :, 4 * n + 2 * m] = cut(re, 0, m)
            inv[0, :, 4 * n + 2 * m + 1] = cut(im, 0, m)
    for c in (1, 2, 3):
        f = c + 8 * np.arange(256)[None, :]
        ang = 2 * np.pi * b * f / NFFT
        co, si = np.cos(ang), np.sin(ang)
        ic, isn = 2 * co.T / NFFT, 2 * si.T / NFFT
        for m in range(2):
            for k in range(2):
                fwd[2 * c - 1, :, 4 * m + k] = cut(co, k, m)
                fwd[2 * c - 1, :, 4 * m + 2 + k] = cut(-si, k, m)
                fwd[2 * c, :, 4 * m + k] = cut(-si, k, m)
                fwd[2 * c, :, 4 * m + 2 + k] = cut(-co, k, m)
                inv[2 * c - 1, :, 4 * m + k] = cut(ic, k, m)
                inv[2 * c - 1, :, 4 * m + 2 + k] = cut(-isn, k, m)
                inv[2 * c, :, 4 * m + k] = cut(isn, k, m)
                inv[2 * c, :, 4 * m + 2 + k] = cut(ic, k, m)
    return (fwd.reshape(7, P, 8 * P).astype(np.float32), inv.reshape(7, P, 8 * P).astype(np.float32))



FIXED = 16512
KB = 1024

N_CQ, N_CKV = 0, 2
N_LAT, N_CTX, N_POST1, N_PRE2, N_POST2, N_PREH, N_POSTH, N_PREM, N_POSTM = 0, 2, 3, 5, 7, 9, 11, 13, 15
N_END = 17


def token_tiles(i):
    return 2 if i == N_CTX else 4


SPREAD_END = [sum(token_tiles(a) for a in range(i + 1)) for i in range(N_END)]
A_LAT, A_CTX, A_MLP0, A_HY, A_MLP1 = 0, 16, 24, 40, 56
B_ATT, B_MLP0, B_HY, B_MLP1 = 0, 16, 32, 48
W_FILT = 0
W_DOWN = W_FILT + 16
W_HEAD = W_DOWN + 4
W_O = W_HEAD + 8
W_MLP0 = W_O + 8
W_IN = W_MLP0 + 8 * NCHUNK
W_CONV = W_IN + 24
W_OUT = W_CONV + 28
W_MLP1 = W_OUT + 8

AQUART = 6 * D // 4
ABLOCKS = 3
ACOLS = 6 * D // (ABLOCKS * NCHUNK)


class Chain:

    def __init__(self, eng, sem):
        self.eng, self.sem, self.base, self.n = eng, sem, 0, 0

    def did(self, inst):
        inst.then_inc(self.sem, 1)
        self.n += 1

    def wait(self):
        self.eng.wait_ge(self.sem, self.base + self.n)

    def enter(self, i, per):
        self.before, self.per = self.base + self.n, per
        self.base, self.n = self.before + i * per, 0

    def leave(self, rounds):
        assert self.n == self.per, (self.n, self.per)
        self.base, self.n = self.before + rounds * self.per, 0


def build_program(nc, x, ctx, vecs, ada_w, w_down, w_head, w_o, w_in, w_out, mlp_w1, mlp_w2,
                  f_w1, f_w2, f_w3, hy_bias, rope, ropesum, ident, zpos, decay, dft_fwd, dft_inv, out):
    at = [FIXED]

    def fixed(name, shape, dt=F32):
        off = at[0]
        at[0] += -(-int(np.prod(shape[1:])) * 4 // 32) * 32
        return nc.alloc_sbuf_tensor_at(name, list(shape), dt, offset=off)

    raw = [fixed(f"w_raw{s}", [P, 1024]) for s in range(2)]
    whi = [fixed(f"w_hi{s}", [P, 8, P], F32R) for s in range(2)]
    wlo = [fixed(f"w_lo{s}", [P, 8, P], F32R) for s in range(2)]
    idm = fixed("idm", [P, P])
    ones = fixed("ones", [P, P])
    vec = fixed("vec", [P, NVEC])
    mod = fixed("mod", [P, 112])
    fac = fixed("fac", [P, 72])
    sil = fixed("sil", [P, 16])
    sile = fixed("sile", [P, 16])
    eps = fixed("eps", [P, 1])
    nrec = [fixed(f"nrec{s}", [P, 4]) for s in range(2)]
    mx = fixed("mx", [P, 4])
    mxr = fixed("mxr", [P, 4])
    sm = fixed("sm", [P, 4])
    inv_sum = fixed("inv_sum", [P, 2])
    zero = fixed("zero", [P, 1])
    notop = fixed("notop", [P, 1])
    ARENA = -(-at[0] // 64) * 64

    def arena(name, kb, shape, dt=F32):
        return nc.alloc_sbuf_tensor_at(name, list(shape), dt, offset=ARENA + int(kb * KB))

    f_s = arena("f_s", 0, [P, 4, 2, D])
    f_d = arena("f_d", 32, [P, 4, 2, D])
    rg_hi = [arena(f"rg_hi{s}", 64 + 16 * s, [P, 4, HALF], F32R) for s in range(2)]
    rg_lo = [arena(f"rg_lo{s}", 72 + 16 * s, [P, 4, HALF], F32R) for s in range(2)]
    bq = arena("bq", 96, [P, 2, D])
    bs = arena("bs", 104, [P, 2, D])
    val = [arena(f"val{s}", 112 + 8 * s, [P, 4, HALF]) for s in range(2)]
    fb = [arena(f"fb{s}", off, [P, 2, D]) for s, off in enumerate((128, 120))]
    dec = [arena(f"dec{s}", 136 + 4 * s, [P, D]) for s in range(2)]
    fw3 = arena("fw3", 144, [FH, 2 * D])
    fbias = arena("fbias", 152, [1, 2 * D])
    ko = [arena(f"ko{s}", 160 + 2 * s, [P, HALF]) for s in range(4)]
    hda = arena("hda", 168, [FH, T])
    hdn = arena("hdn", 172, [FH, T])
    hd2 = arena("hd2", 176, [FH, T])
    zp = arena("zp", 128, [EMB, T])
    hd1 = arena("hd1", 132, [FH, T])
    fw12 = arena("fw12", 136, [FH, 2, FH])
    vrow = arena("vrow", 64, [P, NVEC // P, P])
    aacc = [arena(f"aacc{s}", 160 + 8 * s, [P, AQUART]) for s in range(2)]
    aaccc = arena("aaccc", 66, [P, 2 * D])
    araw = [arena(f"araw{s}", 90 + 6 * s, [P, AQUART]) for s in range(5)]
    xa = arena("xa", 0, [P, KT, T])
    xtm = arena("xtm", 128, [P, TT, D])
    xctm = arena("xctm", 168, [P, 2, D])
    xc = arena("xc", 144, [P, KT, C])
    hh = arena("hh", 32, [P, KT, T], F32R)
    hl = arena("hl", 64, [P, KT, T], F32R)
    hch = arena("hch", 96, [P, KT, C], F32R)
    hcl = arena("hcl", 104, [P, KT, C], F32R)
    asq = arena("asq", 112, [P, KT, HALF])
    atmp = [arena(f"atmp{s}", 136 + 2 * s, [P, HALF]) for s in range(2)]
    aspread = arena("aspread", 140, [P, 4, P])
    anstd = arena("anstd", 142, [P, HALF])
    cq = arena("cq", 144, [P, 2, T])
    ckv = arena("ckv", 152, [P, KEYS])
    krt = arena("krt", 112, [P, KEYS])
    cqh = arena("cqh", 118, [P, 2, T], F32R)
    cql = arena("cql", 126, [P, 2, T], F32R)
    ckvh = arena("ckvh", 134, [P, KEYS], F32R)
    ckvl = arena("ckvl", 139, [P, KEYS], F32R)
    rtab = arena("rtab", 160, [P, KEYS])
    rsm = arena("rsm", 117, [P, P])
    csq = arena("csq", 165, [P, 2, HALF])
    crstd = arena("crstd", 169, [P, KEYS])
    cssum = arena("cssum", 174, [P, HALF])
    cstd = arena("cstd", 176, [P, HALF])
    ao = arena("ao", 0, [P, KT, T])
    qh = arena("qh", 32, [P, 2, T], F32R)
    ql = arena("ql", 40, [P, 2, T], F32R)
    kh = arena("kh", 48, [P, 2, KEYS], F32R)
    kl = arena("kl", 58, [P, 2, KEYS], F32R)
    vh = arena("vh", 68, [P, 10, 2, VD], F32R)
    vl = arena("vl", 78, [P, 10, 2, VD], F32R)
    pr = arena("pr", 88, [P, 2, 2, KEYS])
    pth = [arena(f"pth{s}", 144 + 2 * s, [P, 2, 256], F32R) for s in range(4)]
    ptl = [arena(f"ptl{s}", 152 + 2 * s, [P, 2, 256], F32R) for s in range(4)]
    qf = [arena(f"qf{s}", 165 + 2 * s, [P, HALF]) for s in range(2)]
    rc = arena("rc", 169, [VD, 256])
    rb = arena("rb", 170, [P, 2, VD])
    xm = arena("xm", 128, [P, KT, T])
    y = arena("y", 96, [P, KT, T])
    hidh = arena("hidh", 0, [P, HIDT, T], F32R)
    hidl = arena("hidl", 16, [P, HIDT, T], F32R)
    msq = arena("msq", 0, [P, KT, HALF])
    mr = [arena(f"mr{s}", 160 + 2 * s, [P, HALF]) for s in range(2)]
    ms2 = [arena(f"ms2{s}", 164 + 2 * s, [P, HALF]) for s in range(2)]
    mtmp = [arena(f"mtmp{s}", 172 + 2 * s, [P, HALF]) for s in range(2)]
    mnstd = arena("mnstd", 176, [P, HALF])
    mspread = arena("mspread", 178, [P, 4, P])
    bacc = arena("bacc", 176, [P, ABLOCKS, ACOLS])
    braw = arena("braw", 168, [P, KT, ACOLS])
    ub = [arena(f"ub{s}", 96 + 5 * s, [P, T + 2]) for s in range(2)]
    uc = [arena(f"uc{s}", 106 + 4 * s, [P, T]) for s in range(2)]
    ut = [arena(f"ut{s}", 172 + 4 * s, [P, TT, P]) for s in range(2)]
    src = arena("src", 128, [P, 4, 2, D])
    pz = arena("pz", 0, [P, 4, 4, D])
    ks = [arena(f"ks{s}", 160 + 6 * s, [P, 3, HALF]) for s in range(2)]
    pt = [arena(f"pt{s}", 172 + 4 * s, [P, 2, HALF]) for s in range(2)]
    gate = arena("gate", 0, [P, 4, 2, D])
    zh = arena("zh", 0, [P, KT, T], F32R)
    zl = arena("zl", 32, [P, KT, T], F32R)
    ot = [arena(f"ot{s}", 4 * s, [P, D]) for s in range(2)]

    ps = nc.alloc_psum_tensor("ps", [P, 8, HALF], F32)
    psf = ps[:, :, :].rearrange("p b n -> p (b n)")

    x_spill = nc.dram_tensor("x_spill", [KT, P, T], F32, kind="Internal").ap()
    spec = nc.dram_tensor("spec", [ORDERS * 8 * 3 * P, D], F32, kind="Internal").ap()
    u_tm = nc.dram_tensor("u_tm", [3 * KT, T, P], F32, kind="Internal").ap()

    names = set()

    def sem(name):
        assert name not in names
        names.add(name)
        return nc.alloc_semaphore(name)

    w_arrived = [sem(f"w_arrived{s}") for s in range(2)]
    w_hi_made, w_staged = sem("w_hi_made"), sem("w_staged")
    const_in, filt_in, filt_w3_in = sem("const_in"), sem("filt_in"), sem("filt_w3_in")
    dec_in = [sem(f"dec_in{s}") for s in range(2)]
    vec_t, vec_made, sil_exp = sem("vec_t"), sem("vec_made"), sem("sil_exp")
    ones_made, zero_made = sem("ones_made"), sem("zero_made")
    dve_chain = sem("dve_chain")
    ada_in = [sem(f"ada_in{s}") for s in range(5)]
    ada1_in, ada1_acc, ada1_sum, ada1_mod = sem("ada1_in"), sem("ada1_acc"), sem("ada1_sum"), sem("ada1_mod")
    ada_acc, ada_sum = sem("ada_acc"), sem("ada_sum")
    hd_done, hd_arg, hd_sin = sem("hd_done"), sem("hd_arg"), sem("hd_sin")
    hf_done, hf_free = sem("hf_done"), sem("hf_free")
    fs_done, fs_free = sem("fs_done"), sem("fs_free")
    fb_made, fd_made = sem("fb_made"), sem("fd_made")
    fr_val, fr_hi, fr_lo = sem("fr_val"), sem("fr_hi"), sem("fr_lo")
    ko_out = [sem(f"ko_out{s}") for s in range(4)]
    x_in, xt_done, xt_free = sem("x_in"), sem("xt_done"), sem("xt_free")
    sq_made, sum_made, ms_made, std_made, rstd_made = sem("sq_made"), sem("sum_made"), sem("ms_made"), sem("std_made"), sem("rstd_made")
    nsq_made, nsum_made, nstd_made, nrec_made = sem("nsq_made"), sem("nsum_made"), sem("nstd_made"), sem("nrec_made")
    std_turned, spread_made, turned_made = sem("std_turned"), sem("spread_made"), sem("turned_made")
    pre_t, pre_hi, pre_lo, post_y, post_x = sem("pre_t"), sem("pre_hi"), sem("pre_lo"), sem("post_y"), sem("post_x")
    post_xp, y_zero = sem("post_xp"), sem("y_zero")
    x_saved, x_back = sem("x_saved"), sem("x_back")
    dn_done, dn_free = sem("dn_done"), sem("dn_free")
    cn_hi, cn_val, cn_lo = sem("cn_hi"), sem("cn_val"), sem("cn_lo")
    kr_made, kr_done, kr_hi, kr_lo = sem("kr_made"), sem("kr_done"), sem("kr_hi"), sem("kr_lo")
    tab_in = sem("tab_in")
    pp_done, pp_free, q_val, pp_hi = sem("pp_done"), sem("pp_free"), sem("q_val"), sem("pp_hi")
    q_lo, k_lo, raw_max, uc_left = sem("q_lo"), sem("k_lo"), sem("raw_max"), sem("uc_left")
    s_done, max_made, p_made = sem("s_done"), sem("max_made"), sem("p_made")
    t_done, t_hi, t_free = sem("t_done"), sem("t_hi"), sem("t_free")
    pv_done, rc_made, o_made = sem("pv_done"), sem("rc_made"), sem("o_made")
    rs_made, rb_made, rt_done = sem("rs_made"), sem("rb_made"), sem("rt_done")
    oh_made, ol_made = sem("oh_made"), sem("ol_made")
    wo_done, wo_free = sem("wo_done"), sem("wo_free")
    hid_done, hid_free = [sem(f"hid_done{i}") for i in range(2)], [sem(f"hid_free{i}") for i in range(2)]
    hid_sq, hid_hi, hid_lo = [sem(f"hid_sq{i}") for i in range(2)], [sem(f"hid_hi{i}") for i in range(2)], [sem(f"hid_lo{i}") for i in range(2)]
    acc_done, acc_free = [sem(f"acc_done{i}") for i in range(2)], [sem(f"acc_free{i}") for i in range(2)]
    wi_done, wi_free, uc_mid, uc_made, ut_done, ut_made = (sem("wi_done"), sem("wi_free"), sem("uc_mid"), sem("uc_made"), sem("ut_done"), sem("ut_made"))
    ut_out = [sem(f"ut_out{s}") for s in range(2)]
    src_in, k_ny_in, gate_in = sem("src_in"), sem("k_ny_in"), sem("gate_in")
    k_in = [sem(f"k_in{s}") for s in range(2)]
    cf_done, cf_free = sem("cf_done"), sem("cf_free")
    ci_done, ci_free = sem("ci_done"), sem("ci_free")
    cr_val, cr_hi, cr_lo = sem("cr_val"), sem("cr_hi"), sem("cr_lo")
    pz_made, z_made = sem("pz_made"), sem("z_made")
    zt_done, z_hi, z_lo = sem("zt_done"), sem("z_hi"), sem("z_lo")
    out_done, out_made = sem("out_done"), sem("out_made")
    out_sent = [sem(f"out_sent{s}") for s in range(2)]
    ho_done, ho_free = sem("ho_done"), sem("ho_free")

    def w_tiles(ap):
        return ap.rearrange("(k p) m -> p k m", p=P)

    RING = [(c, n) for c in range(4) for n in range(2)]
    def s_groups(c):
        if c == 0:
            return [((0, 1), (0, 1), 0, 0), ((2, 3), (0, 1), 0, 2), ((4, 5), (2, 3), 1, 0)]
        return [((4 * m, 4 * m + 1, 4 * m + 2, 4 * m + 3), (0, 1, 2, 3), 2 * c + m, 0) for m in range(2)]

    def d_groups(c):
        if c == 0:
            return [((2, 3), (0, 1), 0, 1), ((6, 7), (2, 3), 1, 1)]
        return [((4 * m, 4 * m + 1, 4 * m + 2, 4 * m + 3), (0, 1, 2, 3), 2 * c + m, 1) for m in range(2)]

    S_CNT = [len(s_groups(c)) for c, _ in RING]
    D_CNT = [len(d_groups(c)) for c, _ in RING]
    FS_PER = sum(S_CNT) + sum(D_CNT)
    S_END = [sum(S_CNT[:i + 1]) for i in range(8)]
    D_END = [sum(S_CNT) + sum(D_CNT[:i + 1]) for i in range(8)]
    RING_END = S_END + D_END

    FS_GROUPS = [(c, n, *g) for groups in (s_groups, d_groups) for c, n in RING for g in groups(c)]
    KO_USES = [sum(2 if g[4:] == (0, 0) else 1 for g in FS_GROUPS[q::4]) for q in range(4)]
    STEP_END = [8 + 4 * s for s in range(7)]

    PIECE_BANK = (0, 1, 2, 3, 0, 1, 2, 3, 5, 6)

    def half(n):
        return slice(n * HALF, (n + 1) * HALF)

    def transform_groups(s, inverse):
        out = []
        for n in range(2):
            if s == 0:
                for q in range(4):
                    out.append((n, (2 * q, 2 * q + 1), (2 * (q // 2), 2 * (q // 2) + 1), 4 * n + q))
            else:
                for m in range(2):
                    out.append((n, tuple(range(4 * m, 4 * m + 4)), (0, 1, 2, 3), STEP_END[s - 1] + 2 * n + m))
        return out

    def pair_tile(p):
        return (p % 2, p // 2) if p < 4 else (2 * (p // 4) + p % 2, p % 4 // 2)

    def pair_groups(p):
        if p < 4:
            return 2 * p, 2 * p + 1
        return 8 * (p // 4) + p % 4, 8 * (p // 4) + 4 + p % 4

    def ring_read(c, n):
        return 4 * (n + 1) if c == 0 else 8 * c + 6 + 2 * n

    def filter_step_src(o8):
        return (0, 1, 3, 5, 0, 2, 4, 6)[o8]

    block = nc.Block()
    with block as blk:

        @blk.sync
        def _(sp):
            def load(slot, s, source, shape=None):
                if not (isinstance(s, int) and s < 2):
                    sp.wait_ge(w_staged, s - 1)
                dst = raw[slot][:, :]
                if shape:
                    dst = dst.rearrange("p (k m) -> p k m", k=shape)
                sp.dma_start(dst, source).then_inc(w_arrived[slot], 16)

            sp.dma_start(vrow[:, :, :], vecs.rearrange("(a p) c -> p a c", p=P)).then_inc(const_in, 16)
            sp.dma_start(idm[:, :], ident).then_inc(const_in, 16)
            sp.dma_start(zp[:, :], zpos).then_inc(filt_in, 16)
            sp.dma_start(fw12[0:EMB, 0, :], f_w1).then_inc(filt_in, 16)
            sp.dma_start(fw12[:, 1, :], f_w2).then_inc(filt_in, 16)
            sp.dma_start(fbias[:, :], hy_bias.rearrange("(a o) d -> a (o d)", a=1)).then_inc(filt_in, 16)

            def modulation_weights(n):
                q, k = n // KT, n % KT
                if n >= 5:
                    sp.wait_ge(ada_acc, n - 4)
                sp.dma_start(araw[n % 5][:, :], ada_w[0, k * P:(k + 1) * P, q * AQUART:(q + 1) * AQUART]).then_inc(ada_in[n % 5], 16)

            for n in range(5):
                modulation_weights(n)
            sp.wait_ge(hd_sin, 2)
            for o in range(ORDERS):
                if o:
                    sp.wait_ge(hf_done, 32 * o)
                sp.dma_start(fw3[:, :], f_w3[:, o * 2 * D:(o + 1) * 2 * D]).then_inc(filt_w3_in, 16)
                for t in range(TT):
                    if 8 * o + t >= 2:
                        sp.wait_ge(hf_free, 4 + 4 * (8 * o + t - 1))
                    sp.dma_start(dec[t % 2][:, :], decay[t * P:(t + 1) * P, :]).then_inc(dec_in[t % 2], 16)
                    if o == 0 and t >= 1:
                        for n in range(4 * t + 1, 4 * t + 5):
                            if n < 4 * KT:
                                modulation_weights(n)
                    if t < 2:
                        load(t % 2, W_FILT + 8 * o + t, dft_fwd[filter_step_src(t)])
                for s in range(2, 8):
                    load(s % 2, W_FILT + 8 * o + s, dft_fwd[filter_step_src(s)])
                    if o == ORDERS - 1 and s == 3:
                        sp.wait_ge(fb_made, 8 * ORDERS)
                        sp.wait_ge(fd_made, 8 * ORDERS)
                        sp.dma_start(xtm[:, :, :], x.rearrange("(a p) d -> p a d", p=P)).then_inc(x_in, 16)
                        sp.dma_start(xctm[:, :, :], ctx.rearrange("(a p) d -> p a d", p=P)).then_inc(x_in, 16)
            for q in range(4):
                sp.wait_ge(ko_out[q], 16 * ORDERS * KO_USES[q])
            for s in range(4):
                load(s % 2, W_DOWN + s, w_tiles(w_down)[:, :, s * P:(s + 1) * P], 8)
            sp.wait_ge(xt_free, 20)
            sp.dma_start(rtab[:, :], rope).then_inc(tab_in, 16)
            sp.wait_ge(pre_t, A_LAT + 16)
            sp.dma_start(x_spill.rearrange("k p t -> p k t"), xa[:, :, :]).then_inc(x_saved, 16)
            sp.wait_ge(pre_lo, A_CTX + 8)
            sp.dma_start(rsm[:, :], ropesum).then_inc(tab_in, 16)
            for s in range(2):
                load(s % 2, W_HEAD + s, w_head[s])
            with sp.Fori(1, HEADS // 4) as i:
                for s in range(2):
                    load(s, W_HEAD + 2 * i + s, w_head[bass.ds(2 * i + s, 1)].rearrange("a p n -> (a p) n"))
            for s in range(2):
                load(s, W_O + s, w_tiles(w_o)[:, :, s * P:(s + 1) * P], 8)
            with sp.Fori(1, 4) as i:
                for s in range(2):
                    load(s, W_O + 2 * i + s, w_tiles(w_o)[:, :, bass.ds((2 * i + s) * P, P)], 8)
            sp.wait_ge(ol_made, 8)
            sp.wait_ge(x_saved, 16)
            sp.dma_start(xm[:, :, :], x_spill.rearrange("k p t -> p k t")).then_inc(x_back, 16)

            def mlp(layer, base):
                w1 = w_tiles(mlp_w1[layer])
                w2 = mlp_w2[layer].rearrange("(c k p) m -> c p k m", k=HIDT, p=P)

                def step(j, s):
                    if s < 4:
                        load(s % 2, base + 8 * j + s, w1[:, :, bass.ds((4 * j + s) * P, P)], 8)
                    else:
                        load(s % 2, base + 8 * j + s, w2[bass.ds(j, 1), :, :, (s - 4) * 256:(s - 3) * 256].rearrange("c p k m -> (c p) k m"), 4)

                with sp.Fori(0, NCHUNK) as j:
                    for s in range(8):
                        if layer == 0 and s in (2, 5, 7):
                            b = (2, 5, 7).index(s)
                            sp.wait_ge(ada1_acc, 1 + KT * (ABLOCKS * j + b))
                            sp.dma_start(braw[:, :, :], ada_w[1].rearrange("(k p) n -> p k n", p=P)[:, :, bass.ds((ABLOCKS * j + b) * ACOLS, ACOLS)]).then_inc(ada1_in, 16)
                        step(j, s)

            mlp(0, W_MLP0)
            for s in range(2):
                load(s, W_IN + s, w_tiles(w_in)[:, :, s * P:(s + 1) * P], 8)
            sp.wait_ge(pre_t, A_HY + 16)
            sp.dma_start(x_spill.rearrange("k p t -> p k t"), xm[:, :, :]).then_inc(x_saved, 16)
            def input_weights(i):
                for s in range(2):
                    load(s, W_IN + 2 * i + s, w_tiles(w_in)[:, :, bass.ds((2 * i + s) * P, P)], 8)

            def token_major(dst, first, arrived):
                for k in range(KT):
                    sp.dma_start(dst[:, :, :, k * P:(k + 1) * P].rearrange("p a b c -> p (a b) c"),
                                 u_tm[bass.ds(first + k, 1)].rearrange("m (a p) c -> (m p) a c", p=P)).then_inc(arrived, 16)

            with sp.Fori(1, 8) as i:
                input_weights(i)
            sp.wait_ge(x_saved, 32)
            for s in range(2):
                sp.wait_ge(ut_out[s], 16 * 4)
            token_major(src, 0, src_in)
            with sp.Fori(8, 12) as i:
                input_weights(i)
            for s in range(2):
                sp.wait_ge(ut_out[s], 16 * 12)
            with sp.Fori(0, ORDERS) as o:
                def conv_weights(s):
                    load(s % 2, W_CONV + 14 * o + s, dft_fwd[s])

                def inverse_weights(s):
                    load((7 + s) % 2, W_CONV + 14 * o + 7 + s, dft_inv[s])

                def spectrum(p):
                    f, n = pair_tile(p)
                    if p >= 2:
                        sp.wait_ge(cf_free, 16 * o + p - 1)
                    rows = spec[bass.ds((8 * o + f) * 3 * P, 2 * P), half(n)]
                    sp.dma_start(ks[p % 2][:, 0:2, :], rows.rearrange("(a p) d -> p a d", p=P)).then_inc(k_in[p % 2], 16)
                    if f == 0:
                        sp.dma_start(ks[p % 2][:, 2, :], spec[bass.ds(((8 * o + f) * 3 + 2) * P, P), half(n)]).then_inc(k_ny_in, 16)

                conv_weights(0)
                spectrum(0)
                spectrum(1)
                conv_weights(1)
                spectrum(2)
                spectrum(3)
                for c in (1, 2, 3):
                    conv_weights(2 * c)
                    spectrum(4 * c)
                    spectrum(4 * c + 1)
                    if c < 3:
                        conv_weights(2 * c + 1)
                    else:
                        inverse_weights(0)
                        inverse_weights(1)
                    spectrum(4 * c + 2)
                    spectrum(4 * c + 3)
                for s in range(2, 7):
                    if s == 5:
                        sp.wait_ge(cr_lo, 16 * o + 8 + 4)
                        token_major(gate, KT * (o + 1), gate_in)
                    inverse_weights(s)
            for s in range(2):
                load(s, W_OUT + s, w_tiles(w_out)[:, :, s * P:(s + 1) * P], 8)
            sp.wait_ge(z_lo, 16)
            sp.dma_start(xm[:, :, :], x_spill.rearrange("k p t -> p k t")).then_inc(x_back, 16)
            with sp.Fori(1, 4) as i:
                for s in range(2):
                    load(s, W_OUT + 2 * i + s, w_tiles(w_out)[:, :, bass.ds((2 * i + s) * P, P)], 8)
            mlp(1, W_MLP1)
            for t in range(TT):
                sp.wait_ge(out_made, 2 * t + 2)
                sp.dma_start(out[t * P:(t + 1) * P, :], ot[t % 2][:, :]).then_inc(out_sent[t % 2], 16)
            for s in range(2):
                sp.wait_ge(out_sent[s], 16 * 4)

        @blk.gpsimd
        def _(pool):
            nc.gpsimd.memset(zero[:, :], 0.0).then_inc(zero_made, 1)
            pool.wait_ge(zero_made, 1)

            def stage(slot, s, uses, read=None):
                pool.wait_ge(w_arrived[slot], 16 * uses)
                if read:
                    pool.wait_ge(*read)
                hi, lo = (w[slot][:, :, :].rearrange("p k m -> p (k m)") for w in (whi, wlo))
                nc.gpsimd.tensor_tensor(hi, raw[slot][:, :], zero[:, 0:1].to_broadcast([P, 1024]), ALU.add).then_inc(w_hi_made, 1)
                pool.wait_ge(w_hi_made, s + 1)
                nc.gpsimd.tensor_tensor(lo, raw[slot][:, :], hi, ALU.subtract).then_inc(w_staged, 1)

            def uses(s):
                return s // 2 + 1

            done = {}
            for o in range(ORDERS):
                for s in range(8):
                    r = 2 * s + 1
                    done[W_FILT + 8 * o + s] = (fs_done, FS_PER * o + RING_END[r])
            for s, n in enumerate((2, 4, 7, 10)):
                done[W_DOWN + s] = (dn_done, n)
            for g in range(8):
                done[W_HEAD + g] = (pp_done, 10 * g + 10)
            for s in range(8):
                done[W_O + s] = (wo_done, 2 * s + 2)
                done[W_OUT + s] = (ho_done, 2 * s + 2)
            for l, base in enumerate((W_MLP0, W_MLP1)):
                for s in (6, 7):
                    done[base + 8 * (NCHUNK - 1) + s] = (acc_done[l], 16 * (NCHUNK - 1) + 4 * (s - 3))
            for s in range(24):
                done[W_IN + s] = (wi_done, 2 * s + 2)
            for s in (12, 13):
                done[W_CONV + 14 + s] = (ci_done, 32 + STEP_END[s - 7])
            for o in range(ORDERS):
                for s in range(W_FILT + 8 * o, W_FILT + 8 * (o + 1)):
                    stage(s % 2, s, uses(s), done.get(s - 2))
                    if s == W_FILT + 8 * o + 1:
                        for t in range(TT):
                            pool.wait_ge(fb_made, 8 * o + t + 1)
                            nc.gpsimd.tensor_tensor(f_d[:, t // 2, t % 2, :], fb[t % 2][:, 0, :], fb[t % 2][:, 1, :], ALU.subtract).then_inc(fd_made, 1)
            for s in range(W_DOWN, W_HEAD + 2):
                stage(s % 2, s, uses(s), done.get(s - 2))
            with pool.Fori(1, 4) as i:
                for s in range(2):
                    stage(s, W_HEAD + 2 * i + s, W_HEAD // 2 + i + 1, (pp_done, 20 * i + 10 * s - 10))
            for s in range(W_O, W_O + 2):
                stage(s % 2, s, uses(s), done[s - 2])
            with pool.Fori(1, 4) as i:
                for s in range(2):
                    stage(s, W_O + 2 * i + s, W_O // 2 + i + 1, (wo_done, 4 * i + 2 * s - 2))

            def residual(items):
                for n in range(2):
                    for k in range(1, KT, 2):
                        pool.wait_ge(post_y, items + 8 * n + k + 1)
                        nc.gpsimd.tensor_tensor(xm[:, k, half(n)], xm[:, k, half(n)], y[:, k, half(n)], ALU.add).then_inc(post_xp, 1)

            def mlp(l, base):
                def step(j, s):
                    if s < 6:
                        read = (hid_done[l], 8 * j + 2 * (s - 1))
                    else:
                        read = (acc_done[l], 16 * j + 4 * (s - 5))
                    stage(s % 2, base + 8 * j + s, base // 2 + 4 * j + s // 2 + 1, read)

                for s in range(2):
                    stage(s, base + s, uses(base + s), done[base + s - 2])
                items = (B_ATT, B_HY)[l]
                residual(items)
                pool.wait_ge(post_x, items // 2 + 8)
                pool.wait_ge(post_xp, items // 2 + 8)
                nc.gpsimd.memset(y[:, :, :], 0.0).then_inc(y_zero, 1)
                with pool.Fori(0, NCHUNK - 1) as j:
                    for s in range(2, 10):
                        step(j, s)
                for s in range(2, 8):
                    step(NCHUNK - 1, s)

            mlp(0, W_MLP0)
            for s in range(W_IN, W_IN + 2):
                stage(s % 2, s, uses(s), done[s - 2])
            residual(B_MLP0)
            with pool.Fori(1, 12) as i:
                for s in range(2):
                    stage(s, W_IN + 2 * i + s, W_IN // 2 + i + 1, (wi_done, 4 * i + 2 * s - 2))
            for s in range(W_CONV, W_CONV + 2):
                stage(s % 2, s, uses(s), done[s - 2])
            def product_sums(o, first, last):
                for p in range(first, last + 1):
                    f, n = pair_tile(p)
                    c, m = f // 2, f % 2
                    re, im = (2 * m, 2 * m + 1) if c == 0 else (m, 2 + m)
                    pr_, pi_ = pz[:, c, re, half(n)], pz[:, c, im, half(n)]
                    pool.wait_ge(cf_free, 16 * o + p + 1)
                    nc.gpsimd.tensor_tensor(pr_, pr_, pt[p % 2][:, 0, :], ALU.subtract)
                    nc.gpsimd.tensor_tensor(pi_, pi_, pt[p % 2][:, 1, :], ALU.add).then_inc(pz_made, 1)

            SUMS_AFTER = {2: (1, 3), 3: (4, 5), 4: (6, 7), 5: (8, 9), 6: (10, 11), 7: (12, 13), 8: (14, 15)}

            def conv_step(o, s):
                read = (cf_done, 32 * o + STEP_END[s - 2]) if s < 9 else (ci_done, 32 * o + STEP_END[s - 9])
                if s == 2:
                    product_sums(o, 0, 0)
                stage(s % 2, W_CONV + 14 * o + s, W_CONV // 2 + 7 * o + s // 2 + 1, read)
                if s in SUMS_AFTER:
                    product_sums(o, *SUMS_AFTER[s])

            with pool.Fori(0, ORDERS - 1) as o:
                for s in range(2, 16):
                    conv_step(o, s)
            for s in range(2, 14):
                conv_step(ORDERS - 1, s)
            for s in range(W_OUT, W_OUT + 2):
                stage(s % 2, s, uses(s), done[s - 2])
            with pool.Fori(1, 4) as i:
                for s in range(2):
                    stage(s, W_OUT + 2 * i + s, W_OUT // 2 + i + 1, (ho_done, 4 * i + 2 * s - 2))
            mlp(1, W_MLP1)
            residual(B_MLP1)

        @blk.tensor
        def _(pe):
            def products(dst, terms, done):
                n = len(terms)
                for i, (wh, wl, rh, rl, ready) in enumerate(terms):
                    if ready:
                        pe.wait_ge(*ready)
                    nc.tensor.matmul(dst, wh, rh, start=(i == 0), stop=False)
                    nc.tensor.matmul(dst, wh, rl, start=False, stop=False)
                    last = nc.tensor.matmul(dst, wl, rh, start=False, stop=(i == n - 1))
                last.then_inc(done, 1)

            def w(slot, k):
                return whi[slot][:, k, :], wlo[slot][:, k, :]

            def mean_square(c, ssum, width, bank):
                pe.wait_ge(sum_made, c + 1)
                nc.tensor.matmul(ps[:, bank, 0:width], ones[:, :], ssum[:, 0:width], start=True, stop=True).then_inc(ms_made, 1)

            def norm_sums(i, sq, std):
                n = token_tiles(i)
                if i >= 2:
                    pe.wait_ge(nrec_made, i - 1)
                for k in range(KT):
                    pe.wait_ge(nsq_made, KT * i + k + 1)
                    last = nc.tensor.matmul(ps[:, 4 + i % 2, 0:n * P], ones[:, :], sq[:, k, 0:n * P], start=(k == 0), stop=(k == KT - 1))
                last.then_inc(nsum_made, 1)
                pe.wait_ge(nstd_made, i + 1)
                for q in range(n):
                    last = nc.tensor.transpose(ps[:, 4 + i % 2, q * P:(q + 1) * P], std[:, q * P:(q + 1) * P], idm[:, :])
                last.then_inc(std_turned, 1)

            def norm_turn(i, spread, *used):
                if used:
                    pe.wait_ge(*used)
                pe.wait_ge(spread_made, SPREAD_END[i])
                for q in range(token_tiles(i)):
                    last = nc.tensor.transpose(ps[:, 6 + i % 2, q * P:(q + 1) * P], spread[:, q, :], idm[:, :])
                last.then_inc(turned_made, 1)

            pe.wait_ge(const_in, 32)
            pe.wait_ge(ones_made, 1)
            for a in range(3):
                last = nc.tensor.transpose(ps[:, 0, a * P:(a + 1) * P], vrow[:, a, :], idm[:, :])
            last.then_inc(vec_t, 1)
            pe.wait_ge(filt_in, 64)
            for n in range(2):
                last = nc.tensor.matmul(ps[0:FH, 2 + n, :], fw12[0:EMB, 0, :], zp[0:EMB, half(n)], start=True, stop=True)
            last.then_inc(hd_done, 1)
            pe.wait_ge(hd_sin, 1)
            for n in range(2):
                last = nc.tensor.matmul(ps[0:FH, 2 + n, :], fw12[:, 1, :], hd1[:, half(n)], start=True, stop=True)
            last.then_inc(hd_done, 1)
            pe.wait_ge(hd_sin, 2)
            def modulation_sums(q):
                tiles = AQUART // P
                pe.wait_ge(ada_acc, KT * (q + 1))
                for m in range(tiles):
                    last = nc.tensor.matmul(ps[:, 3, q * tiles + m:q * tiles + m + 1], aacc[q % 2][:, m * P:(m + 1) * P], ones[:, 0:1], start=True, stop=True)
                for m in range(q * tiles, min((q + 1) * tiles, 2 * KT)):
                    last = nc.tensor.matmul(ps[:, 3, 48 + m:49 + m], aaccc[:, m * P:(m + 1) * P], ones[:, 0:1], start=True, stop=True)
                last.then_inc(ada_sum, 1)

            for o in range(ORDERS):
                pe.wait_ge(filt_w3_in, 16 * o + 16)
                for t in range(TT):
                    for j in range(4):
                        pe.wait_ge(hf_free, 32 * o + 4 * t + j + 1)
                        nc.tensor.matmul(ps[:, 4 + j, :], hd2[:, t * P:(t + 1) * P], fw3[:, half(j)], start=True, stop=True).then_inc(hf_done, 1)
                    if o == 0 and t % 2:
                        modulation_sums(t // 2)
                idx = 0
                for rnd, groups in ((0, s_groups), (1, d_groups)):
                    for r, (c, n) in enumerate(RING):
                        slot = r % 2
                        pe.wait_ge(fr_lo, 16 * o + 8 * rnd + r + 1)
                        if n == 0:
                            pe.wait_ge(w_staged, W_FILT + 8 * o + 4 * rnd + c + 1)
                        for tiles, rows, _, _ in groups(c):
                            pe.wait_ge(fs_free, FS_PER * o + max(idx + 1, 4))
                            products(ps[:, idx % 4, :],
                                     [(*w(c % 2, a), rg_hi[slot][:, b, :], rg_lo[slot][:, b, :], None) for a, b in zip(tiles, rows)], fs_done)
                            idx += 1
            pe.wait_ge(x_in, 32)
            for g in range(20):
                bank = g % 4
                if g == 0:
                    pe.wait_ge(fs_free, 4 + 2 * FS_PER)
                if g >= 4:
                    pe.wait_ge(xt_free, g - 3)
                for j in range(4):
                    if g < 16:
                        blk_in = xtm[:, 4 * (g % 2) + j, (g // 2) * P:(g // 2 + 1) * P]
                    else:
                        dt = 2 * (g - 16) + j // 2
                        blk_in = xctm[:, j % 2, dt * P:(dt + 1) * P]
                    last = nc.tensor.transpose(ps[:, bank, j * P:(j + 1) * P], blk_in, idm[:, :])
                last.then_inc(xt_done, 1)
            for n in range(2):
                norm_sums(N_LAT + n, asq, anstd)
                norm_turn(N_LAT + n, aspread)
            norm_sums(N_CTX, asq, anstd)
            norm_turn(N_CTX, aspread, pre_t, A_LAT + KT)
            g = 0
            for s in range(4):
                pe.wait_ge(w_staged, W_DOWN + s + 1)
                for n in range(3 if s >= 2 else 2):
                    if g >= 6:
                        pe.wait_ge(dn_free, g - 5)
                    width = HALF if n < 2 else C
                    rh, rl = (hh, hl) if n < 2 else (hch, hcl)
                    cols = half(n) if n < 2 else slice(0, C)
                    base = A_LAT + 8 * n if n < 2 else A_CTX
                    products(ps[:, g % 6, 0:width],
                             [(*w(s % 2, k), rh[:, k, cols], rl[:, k, cols], (pre_lo, base + k + 1)) for k in range(KT)], dn_done)
                    g += 1
                if s >= 2:
                    mean_square(N_CQ + s - 2, cssum, HALF, 6 + (s + 1) % 2)
            for c in range(3):
                pe.wait_ge(std_made, N_CKV + c - 1)
                mean_square(N_CKV + c, cssum, HALF if c < 2 else C, 6 + (c + 1) % 2)
            pe.wait_ge(tab_in, 32)
            for c in range(3):
                width = HALF if c < 2 else C
                pe.wait_ge(kr_made, c + 1)
                nc.tensor.matmul(ps[:, 3 + c, 0:width], rsm[:, :], krt[:, c * HALF:c * HALF + width], start=True, stop=True).then_inc(kr_done, 1)
            def project_piece(g, gg, j):
                if j == 0:
                    pe.wait_ge(w_staged, W_HEAD + g + 1)
                pe.wait_ge(pp_free, 10 * g + max(min(j, 7) + 1, 4))
                bank = PIECE_BANK[j]
                if j < 4:
                    hd, n = j // 2, j % 2
                    products(ps[:, bank, :], [(*w(gg, 2 * k + hd), cqh[:, k, half(n)], cql[:, k, half(n)], None) for k in range(2)], pp_done)
                elif j < 7:
                    n = j - 4
                    width = HALF if n < 2 else C
                    cols = slice(n * HALF, n * HALF + width)
                    products(ps[:, bank, 0:width], [(*w(gg, 4), ckvh[:, cols], ckvl[:, cols], None)], pp_done)
                else:
                    for q, t in enumerate(range(4 * (j - 7), min(10, 4 * (j - 7) + 4))):
                        dst = ps[:, bank, q * P:(q + 1) * P]
                        a, b = ckvh[:, t * P:(t + 1) * P], ckvl[:, t * P:(t + 1) * P]
                        vw_h, vw_l = w(gg, 5)
                        nc.tensor.matmul(dst, a, vw_h, start=True, stop=False)
                        nc.tensor.matmul(dst, a, vw_l, start=False, stop=False)
                        last = nc.tensor.matmul(dst, b, vw_h, start=False, stop=True)
                    last.then_inc(pp_done, 1)

            def scores(u, j, cuts):
                hd, q = u // 4, 2 * (u % 4) + j
                qs = slice(q * P, (q + 1) * P)
                for a, b in cuts:
                    dst = psf[:, j * KEYS + a:j * KEYS + b]
                    nc.tensor.matmul(dst, qh[:, hd, qs], kh[:, hd, a:b], start=True, stop=False)
                    nc.tensor.matmul(dst, qh[:, hd, qs], kl[:, hd, a:b], start=False, stop=False)
                    last = nc.tensor.matmul(dst, ql[:, hd, qs], kh[:, hd, a:b], start=False, stop=True)
                return last

            def scores_first(g, u):
                if u >= 1:
                    pe.wait_ge(p_made, 16 * g + 2 * u - 1)
                scores(u, 0, ((0, 512), (512, 1024)))

            def scores_first_end(g, u):
                if u >= 1:
                    pe.wait_ge(p_made, 16 * g + 2 * u)
                scores(u, 0, ((1024, 1280),)).then_inc(s_done, 1)

            def scores_shared(g, u):
                pe.wait_ge(p_made, 16 * g + 2 * u + 1)
                scores(u, 1, ((0, 256),)).then_inc(s_done, 1)

            def turn(g, u, jj):
                if jj == 0:
                    pe.wait_ge(p_made, 16 * g + 2 * u + 2)
                if 5 * u + jj >= 2:
                    pe.wait_ge(t_free, 40 * g + 5 * u + jj - 1)
                for k in range(2):
                    for j in range(2):
                        last = nc.tensor.transpose(ps[:, 5 + (5 * u + jj) % 2, k * 256 + j * P:k * 256 + (j + 1) * P],
                                                   pr[:, u % 2, j, (2 * jj + k) * P:(2 * jj + k + 1) * P], idm[:, :])
                last.then_inc(t_done, 1)

            def weigh(g, u, jj):
                pe.wait_ge(t_free, 40 * g + 5 * u + jj + 1)
                if jj == 0 and u >= 1:
                    pe.wait_ge(o_made, 8 * g + u)
                if jj == 4:
                    pe.wait_ge(rb_made, 16 * g + 2 * u + 2)
                slot = (5 * u + jj) % 4
                for k in range(2):
                    t = 2 * jj + k
                    a, b = vh[:, t, u // 4, :], vl[:, t, u // 4, :]
                    nc.tensor.matmul(ps[0:VD, 7, 0:256], a, pth[slot][:, k, :], start=(t == 0), stop=False)
                    nc.tensor.matmul(ps[0:VD, 7, 0:256], a, ptl[slot][:, k, :], start=False, stop=False)
                    last = nc.tensor.matmul(ps[0:VD, 7, 0:256], b, pth[slot][:, k, :], start=False, stop=(t == 9))
                last.then_inc(pv_done, 1)
                if jj == 4:
                    for j in range(2):
                        last = nc.tensor.transpose(ps[0:VD, 7, 256 + j * P:256 + (j + 1) * P], rb[:, j, :], idm[:, :])
                    last.then_inc(rt_done, 1)

            def group(g, gg, more):
                pe.wait_ge(pp_free, 4 + 10 * g + 7)
                scores_first(g, 0)
                scores_first_end(g, 0)
                pe.wait_ge(pp_free, 4 + 10 * g + 8)
                scores(0, 1, ((256, 768), (768, 1280)))
                scores_shared(g, 0)
                pe.wait_ge(pp_free, 4 + 10 * g + 10)
                scores_first(g, 1)
                for u in range(7):
                    scores_first_end(g, u + 1)
                    turn(g, u, 0)
                    turn(g, u, 1)
                    scores(u + 1, 1, ((256, 768), (768, 1280)))
                    weigh(g, u, 0)
                    turn(g, u, 2)
                    weigh(g, u, 1)
                    scores_shared(g, u + 1)
                    turn(g, u, 3)
                    weigh(g, u, 2)
                    turn(g, u, 4)
                    if u < 6:
                        scores_first(g, u + 2)
                    weigh(g, u, 3)
                    weigh(g, u, 4)
                turn(g, 7, 0)
                turn(g, 7, 1)
                if not more:
                    for jj in range(3):
                        weigh(g, 7, jj)
                        turn(g, 7, jj + 2)
                    weigh(g, 7, 3)
                    weigh(g, 7, 4)
                    return
                project_piece(g + 1, 1 - gg, 0)
                project_piece(g + 1, 1 - gg, 1)
                for jj in range(3):
                    weigh(g, 7, jj)
                    turn(g, 7, jj + 2)
                    project_piece(g + 1, 1 - gg, 2 + jj)
                weigh(g, 7, 3)
                project_piece(g + 1, 1 - gg, 5)
                weigh(g, 7, 4)
                for j in range(6, 10):
                    project_piece(g + 1, 1 - gg, j)

            pe.wait_ge(cn_lo, 3)
            pe.wait_ge(kr_lo, 6)
            for j in range(10):
                project_piece(0, 0, j)
            with pe.Fori(0, HEADS // 4 - 1) as i:
                group(2 * i, 0, True)
                group(2 * i + 1, 1, True)
            group(HEADS // 2 - 2, 0, True)
            group(HEADS // 2 - 1, 1, False)

            def project(base, rows_hi, rows_lo, done, free, first):
                with pe.Fori(0, 4) as i:
                    for s in range(2):
                        pe.wait_ge(w_staged, base + 2 * i + s + 1)
                        for n in range(2):
                            pe.wait_ge(free, 4 * i + 2 * s + n + 1)
                            products(ps[:, 2 * s + n, :],
                                     [(*w(s, k), rows_hi[:, k, half(n)], rows_lo[:, k, half(n)], first(k, n) if s == 0 else None) for k in range(KT)], done)

            def norms(post, pre, applied):
                for n in range(2):
                    norm_sums(post + n, msq, mnstd)
                    norm_turn(post + n, mspread)
                if pre is None:
                    return
                for n in range(2):
                    norm_sums(pre + n, msq, mnstd)
                    norm_turn(pre + n, mspread, post_y, applied + KT * (n + 1))

            def mlp(l, pre):
                with pe.Fori(0, NCHUNK) as j:
                    if l == 0:
                        pe.wait_ge(ada1_mod, j + 1)
                    for s in range(4):
                        pe.wait_ge(w_staged, (W_MLP0, W_MLP1)[l] + 8 * j + s + 1)
                        for n in range(2):
                            pe.wait_ge(hid_free[l], 8 * j + 2 * s + n + 1)
                            products(ps[:, (2 * s + n) % 4, :],
                                     [(*w(s % 2, k), hh[:, k, half(n)], hl[:, k, half(n)], (pre_lo, pre + 8 * n + k + 1) if s == 0 else None)
                                      for k in range(KT)], hid_done[l])
                    for s in range(4):
                        if l == 0 and s == 3:
                            pe.wait_ge(ada1_acc, 1 + KT * ABLOCKS * (j + 1))
                            for b in range(ABLOCKS):
                                for m in range(ACOLS // P):
                                    col = b * (ACOLS // P) + m
                                    last = nc.tensor.matmul(ps[:, 0, col:col + 1], bacc[:, b, m * P:(m + 1) * P], ones[:, 0:1], start=True, stop=True)
                            last.then_inc(ada1_sum, 1)
                        pe.wait_ge(w_staged, (W_MLP0, W_MLP1)[l] + 8 * j + 4 + s + 1)
                        for n in range(2):
                            for m in range(2):
                                pe.wait_ge(acc_free[l], 16 * j + 4 * s + 2 * n + m + 1)
                                products(ps[:, 4 + 2 * n + m, :],
                                         [(*w(s % 2, 2 * k + m), hidh[:, k, half(n)], hidl[:, k, half(n)],
                                           (hid_lo[l], 8 * j + 2 * k + n + 1) if s == 0 and m == 0 else None) for k in range(HIDT)], acc_done[l])

            project(W_O, hh, hl, wo_done, wo_free, lambda k, n: (ol_made, k + 1))
            norms(N_POST1, N_PRE2, B_ATT)
            mlp(0, A_MLP0)
            norms(N_POST2, N_PREH, B_MLP0)
            def project_u(i, s, first):
                pe.wait_ge(w_staged, W_IN + 2 * i + s + 1)
                for n in range(2):
                    pe.wait_ge(wi_free, 4 * i + 2 * s + n + 1)
                    products(ps[:, 2 * (s % 2) + n, :],
                             [(*w(s % 2, k), hh[:, k, half(n)], hl[:, k, half(n)], (pre_lo, A_HY + 8 * n + k + 1) if first else None) for k in range(KT)], wi_done)

            def turn_u(i, s):
                pe.wait_ge(uc_made, 2 * i + s + 1)
                for n in range(2):
                    pe.wait_ge(ut_made, 4 * i + 2 * s + n + 1)
                    for q in range(4):
                        last = nc.tensor.transpose(ps[:, 4 + 2 * s + n, q * P:(q + 1) * P], uc[s][:, (4 * n + q) * P:(4 * n + q + 1) * P], idm[:, :])
                    last.then_inc(ut_done, 1)

            project_u(0, 0, True)
            with pe.Fori(0, 11) as i:
                project_u(i, 1, False)
                turn_u(i, 0)
                project_u(i, 2, False)
                turn_u(i, 1)
            project_u(11, 1, False)
            turn_u(11, 0)
            turn_u(11, 1)
            with pe.Fori(0, ORDERS) as o:
                for s in range(7):
                    pe.wait_ge(w_staged, W_CONV + 14 * o + s + 1)
                    cls = (s + 1) // 2
                    for n, tiles, rows, idx in transform_groups(s, False):
                        pe.wait_ge(cr_lo, 16 * o + 2 * cls + n + 1)
                        if cls == 1:
                            pe.wait_ge(cf_free, 16 * o + idx % 8 // 2 + 1)
                        elif cls > 1:
                            pe.wait_ge(cf_free, 16 * o + 4 * (cls - 1) + idx % 4 + 1)
                        products(ps[:, idx % 8, :], [(*w(s % 2, a), rg_hi[n][:, b, :], rg_lo[n][:, b, :], None) for a, b in zip(tiles, rows)], cf_done)
                pe.wait_ge(cf_free, 16 * o + 16)
                for s in range(7):
                    pe.wait_ge(w_staged, W_CONV + 14 * o + 7 + s + 1)
                    cls = (s + 1) // 2
                    for n, tiles, rows, idx in transform_groups(s, True):
                        pe.wait_ge(cr_lo, 16 * o + 8 + 2 * cls + n + 1)
                        pe.wait_ge(ci_free, 32 * o + idx + 1)
                        products(ps[:, idx % 8, :], [(*w((7 + s) % 2, a), rg_hi[n][:, b, :], rg_lo[n][:, b, :], None) for a, b in zip(tiles, rows)], ci_done)
            for g in range(16):
                pe.wait_ge(z_made, 2)
                if g == 0:
                    pe.wait_ge(ci_free, 8 + 32 * ORDERS)
                if g >= 4:
                    pe.wait_ge(z_lo, g - 3)
                for j in range(4):
                    tt = 4 * (g % 2) + j
                    last = nc.tensor.transpose(ps[:, g % 4, j * P:(j + 1) * P], src[:, tt // 2, tt % 2, (g // 2) * P:(g // 2 + 1) * P], idm[:, :])
                last.then_inc(zt_done, 1)
            project(W_OUT, zh, zl, ho_done, ho_free, lambda k, n: (z_lo, 2 * k + n + 1))
            norms(N_POSTH, N_PREM, B_HY)
            mlp(1, A_MLP1)
            norms(N_POSTM, None, B_MLP1)
            for g in range(16):
                if g < 2:
                    pe.wait_ge(post_x, B_MLP1 // 2 + 8)
                    pe.wait_ge(post_xp, B_MLP1 // 2 + 8)
                if g >= 4:
                    pe.wait_ge(out_made, g - 3)
                for j in range(4):
                    last = nc.tensor.transpose(ps[:, g % 4, j * P:(j + 1) * P], xm[:, 4 * (g % 2) + j, (g // 2) * P:(g // 2 + 1) * P], idm[:, :])
                last.then_inc(out_done, 1)

        @blk.scalar
        def _(act):
            def square(c, sq, source, ready):
                if ready:
                    act.wait_ge(*ready)
                if c:
                    act.wait_ge(sum_made, c)
                nc.scalar.activation(sq, source, ACT.Square).then_inc(sq_made, 1)

            def root(c, std, bank, width, count):
                act.wait_ge(ms_made, c + 1)
                if c:
                    act.wait_ge(rstd_made, c)
                nc.scalar.activation(std[:, 0:width], ps[:, bank, 0:width], ACT.Sqrt, bias=eps[:, 0:1], scale=1.0 / count).then_inc(std_made, 1)

            def square_tile(i, k, sq, source, ready):
                if ready:
                    act.wait_ge(*ready)
                if i and k == 0:
                    act.wait_ge(nsum_made, i)
                nc.scalar.activation(sq[:, k, 0:token_tiles(i) * P], source, ACT.Square).then_inc(nsq_made, 1)

            def norm_root(i, std):
                width = token_tiles(i) * P
                act.wait_ge(nsum_made, i + 1)
                if i:
                    act.wait_ge(std_turned, i)
                nc.scalar.activation(std[:, 0:width], ps[:, 4 + i % 2, 0:width], ACT.Sqrt, bias=eps[:, 0:1], scale=1.0 / D).then_inc(nstd_made, 1)

            def pre_high(it, dst, tmp, shift):
                act.wait_ge(pre_t, it + 1)
                nc.scalar.activation(dst, tmp, ACT.Identity, bias=shift).then_inc(pre_hi, 1)

            act.wait_ge(vec_made, 1)
            nc.scalar.activation(sile[:, :], vec[:, V_C:V_C + 16], ACT.Exp, scale=-1.0).then_inc(sil_exp, 1)
            for l in range(2):
                act.wait_ge(hd_arg, l + 1)
                nc.scalar.activation((hd1, hd2)[l][:, :], hda[:, :], ACT.Sin).then_inc(hd_sin, 1)
            act.sem_inc(fs_free, 4)
            for o in range(ORDERS):
                sent = [0] * 4

                def high(r):
                    act.wait_ge(fr_val, 16 * o + r + 1)
                    if r >= 2:
                        act.wait_ge(fs_done, FS_PER * o + RING_END[r - 2])
                    nc.scalar.activation(rg_hi[r % 2][:, :, :], val[r % 2][:, :, :], ACT.Copy).then_inc(fr_hi, 1)

                high(0)
                high(1)
                idx = 0
                for r in range(16):
                    c, n = RING[r % 8]
                    for _, _, f, plane in (s_groups if r < 8 else d_groups)(c):
                        q = idx % 4
                        act.wait_ge(fs_done, FS_PER * o + idx + 1)
                        if sent[q]:
                            act.wait_ge(ko_out[q], 16 * (KO_USES[q] * o + sent[q]))
                        if (f, plane) == (0, 1):
                            inst = nc.scalar.activation(ko[q][:, :], ps[:, q, :], ACT.Copy, scale=notop[:, 0:1])
                        else:
                            inst = nc.scalar.activation(ko[q][:, :], ps[:, q, :], ACT.Copy)
                        inst.then_inc(fs_free, 1)
                        act.wait_ge(fs_free, 4 + FS_PER * o + idx + 1)
                        if plane == 2:
                            act.wait_ge(ko_out[before], 16 * (KO_USES[before] * o + sent[before]))
                            act.dma_start(spec[bass.ds(((8 * o + f) * 3 + 2) * P, 1), half(n)], ko[q][0:1, :]).then_inc(ko_out[q], 16)
                            sent[q] += 1
                        else:
                            for pl in ((0, 2) if (f, plane) == (0, 0) else (plane,)):
                                act.dma_start(spec[bass.ds(((8 * o + f) * 3 + pl) * P, P), half(n)], ko[q][:, :]).then_inc(ko_out[q], 16)
                                sent[q] += 1
                        before = q
                        idx += 1
                    if r + 2 < 16:
                        high(r + 2)
                assert sent == KO_USES
                for q in range(4):
                    act.wait_ge(ko_out[q], 16 * (KO_USES[q] * o + KO_USES[q]))
            def first_squares(i):
                for k in range(KT):
                    if i == N_CTX:
                        square_tile(i, k, asq, xc[:, k, :], (xt_free, 20))
                    else:
                        square_tile(i, k, asq, xa[:, k, half(i - N_LAT)], (xt_free, 15 + i - N_LAT))

            def first_high(i, tiles):
                for k in tiles:
                    if i == N_CTX:
                        pre_high(A_CTX + k, hch[:, k, :], atmp[(A_CTX + k) % 2][:, 0:C], mod[:, 48 + k:49 + k])
                    else:
                        pre_high(A_LAT + 8 * i + k, hh[:, k, half(i - N_LAT)], atmp[k % 2][:, :], mod[:, k:k + 1])

            first_squares(N_LAT)
            norm_root(N_LAT, anstd)
            for i in (N_LAT + 1, N_CTX):
                first_squares(i)
                first_high(i - 1, range(4))
                norm_root(i, anstd)
                first_high(i - 1, range(4, KT))
            first_high(N_CTX, range(KT))
            for n in range(2):
                square(N_CQ + n, csq[:, :, :], cq[:, :, half(n)], (dn_free, 4))
                root(N_CQ + n, cstd, 6 + (n + 1) % 2, HALF, QR)
            for n in range(3):
                width = HALF if n < 2 else C
                cols = slice(n * HALF, n * HALF + width)
                square(N_CKV + n, csq[:, 0, 0:width], ckv[:, cols], (dn_free, 7))
                root(N_CKV + n, cstd, 6 + (n + 1) % 2, width, KVR)
            for k in range(2):
                act.wait_ge(cn_val, k + 1)
                nc.scalar.activation(cqh[:, k, :], cq[:, k, :], ACT.Copy).then_inc(cn_hi, 1)
            act.wait_ge(cn_val, 3)
            nc.scalar.activation(ckvh[:, :], ckv[:, :], ACT.Copy).then_inc(cn_hi, 1)
            for c in range(3):
                width = HALF if c < 2 else C
                cols = slice(c * HALF, c * HALF + width)
                act.wait_ge(kr_done, c + 1)
                for hd in range(2):
                    nc.scalar.activation(kh[NOPE:P, hd, cols], ps[NOPE:P, 3 + c, 0:width], ACT.Copy).then_inc(kr_hi, 1)
            def piece_high(g, j):
                bank = PIECE_BANK[j]
                if j < 4:
                    act.wait_ge(q_val, 4 * g + j + 1)
                    nc.scalar.activation(qh[:, j // 2, half(j % 2)], qf[j % 2][:, :], ACT.Copy).then_inc(pp_hi, 1)
                    return
                act.wait_ge(pp_done, 10 * g + j + 1)
                if j < 7:
                    width = HALF if j < 6 else C
                    cols = slice((j - 4) * HALF, (j - 4) * HALF + width)
                    for hd in range(2):
                        nc.scalar.activation(kh[0:NOPE, hd, cols], ps[NOPE * hd:NOPE * hd + NOPE, bank, 0:width], ACT.Copy).then_inc(pp_hi, 1)
                else:
                    t0 = 4 * (j - 7)
                    nt = min(10, t0 + 4) - t0
                    nc.scalar.activation(vh[:, t0:t0 + nt, :, :].rearrange("p t h v -> p (t h) v"),
                                         ps[:, bank, 0:nt * P].rearrange("p (g v) -> p g v", v=VD), ACT.Copy).then_inc(pp_hi, 1)

            def weights_of(g, u, j):
                act.wait_ge(max_made, 16 * g + 2 * u + j + 1)
                if u >= 2:
                    act.wait_ge(t_done, 40 * g + 5 * (u - 1))
                a = 2 * (u % 2) + j
                nc.scalar.activation(pr[:, u % 2, j, :], psf[:, j * KEYS:(j + 1) * KEYS], ACT.Exp, bias=mx[:, a:a + 1], scale=SCALE, accum_out=sm[:, a:a + 1]).then_inc(p_made, 1)

            def turned_high(g, u, jj):
                idx = 5 * u + jj
                act.wait_ge(t_done, 40 * g + idx + 1)
                if idx >= 4:
                    act.wait_ge(pv_done, 40 * g + idx - 3)
                nc.scalar.activation(pth[idx % 4][:, :, :], ps[:, 5 + idx % 2, :].rearrange("p (k q) -> p k q", k=2), ACT.Copy).then_inc(t_hi, 1)

            def inverse_sums(g, u):
                act.wait_ge(rt_done, 8 * g + u + 1)
                if u >= 1:
                    act.wait_ge(o_made, 8 * g + u)
                nc.scalar.activation(rc[:, :], ps[0:VD, 7, 256:512], ACT.Copy).then_inc(rc_made, 1)

            def group(g, more):
                weights_of(g, 0, 0)
                weights_of(g, 0, 1)
                for u in range(7):
                    turned_high(g, u, 0)
                    turned_high(g, u, 1)
                    weights_of(g, u + 1, 0)
                    turned_high(g, u, 2)
                    turned_high(g, u, 3)
                    turned_high(g, u, 4)
                    weights_of(g, u + 1, 1)
                    inverse_sums(g, u)
                turned_high(g, 7, 0)
                turned_high(g, 7, 1)
                if more:
                    piece_high(g + 1, 0)
                    piece_high(g + 1, 1)
                for jj in range(2, 5):
                    turned_high(g, 7, jj)
                    if more:
                        piece_high(g + 1, jj)
                if more:
                    piece_high(g + 1, 5)
                inverse_sums(g, 7)
                if more:
                    piece_high(g + 1, 6)
                    act.wait_ge(pv_done, 40 * g + 40)
                    for j in range(7, 10):
                        piece_high(g + 1, j)

            for j in range(10):
                piece_high(0, j)
            with act.Fori(0, HEADS // 4 - 1) as i:
                group(2 * i, True)
                group(2 * i + 1, True)
            group(HEADS // 2 - 2, True)
            group(HEADS // 2 - 1, False)
            act.wait_ge(o_made, 64)
            for k in range(KT):
                nc.scalar.activation(hh[:, k, :], ao[:, k, :], ACT.Copy).then_inc(oh_made, 1)

            def post_then_pre(post, pre, items, shift, ready):
                for n in range(2):
                    for k in range(KT):
                        square_tile(post + n, k, msq, y[:, k, half(n)], ready)
                    norm_root(post + n, mnstd)
                if pre is None:
                    return
                added = {N_PRE2: B_ATT, N_PREH: B_MLP0, N_PREM: B_HY}[pre]

                def high(n, tiles):
                    for k in tiles:
                        it = items + 8 * n + k
                        pre_high(it, hh[:, k, half(n)], mtmp[it % 2][:, :], mod[:, shift + k:shift + k + 1])

                for n in range(2):
                    for k in range(KT):
                        square_tile(pre + n, k, msq, xm[:, k, half(n)], ((post_x, post_xp)[k % 2], added // 2 + 4 * n + k // 2 + 1))
                    if n:
                        high(0, range(4))
                    norm_root(pre + n, mnstd)
                high(0, range(4, KT))
                high(1, range(KT))

            def mlp(l):
                with act.Fori(0, NCHUNK) as j:
                    for g in range(8):
                        act.wait_ge(hid_free[l], 4 + 8 * j + g + 1)
                        if g >= 2:
                            act.wait_ge(hid_lo[l], 8 * j + g - 1)
                        nc.scalar.activation(ms2[g % 2][:, :], mr[g % 2][:, :], ACT.Square).then_inc(hid_sq[l], 1)
                        act.wait_ge(hid_sq[l], 8 * j + g + 1)
                        nc.scalar.activation(hidh[:, g // 2, half(g % 2)], ms2[g % 2][:, :], ACT.Copy).then_inc(hid_hi[l], 1)
                    act.wait_ge(acc_done[l], 16 * j + 16)

            post_then_pre(N_POST1, N_PRE2, A_MLP0, 24, (wo_free, 4 + 16))
            mlp(0)
            post_then_pre(N_POST2, N_PREH, A_HY, 64, (acc_free[0], 4 + 16 * NCHUNK))

            def send_u(i, s):
                act.wait_ge(ut_made, 4 + 4 * i + 2 * s + 2)
                act.dma_start(u_tm[bass.ds(2 * i + s, 1)].rearrange("m (a p) c -> (m p) a c", p=P), ut[s][:, :, :]).then_inc(ut_out[s], 16)

            def middle(i, s, first):
                act.wait_ge(wi_free, 4 + 4 * i + 2 * s + 2)
                if not first:
                    act.wait_ge(ut_done, 4 * i + 2 * s - 2)
                nc.scalar.activation(uc[s][:, :], ub[s][:, 1:T + 1], ACT.Identity, bias=vec[:, bass.ds(V_BSH + 2 * i + s, 1)],
                                     scale=vec[:, bass.ds(V_WSH + 24 + 2 * i + s, 1)]).then_inc(uc_mid, 1)

            middle(0, 0, True)
            middle(0, 1, True)
            send_u(0, 0)
            with act.Fori(1, 12) as i:
                middle(i, 0, False)
                send_u(i - 1, 1)
                middle(i, 1, False)
                send_u(i, 0)
            send_u(11, 1)
            with act.Fori(0, ORDERS) as o:
                def high(r, *read):
                    act.wait_ge(cr_val, 8 * o + r + 1)
                    if read:
                        act.wait_ge(*read)
                    nc.scalar.activation(rg_hi[r % 2][:, :, :], val[r % 2][:, :, :], ACT.Copy).then_inc(cr_hi, 1)

                for r, (c, n) in enumerate(RING):
                    high(r, *((cf_done, 32 * o + ring_read(c - 1, n)) if c else ()))

                def high_inverse(c, n):
                    if c == 0:
                        act.wait_ge(cf_done, 32 * o + ring_read(3, n))
                    else:
                        act.wait_ge(ci_done, 32 * o + ring_read(c - 1, n))
                    act.wait_ge(pz_made, 16 * o + 4 * c + 2 * n + 2)
                    nc.scalar.activation(rg_hi[n][:, :, :], pz[:, c, :, half(n)], ACT.Copy).then_inc(cr_hi, 1)

                high_inverse(0, 0)
                high_inverse(0, 1)
                for c in range(1, 4):
                    for n in range(2):
                        high_inverse(c, n)
            for g in range(16):
                act.wait_ge(zt_done, g + 1)
                nc.scalar.activation(zh[:, g // 2, half(g % 2)], ps[:, g % 4, :], ACT.Copy).then_inc(z_hi, 1)
            post_then_pre(N_POSTH, N_PREM, A_MLP1, 64 + 24, (ho_free, 4 + 16))
            mlp(1)
            post_then_pre(N_POSTM, None, None, None, (acc_free[1], 4 + 16 * NCHUNK))

        @blk.vector
        def _(dve):
            dv = Chain(dve, dve_chain)
            tt, ts, stt = nc.vector.tensor_tensor, nc.vector.tensor_scalar, nc.vector.scalar_tensor_tensor

            def feature_sums(c, sq, ssum, width):
                dve.wait_ge(sq_made, c + 1)
                if c:
                    dve.wait_ge(ms_made, c)
                nc.vector.tensor_reduce(ssum[:, 0:width], sq.rearrange("p k t -> p t k"), AXX, ALU.add).then_inc(sum_made, 1)

            def inverse_root(c, std, rstd, width):
                dve.wait_ge(std_made, c + 1)
                nc.vector.reciprocal(rstd, std[:, 0:width]).then_inc(rstd_made, 1)
                dve.wait_ge(rstd_made, c + 1)

            def norm_inverse(i, spread):
                n = token_tiles(i)
                dve.wait_ge(std_turned, i + 1)
                if i >= 2:
                    dve.wait_ge(spread_made, SPREAD_END[i - 2])
                nc.vector.reciprocal(nrec[i % 2][:, 0:n], ps[:, 4 + i % 2, :].rearrange("p (q t) -> p q t", t=P)[:, 0:n, 0]).then_inc(nrec_made, 1)
                dve.wait_ge(nrec_made, i + 1)
                if i:
                    dve.wait_ge(turned_made, i)
                for q in range(n):
                    ts(spread[:, q, :], ones[:, :], nrec[i % 2][:, q:q + 1], None, ALU.mult).then_inc(spread_made, 1)

            def pre_apply(items, src_of, tmp_of, hi_of, lo_of, factor, rstd, shift, between=None):
                def low(it, k):
                    dve.wait_ge(pre_hi, it + 1)
                    stt(lo_of(k), tmp_of(it), shift(k), hi_of(k), ALU.add, ALU.subtract).then_inc(pre_lo, 1)

                for k in range(KT):
                    it = items + k
                    if it >= 2:
                        dve.wait_ge(pre_lo, it - 1)
                    stt(tmp_of(it), src_of(k), factor(k), rstd, ALU.mult, ALU.mult).then_inc(pre_t, 1)
                    if k:
                        low(it - 1, k - 1)
                    if k == 4 and between:
                        between()
                low(items + KT - 1, KT - 1)

            nc.vector.memset(ones[:, :], 1.0).then_inc(ones_made, 1)
            dv.did(nc.vector.memset(eps[:, :], EPS))
            dv.did(nc.vector.memset(notop[:, :], 1.0))
            dv.wait()
            dv.did(nc.vector.memset(notop[0:1, :], 0.0))
            dve.wait_ge(vec_t, 1)
            nc.vector.tensor_copy(vec[:, :], ps[:, 0, 0:NVEC]).then_inc(vec_made, 1)
            dve.wait_ge(vec_made, 1)
            dve.wait_ge(sil_exp, 1)
            dv.did(ts(sile[:, :], sile[:, :], 1.0, None, ALU.add))
            dv.wait()
            dv.did(nc.vector.reciprocal(sile[:, :], sile[:, :]))
            dv.wait()
            dv.did(tt(sil[:, :], sile[:, :], vec[:, V_C:V_C + 16], ALU.mult))
            dv.wait()
            MAGIC = 12582912.0
            C1 = 6.28125
            C2 = float(np.float32(2 * math.pi - C1))
            C3 = 2 * math.pi - C1 - C2
            PI = float(np.nextafter(np.float32(math.pi), np.float32(0)))
            for l in range(2):
                dve.wait_ge(hd_done, l + 1)
                if l:
                    dve.wait_ge(hd_sin, 1)
                dv.did(ts(hda[:, :], ps[0:FH, 2:4, :].rearrange("p b n -> p (b n)"), vec[0:FH, V_FB1 + l:V_FB1 + l + 1], vec[0:FH, V_FREQ:V_FREQ + 1], ALU.add, ALU.mult))
                dv.wait()
                dv.did(ts(hdn[:, :], hda[:, :], 1 / (2 * math.pi), MAGIC, ALU.mult, ALU.add))
                dv.wait()
                dv.did(ts(hdn[:, :], hdn[:, :], MAGIC, None, ALU.subtract))
                for part in (C1, C2, C3):
                    dv.wait()
                    dv.did(stt(hda[:, :], hdn[:, :], -part, hda[:, :], ALU.mult, ALU.add))
                dv.wait()
                ts(hda[:, :], hda[:, :], PI, -PI, ALU.min, ALU.max).then_inc(hd_arg, 1)
            def factors(l):
                m, g = 64 * l, V_NORMG + 32 * l
                for j, col in ((0, 8), (2, 32)):
                    dv.did(stt(fac[:, 32 * l + 8 * j:32 * l + 8 * j + 8], mod[:, m + col:m + col + 8], 1.0, vec[:, g + 8 * j:g + 8 * j + 8], ALU.add, ALU.mult))
                for j, col in ((1, 16), (3, 40)):
                    dv.did(tt(fac[:, 32 * l + 8 * j:32 * l + 8 * j + 8], mod[:, m + col:m + col + 8], vec[:, g + 8 * j:g + 8 * j + 8], ALU.mult))
                if l == 0:
                    dv.did(stt(fac[:, 64:72], mod[:, 56:64], 1.0, vec[:, g:g + 8], ALU.add, ALU.mult))
                dv.wait()

            def modulation_part(n):
                q, k = n // KT, n % KT
                weights, acc = araw[n % 5], aacc[q % 2]
                own = min((q + 1) * AQUART, 2 * D) - q * AQUART
                if n == 0:
                    dve.wait_ge(hd_sin, 2)
                dve.wait_ge(ada_in[n % 5], 16 * (n // 5 + 1))
                if k == 0 and q >= 2:
                    dve.wait_ge(ada_sum, q - 1)
                if own > 0:
                    acc_c = aaccc[:, q * AQUART:q * AQUART + own]
                    if k == 0:
                        dv.did(ts(acc_c, weights[:, 0:own], sil[:, 8:9], None, ALU.mult))
                    else:
                        dv.wait()
                        dv.did(stt(acc_c, weights[:, 0:own], sil[:, 8 + k:9 + k], acc_c, ALU.mult, ALU.add))
                if k == 0:
                    ts(acc[:, :], weights[:, :], sil[:, 0:1], None, ALU.mult).then_inc(ada_acc, 1)
                else:
                    dve.wait_ge(ada_acc, n)
                    stt(acc[:, :], weights[:, :], sil[:, k:k + 1], acc[:, :], ALU.mult, ALU.add).then_inc(ada_acc, 1)

            def modulation_vectors():
                dve.wait_ge(ada_sum, 4)
                dv.did(tt(mod[:, 0:48], ps[:, 3, 0:48], vec[:, V_ADAB:V_ADAB + 48], ALU.add))
                dv.did(tt(mod[:, 48:64], ps[:, 3, 48:64], vec[:, V_ADAB:V_ADAB + 16], ALU.add))
                dv.wait()
                factors(0)

            dve.sem_inc(hf_free, 4)

            def operand(c, n, x4, v, made):
                q, s, x0, x2 = bq[:, :, half(n)], bs[:, :, half(n)], x4[:, 0, :, half(n)], x4[:, 2, :, half(n)]
                re, im = v[:, 0:2, :], v[:, 2:4, :]
                if c == 0:
                    dv.did(tt(re, x0, x2, ALU.add))
                    dv.wait()
                    dv.did(tt(im, re, q, ALU.subtract))
                    dv.wait()
                    tt(re, re, q, ALU.add).then_inc(made, 1)
                elif c == 2:
                    dv.did(tt(re, x0, x2, ALU.subtract))
                    nc.vector.tensor_copy(im, s).then_inc(made, 1)
                else:
                    r4 = R4 if c == 1 else -R4
                    dv.did(stt(re, s, r4, x0, ALU.mult, ALU.add))
                    stt(im, q, R4, x2, ALU.mult, ALU.add if c == 1 else ALU.subtract).then_inc(made, 1)

            def butterflies(x4, chans):
                dv.did(tt(bq[:, :, chans], x4[:, 1, :, chans], x4[:, 3, :, chans], ALU.add))
                dv.did(tt(bs[:, :, chans], x4[:, 1, :, chans], x4[:, 3, :, chans], ALU.subtract))
                dv.wait()

            for o in range(ORDERS):
                for t in range(TT):
                    if o == 0:
                        for n in range(4 * t, 4 * t + 4):
                            modulation_part(n)
                    taps = fb[t % 2]
                    dve.wait_ge(dec_in[t % 2], 16 * (4 * o + t // 2 + 1))
                    if t >= 2:
                        dve.wait_ge(fd_made, 8 * o + t - 1)
                    for j in range(4):
                        dve.wait_ge(hf_done, 32 * o + 4 * t + j + 1)
                        tt(taps[:, j // 2, half(j % 2)], ps[:, 4 + j, :], dec[t % 2][:, half(j % 2)], ALU.mult).then_inc(hf_free, 1)
                    dve.wait_ge(hf_free, 4 + 32 * o + 4 * t + 4)
                    if t == 0:
                        dv.did(nc.vector.memset(taps[0:1, 1, :], 0.0))
                        dv.did(tt(taps[0:1, 0, :], taps[0:1, 0, :], fbias[0:1, bass.ds(o * D, D)], ALU.add))
                        dv.wait()
                    tt(f_s[:, t // 2, t % 2, :], taps[:, 0, :], taps[:, 1, :], ALU.add).then_inc(fb_made, 1)
                dve.wait_ge(fb_made, 8 * o + 8)

                def filter_operand(r):
                    x4 = (f_s, f_d)[r // 8]
                    if r % 8 < 2:
                        dve.wait_ge(fr_val, 16 * o + r)
                        butterflies(x4, half(r % 2))
                    operand(*RING[r % 8], x4, val[r % 2], fr_val)

                def low(r):
                    dve.wait_ge(fr_hi, 16 * o + r + 1)
                    tt(rg_lo[r % 2][:, :, :], val[r % 2][:, :, :], rg_hi[r % 2][:, :, :], ALU.subtract).then_inc(fr_lo, 1)

                butterflies(f_s, half(0))
                operand(*RING[0], f_s, val[0], fr_val)
                butterflies(f_s, half(1))
                low(0)
                dve.wait_ge(fd_made, 8 * o + 8)
                operand(*RING[1], f_s, val[1], fr_val)
                if o == 0:
                    modulation_vectors()
                for r in range(16):
                    if r:
                        low(r)
                    if r + 2 < 16:
                        dve.wait_ge(fr_lo, 16 * o + r + 1)
                        filter_operand(r + 2)
                dve.wait_ge(fr_lo, 16 * o + 16)
            for g in range(20):
                dve.wait_ge(xt_done, g + 1)
                if g < 16:
                    nc.vector.tensor_copy(xa[:, g // 2, half(g % 2)], ps[:, g % 4, :]).then_inc(xt_free, 1)
                else:
                    nc.vector.tensor_copy(xc[:, 2 * (g - 16):2 * (g - 16) + 2, :], ps[:, g % 4, :].rearrange("p (k t) -> p k t", k=2)).then_inc(xt_free, 1)
            for n in range(2):
                rs = ps[:, 6 + (N_LAT + n) % 2, :]
                norm_inverse(N_LAT + n, aspread)
                dve.wait_ge(turned_made, N_LAT + n + 1)
                pre_apply(A_LAT + 8 * n, lambda k: xa[:, k, half(n)], lambda it: atmp[it % 2][:, :], lambda k: hh[:, k, half(n)],
                          lambda k: hl[:, k, half(n)], lambda k: fac[:, k:k + 1], rs, lambda k: mod[:, k:k + 1])
            rs = ps[:, 6 + N_CTX % 2, 0:C]
            norm_inverse(N_CTX, aspread)
            dve.wait_ge(turned_made, N_CTX + 1)
            pre_apply(A_CTX, lambda k: xc[:, k, :], lambda it: atmp[it % 2][:, 0:C], lambda k: hch[:, k, :], lambda k: hcl[:, k, :],
                      lambda k: fac[:, 64 + k:65 + k], rs, lambda k: mod[:, 48 + k:49 + k])
            g = 0
            dve.wait_ge(tab_in, 32)
            for s in range(4):
                for n in range(3 if s >= 2 else 2):
                    width = HALF if n < 2 else C
                    cols = slice(n * HALF, n * HALF + width)
                    dve.wait_ge(dn_done, g + 1)
                    bank = ps[:, g % 6, 0:width]
                    if s < 2:
                        nc.vector.tensor_copy(cq[:, s, cols], bank).then_inc(dn_free, 1)
                    elif s == 2:
                        nc.vector.tensor_copy(ckv[:, cols], bank).then_inc(dn_free, 1)
                    else:
                        tt(krt[:, cols], bank, rtab[:, cols], ALU.mult).then_inc(dn_free, 1)
                    g += 1
                if s == 1:
                    feature_sums(N_CQ, csq[:, :, :], cssum, HALF)
                elif s == 2:
                    inverse_root(N_CQ, cstd, crstd[:, 0:HALF], HALF)
                    feature_sums(N_CQ + 1, csq[:, :, :], cssum, HALF)
            dve.wait_ge(dn_free, 10)
            dve.sem_inc(kr_made, 3)
            def key_sums(n):
                width = HALF if n < 2 else C
                feature_sums(N_CKV + n, csq[:, 0:1, 0:width], cssum, width)

            def key_inverse(n):
                width = HALF if n < 2 else C
                inverse_root(N_CKV + n, cstd, crstd[:, n * HALF:n * HALF + width], width)

            key_sums(0)
            inverse_root(N_CQ + 1, cstd, crstd[:, HALF:T], HALF)
            for k in range(2):
                stt(cq[:, k, :], cq[:, k, :], vec[:, V_GQ + k:V_GQ + k + 1], crstd[:, 0:T], ALU.mult, ALU.mult).then_inc(cn_val, 1)
            dve.wait_ge(cn_val, 2)
            key_sums(1)
            key_inverse(0)
            key_sums(2)
            key_inverse(1)
            key_inverse(2)
            stt(ckv[:, :], ckv[:, :], vec[:, V_GKV:V_GKV + 1], crstd[:, :], ALU.mult, ALU.mult).then_inc(cn_val, 1)
            for k in range(2):
                dve.wait_ge(cn_hi, k + 1)
                tt(cql[:, k, :], cq[:, k, :], cqh[:, k, :], ALU.subtract).then_inc(cn_lo, 1)
            dve.wait_ge(cn_hi, 3)
            dve.wait_ge(cn_val, 3)
            tt(ckvl[:, :], ckv[:, :], ckvh[:, :], ALU.subtract).then_inc(cn_lo, 1)
            for c in range(3):
                width = HALF if c < 2 else C
                cols = slice(c * HALF, c * HALF + width)
                for hd in range(2):
                    dve.wait_ge(kr_hi, 2 * c + 2)
                    tt(kl[NOPE:P, hd, cols], ps[NOPE:P, 3 + c, 0:width], kh[NOPE:P, hd, cols], ALU.subtract).then_inc(kr_lo, 1)
            dve.wait_ge(kr_lo, 6)
            dve.wait_ge(x_saved, 16)
            dve.sem_inc(pp_free, 4)

            def query_value(g, j):
                dve.wait_ge(pp_done, 10 * g + j + 1)
                if j >= 2:
                    dve.wait_ge(q_lo, 4 * g + j - 1)
                tt(qf[j % 2][:, :], ps[:, j % 4, :], rtab[:, half(j % 2)], ALU.mult).then_inc(q_val, 1)
                dve.wait_ge(q_val, 4 * g + j + 1)
                dve.sem_inc(pp_free, 1)

            def query_low(g, j):
                dve.wait_ge(pp_hi, 13 * g + j + 1)
                tt(ql[:, j // 2, half(j % 2)], qf[j % 2][:, :], qh[:, j // 2, half(j % 2)], ALU.subtract).then_inc(q_lo, 1)

            def key_low(g, j):
                width = HALF if j < 6 else C
                cols = slice((j - 4) * HALF, (j - 4) * HALF + width)
                for hd in range(2):
                    dve.wait_ge(pp_hi, 13 * g + 4 + 2 * (j - 4) + 2)
                    inst = tt(kl[0:NOPE, hd, cols], ps[NOPE * hd:NOPE * hd + NOPE, j % 4, 0:width], kh[0:NOPE, hd, cols], ALU.subtract)
                    inst.then_inc(pp_free if hd else k_lo, 1)

            def value_low(g, j):
                t0 = 4 * (j - 7)
                nt = min(10, t0 + 4) - t0
                dve.wait_ge(pp_hi, 13 * g + 10 + (j - 7) + 1)
                tt(vl[:, t0:t0 + nt, :, :].rearrange("p t h v -> p (t h) v"), ps[:, PIECE_BANK[j], 0:nt * P].rearrange("p (g v) -> p g v", v=VD),
                   vh[:, t0:t0 + nt, :, :].rearrange("p t h v -> p (t h) v"), ALU.subtract).then_inc(pp_free, 1)

            def maximum(g, u, j):
                a = 2 * (u % 2) + j
                dve.wait_ge(s_done, 16 * g + 2 * u + j + 1)
                if u >= 2:
                    dve.wait_ge(p_made, 16 * g + 2 * u + j - 3)
                nc.vector.reduce_max(mxr[:, a:a + 1], psf[:, j * KEYS:(j + 1) * KEYS], AXX).then_inc(raw_max, 1)
                dve.wait_ge(raw_max, 16 * g + 2 * u + j + 1)
                ts(mx[:, a:a + 1], mxr[:, a:a + 1], -SCALE, None, ALU.mult).then_inc(max_made, 1)

            def turned_low(g, u, jj):
                idx = 5 * u + jj
                dve.wait_ge(t_hi, 40 * g + idx + 1)
                tt(ptl[idx % 4][:, :, :], ps[:, 5 + idx % 2, :].rearrange("p (k q) -> p k q", k=2), pth[idx % 4][:, :, :], ALU.subtract).then_inc(t_free, 1)

            def inverse_sum(g, u):
                a = 2 * (u % 2)
                if u >= 1:
                    dve.wait_ge(rb_made, 16 * g + 2 * u)
                nc.vector.reciprocal(inv_sum[:, :], sm[:, a:a + 2]).then_inc(rs_made, 1)
                dve.wait_ge(rs_made, 8 * g + u + 1)
                for j in range(2):
                    ts(rb[:, j, :], ones[:, 0:VD], inv_sum[:, j:j + 1], None, ALU.mult).then_inc(rb_made, 1)

            def result(g, u):
                dve.wait_ge(rc_made, 8 * g + u + 1)
                hd, q = u // 4, u % 4
                feature = slice(g, g + 1) if isinstance(g, int) else bass.ds(g, 1)
                tt(ao[VD * hd:VD * hd + VD, feature, q * 256:(q + 1) * 256], ps[0:VD, 7:8, 0:256],
                   rc[:, :].rearrange("p (a q) -> p a q", a=1), ALU.mult).then_inc(o_made, 1)

            def group(g, more):
                maximum(g, 0, 0)
                value_low(g, 8)
                value_low(g, 9)
                maximum(g, 0, 1)
                for u in range(7):
                    maximum(g, u + 1, 0)
                    turned_low(g, u, 0)
                    turned_low(g, u, 1)
                    inverse_sum(g, u)
                    turned_low(g, u, 2)
                    maximum(g, u + 1, 1)
                    turned_low(g, u, 3)
                    turned_low(g, u, 4)
                    result(g, u)
                turned_low(g, 7, 0)
                turned_low(g, 7, 1)
                inverse_sum(g, 7)
                if not more:
                    for jj in range(2, 5):
                        turned_low(g, 7, jj)
                    result(g, 7)
                    return
                query_value(g + 1, 0)
                query_value(g + 1, 1)
                turned_low(g, 7, 2)
                query_low(g + 1, 0)
                query_value(g + 1, 2)
                turned_low(g, 7, 3)
                query_low(g + 1, 1)
                query_value(g + 1, 3)
                turned_low(g, 7, 4)
                query_low(g + 1, 2)
                query_low(g + 1, 3)
                key_low(g + 1, 4)
                key_low(g + 1, 5)
                result(g, 7)
                key_low(g + 1, 6)
                value_low(g + 1, 7)

            for j in range(4):
                query_value(0, j)
                if j:
                    query_low(0, j - 1)
            query_low(0, 3)
            for j in range(4, 7):
                key_low(0, j)
            value_low(0, 7)
            with dve.Fori(0, HEADS // 4 - 1) as i:
                group(2 * i, True)
                group(2 * i + 1, True)
            group(HEADS // 2 - 2, True)
            group(HEADS // 2 - 1, False)
            dve.wait_ge(o_made, 64)
            for k in range(KT):
                dve.wait_ge(oh_made, k + 1)
                tt(hl[:, k, :], ao[:, k, :], hh[:, k, :], ALU.subtract).then_inc(ol_made, 1)

            def post_apply(items, factor, rstd, n):
                for k in range(KT):
                    stt(y[:, k, half(n)], y[:, k, half(n)], factor(k), rstd, ALU.mult, ALU.mult).then_inc(post_y, 1)
                    if k % 2:
                        dve.wait_ge(post_y, items + k)
                        tt(xm[:, k - 1, half(n)], xm[:, k - 1, half(n)], y[:, k - 1, half(n)], ALU.add).then_inc(post_x, 1)

            def post_then_pre(post, pre, b_items, a_items, f_post, f_pre, shift):
                for n in range(2):
                    norm_inverse(post + n, mspread)
                    dve.wait_ge(turned_made, post + n + 1)
                    post_apply(b_items + 8 * n, lambda k: fac[:, f_post + k:f_post + k + 1], ps[:, 6 + (post + n) % 2, :], n)
                if pre is None:
                    return
                norm_inverse(pre, mspread)
                dve.wait_ge(post_x, b_items // 2 + 8)
                dve.wait_ge(post_xp, b_items // 2 + 8)
                for n in range(2):
                    dve.wait_ge(turned_made, pre + n + 1)
                    pre_apply(a_items + 8 * n, lambda k: xm[:, k, half(n)], lambda it: mtmp[it % 2][:, :], lambda k: hh[:, k, half(n)],
                              lambda k: hl[:, k, half(n)], lambda k: fac[:, f_pre + k:f_pre + k + 1], ps[:, 6 + (pre + n) % 2, :],
                              lambda k: mod[:, shift + k:shift + k + 1], None if n else lambda: norm_inverse(pre + 1, mspread))

            def mlp(l):
                dve.sem_inc(hid_free[l], 4)
                dve.sem_inc(acc_free[l], 4)
                if l == 0:
                    dve.wait_ge(pre_lo, A_MLP0 + 16)
                    dve.sem_inc(ada1_acc, 1)
                    dve.sem_inc(ada1_mod, 1)
                with dve.Fori(0, NCHUNK) as j:
                    def modulation(b):
                        dve.wait_ge(ada1_in, 16 * (ABLOCKS * j + b + 1))
                        for k in range(KT):
                            dve.wait_ge(ada1_acc, 1 + KT * (ABLOCKS * j + b) + k)
                            if k == 0:
                                if b == 0:
                                    dve.wait_ge(ada1_mod, j + 1)
                                ts(bacc[:, b, :], braw[:, k, :], sil[:, k:k + 1], None, ALU.mult).then_inc(ada1_acc, 1)
                            else:
                                stt(bacc[:, b, :], braw[:, k, :], sil[:, k:k + 1], bacc[:, b, :], ALU.mult, ALU.add).then_inc(ada1_acc, 1)

                    def low(g):
                        dve.wait_ge(hid_hi[l], 8 * j + g + 1)
                        tt(hidl[:, g // 2, half(g % 2)], ms2[g % 2][:, :], hidh[:, g // 2, half(g % 2)], ALU.subtract).then_inc(hid_lo[l], 1)

                    for g in range(8):
                        dve.wait_ge(hid_done[l], 8 * j + g + 1)
                        ts(mr[g % 2][:, :], ps[:, g % 4, :], 0.0, None, ALU.max).then_inc(hid_free[l], 1)
                        if g:
                            low(g - 1)
                        if l == 0 and g == 4:
                            modulation(0)
                    low(7)
                    if l == 0:
                        modulation(1)
                    dve.wait_ge(y_zero, l + 1)
                    dve.wait_ge(acc_free[l], 4 + 16 * j)
                    for q in range(16):
                        s, n, m = q // 4, q // 2 % 2, q % 2
                        dve.wait_ge(acc_done[l], 16 * j + q + 1)
                        dst = y[:, 2 * s + m, half(n)]
                        tt(dst, ps[:, 4 + 2 * n + m, :], dst, ALU.add).then_inc(acc_free[l], 1)
                        if l == 0 and q == 5:
                            modulation(2)
                        if l == 0 and q == 12:
                            dve.wait_ge(ada1_sum, j + 1)
                            cols = ABLOCKS * ACOLS // P
                            tt(mod[:, bass.ds(64 + cols * j, cols)], ps[:, 0, 0:cols], vec[:, bass.ds(V_ADAB + 48 + cols * j, cols)], ALU.add).then_inc(ada1_mod, 1)
                dve.wait_ge(acc_free[l], 4 + 16 * NCHUNK)
                if l == 0:
                    dve.wait_ge(ada1_mod, 1 + NCHUNK)
                    factors(1)

            dve.sem_inc(wo_free, 4)
            with dve.Fori(0, 4) as i:
                for g in range(4):
                    dve.wait_ge(wo_done, 4 * i + g + 1)
                    nc.vector.tensor_copy(y[:, bass.ds(2 * i + g // 2, 1), half(g % 2)], ps[:, g:g + 1, :]).then_inc(wo_free, 1)
            dve.wait_ge(x_back, 16)
            post_then_pre(N_POST1, N_PRE2, B_ATT, A_MLP0, 8, 16, 24)
            mlp(0)
            post_then_pre(N_POST2, N_PREH, B_MLP0, A_HY, 24, 32, 64)
            for s in range(2):
                dv.did(nc.vector.memset(ub[s][:, 0:1], 0.0))
                dv.did(nc.vector.memset(ub[s][:, T + 1:T + 2], 0.0))
            dv.wait()
            dve.sem_inc(wi_free, 4)
            dve.sem_inc(ut_made, 4)

            def outer(i, s):
                dve.wait_ge(uc_mid, 2 * i + s + 1)
                stt(uc[s][:, :], ub[s][:, 0:T], vec[:, bass.ds(V_WSH + 2 * i + s, 1)], uc[s][:, :], ALU.mult, ALU.add).then_inc(uc_left, 1)
                dve.wait_ge(uc_left, 2 * i + s + 1)
                stt(uc[s][:, :], ub[s][:, 2:T + 2], vec[:, bass.ds(V_WSH + 48 + 2 * i + s, 1)], uc[s][:, :], ALU.mult, ALU.add).then_inc(uc_made, 1)

            def take(i, s, first):
                for n in range(2):
                    dve.wait_ge(ut_done, 4 * i + 2 * s + n + 1)
                    if not first:
                        dve.wait_ge(ut_out[s], 16 * i)
                    nc.vector.tensor_copy(ut[s][:, 4 * n:4 * n + 4, :], ps[:, 4 + 2 * s + n, :].rearrange("p (q c) -> p q c", q=4)).then_inc(ut_made, 1)

            def biased(i, s, first):
                for n in range(2):
                    dve.wait_ge(wi_done, 4 * i + 2 * s + n + 1)
                    if not first:
                        dve.wait_ge(uc_made, 2 * i + s - 1)
                    ts(ub[s][:, 1 + n * HALF:1 + (n + 1) * HALF], ps[:, 2 * s + n, :], vec[:, bass.ds(V_BIN + 2 * i + s, 1)], None, ALU.add).then_inc(wi_free, 1)

            biased(0, 0, True)
            outer(0, 0)
            biased(0, 1, True)
            take(0, 0, True)
            outer(0, 1)
            biased(1, 0, False)
            take(0, 1, True)
            outer(1, 0)
            with dve.Fori(1, 11) as i:
                biased(i, 1, False)
                take(i, 0, False)
                outer(i, 1)
                biased(i + 1, 0, False)
                take(i, 1, False)
                outer(i + 1, 0)
            biased(11, 1, False)
            take(11, 0, False)
            outer(11, 1)
            take(11, 1, False)
            dve.wait_ge(src_in, 16 * KT)
            dve.wait_ge(ut_made, 4 + 48)
            dve.sem_inc(ci_free, 8)
            with dve.Fori(0, ORDERS) as o:
                dv.enter(o, 4 + 10 + 48 + 16)

                def low(c, n):
                    dve.wait_ge(cr_hi, 16 * o + 2 * c + n + 1)
                    tt(rg_lo[n][:, :, :], val[n][:, :, :], rg_hi[n][:, :, :], ALU.subtract).then_inc(cr_lo, 1)

                def value(c, n):
                    if c:
                        dve.wait_ge(cr_lo, 16 * o + 2 * (c - 1) + n + 1)
                    operand(c, n, src, val[n], cr_val)

                def product(p):
                    f, n = pair_tile(p)
                    gr, gi = pair_groups(p)
                    c, m = f // 2, f % 2
                    re, im = (2 * m, 2 * m + 1) if c == 0 else (m, 2 + m)
                    k = ks[p % 2]
                    ur, ui = ps[:, gr % 8, :], ps[:, gi % 8, :]
                    pr_, pi_ = pz[:, c, re, half(n)], pz[:, c, im, half(n)]
                    dve.wait_ge(k_in[p % 2], 16 * (8 * o + p // 2 + 1))
                    if f == 0:
                        dve.wait_ge(k_ny_in, 16 * (2 * o + n + 1))
                    dve.wait_ge(cf_done, 32 * o + gi + 1)
                    if p >= 2:
                        dve.wait_ge(pz_made, 16 * o + p - 1)
                    tt(pr_, ur, k[:, 0, :], ALU.mult)
                    tt(pi_, ur, k[:, 1, :], ALU.mult)
                    tt(pt[p % 2][:, 0, :], ui, k[:, 1, :], ALU.mult)
                    tt(pt[p % 2][:, 1, :], ui, k[:, 2 if f == 0 else 0, :], ALU.mult).then_inc(cf_free, 1)

                butterflies(src, half(0))
                value(0, 0)
                butterflies(src, half(1))
                low(0, 0)
                value(0, 1)
                value(1, 0)
                low(0, 1)
                value(1, 1)
                for s in range(2):
                    dve.wait_ge(ut_out[s], 16 * 12)
                product(0)
                low(1, 0)
                value(2, 0)
                product(1)
                low(1, 1)
                value(2, 1)
                product(2)
                product(3)
                for n in range(2):
                    product(4 + 2 * n)
                    low(2, n)
                    value(3, n)
                    product(5 + 2 * n)
                for n in range(2):
                    product(8 + 2 * n)
                    low(3, n)
                    product(9 + 2 * n)

                def low_inverse(c, n):
                    dve.wait_ge(cr_hi, 16 * o + 8 + 2 * c + n + 1)
                    tt(rg_lo[n][:, :, :], pz[:, c, :, half(n)], rg_hi[n][:, :, :], ALU.subtract).then_inc(cr_lo, 1)

                def back(s, n, q, idx):
                    dve.wait_ge(ci_done, 32 * o + idx + 1)
                    dve.wait_ge(ci_free, 8 + 32 * o + idx)
                    dv.wait()
                    z = ps[:, idx % 8, :]
                    y0, y1, y2, y3 = (src[:, a, q % 2, half(n)] for a in range(4))
                    if s == 0 and q < 2:
                        last = nc.vector.tensor_copy(y0, z)
                    elif s == 0:
                        dv.did(tt(y1, y0, z, ALU.subtract))
                        dv.wait()
                        last = tt(y0, y0, z, ALU.add)
                    elif s == 1:
                        dv.did(nc.vector.tensor_copy(y2, y0))
                        dv.did(stt(y3, z, -R4, y1, ALU.mult, ALU.add))
                        dv.wait()
                        dv.did(tt(y0, y0, z, ALU.add))
                        last = stt(y1, z, R4, y1, ALU.mult, ALU.add)
                    elif s == 2:
                        dv.did(tt(y2, y2, z, ALU.subtract))
                        dv.did(stt(y1, z, -R4, y1, ALU.mult, ALU.add))
                        last = stt(y3, z, -R4, y3, ALU.mult, ALU.add)
                    elif s == 3:
                        dv.did(tt(y0, y0, z, ALU.add))
                        last = tt(y2, y2, z, ALU.subtract)
                    elif s == 4:
                        dv.did(tt(y1, y1, z, ALU.subtract))
                        last = tt(y3, y3, z, ALU.add)
                    elif s == 5:
                        dv.did(tt(y0, y0, z, ALU.add))
                        dv.did(stt(y1, z, -R4, y1, ALU.mult, ALU.add))
                        last = stt(y3, z, R4, y3, ALU.mult, ALU.add)
                    else:
                        dv.did(tt(y2, y2, z, ALU.add))
                        dv.did(stt(y1, z, -R4, y1, ALU.mult, ALU.add))
                        last = stt(y3, z, -R4, y3, ALU.mult, ALU.add)
                    last.then_inc(ci_free, 1)
                    if s == 6:
                        dve.wait_ge(gate_in, 16 * KT * (o + 1))
                        dve.wait_ge(ci_free, 8 + 32 * o + idx + 1)
                        dv.wait()
                        for a, y_a in enumerate((y0, y1, y2, y3)):
                            dv.did(tt(y_a, y_a, gate[:, a, q % 2, half(n)], ALU.mult))

                for n in range(2):
                    product(12 + 2 * n)
                    product(13 + 2 * n)
                    low_inverse(0, n)
                for s in range(7):
                    c = (s + 1) // 2
                    for n, _, _, idx in transform_groups(s, True):
                        back(s, n, idx % 4 if s == 0 else idx % 2, idx)
                        if c < 3 and idx + 1 == ring_read(c, n):
                            low_inverse(c + 1, n)
                dv.wait()
                dve.sem_inc(z_made, 1)
                dv.leave(ORDERS)
            for g in range(16):
                dve.wait_ge(z_hi, g + 1)
                tt(zl[:, g // 2, half(g % 2)], ps[:, g % 4, :], zh[:, g // 2, half(g % 2)], ALU.subtract).then_inc(z_lo, 1)
            dve.wait_ge(z_lo, 16)
            dve.sem_inc(ho_free, 4)
            with dve.Fori(0, 4) as i:
                for g in range(4):
                    dve.wait_ge(ho_done, 4 * i + g + 1)
                    ts(y[:, bass.ds(2 * i + g // 2, 1), half(g % 2)], ps[:, g:g + 1, :], vec[:, bass.ds(V_BOUT + 2 * i + g // 2, 1)], None, ALU.add).then_inc(ho_free, 1)
            dve.wait_ge(x_back, 32)
            post_then_pre(N_POSTH, N_PREM, B_HY, A_MLP1, 40, 48, 64 + 24)
            mlp(1)
            post_then_pre(N_POSTM, None, B_MLP1, None, 56, None, None)
            for g in range(16):
                t = g // 2
                dve.wait_ge(out_done, g + 1)
                if t >= 2:
                    dve.wait_ge(out_sent[t % 2], 16 * (t // 2))
                nc.vector.tensor_copy(ot[t % 2][:, half(g % 2)], ps[:, g % 4, :]).then_inc(out_made, 1)


def kernel(x, c, ctx, c_ctx, ada_w, ada_b, norm_g, mla_w_dq, mla_g_q, mla_w_uq, mla_w_dkv,
           mla_g_kv, mla_w_ukv, mla_w_o, hy_w_in, hy_b_in, hy_w_short, hy_b_short, hy_f_w1,
           hy_f_b1, hy_f_w2, hy_f_b2, hy_f_w3, hy_f_freq, hy_bias, hy_w_out, hy_b_out,
           mlp_w1, mlp_w2):
    import concourse.bacc as bacc
    from concourse.bass_utils import run_bass_kernel_spmd

    def arr(a):
        return np.ascontiguousarray(np.asarray(a))

    (x, c, ctx, c_ctx, ada_w, ada_b, norm_g, w_dq, g_q, w_uq, w_dkv, g_kv, w_ukv, w_o, w_in, b_in, w_sh, b_sh,
     f_w1, f_b1, f_w2, f_b2, f_w3, freq, hbias, w_out, b_out, w1, w2) = map(arr, (
         x, c, ctx, c_ctx, ada_w, ada_b, norm_g, mla_w_dq, mla_g_q, mla_w_uq, mla_w_dkv, mla_g_kv, mla_w_ukv,
         mla_w_o, hy_w_in, hy_b_in, hy_w_short, hy_b_short, hy_f_w1, hy_f_b1, hy_f_w2, hy_f_b2, hy_f_w3,
         hy_f_freq, hy_bias, hy_w_out, hy_b_out, mlp_w1, mlp_w2))

    def row(v):
        return np.concatenate([v.reshape(1, FH), np.zeros((1, P - FH), v.dtype)], axis=1)

    def v_first(a):
        return np.concatenate([a[..., 2 * D:], a[..., :2 * D]], axis=-1)

    w_in, b_in, w_sh, b_sh = map(v_first, (w_in, b_in, w_sh, b_sh))
    rows = [v.reshape(-1, P) for v in (ada_b, norm_g, b_in, w_sh, b_sh, b_out, g_q, g_kv, c, c_ctx)]
    rows += [row(f_b1), row(f_b2), row(freq)]
    used = sum(r.shape[0] for r in rows)
    vecs = np.concatenate(rows + [np.zeros((NVEC - used, P), x.dtype)], axis=0)

    kr = w_dkv[0][:, KVR:]
    swap = np.concatenate([kr[:, 16:], kr[:, :16]], axis=1)
    w_down = np.concatenate([w_dq[0], w_dkv[0][:, :KVR], w_dkv[0][:, :64], kr, swap], axis=1)

    uq = w_uq[0].reshape(2, P, HEADS, NOPE + ROPE)
    uq = np.concatenate([uq, uq[..., NOPE + 16:], uq[..., NOPE:NOPE + 16]], axis=3)
    ukv = w_ukv[0].reshape(P, HEADS, NOPE + VD)
    w_head = np.zeros((HEADS // 2, P, 8, P), x.dtype)
    for g in range(HEADS // 2):
        for k in range(2):
            for h in range(2):
                w_head[g, :, 2 * k + h] = uq[k, :, 2 * g + h]
        w_head[g, :, 4] = ukv[:, 2 * g:2 * g + 2, :NOPE].reshape(P, P)
        w_head[g, :, 5] = ukv[:, 2 * g:2 * g + 2, NOPE:].reshape(P, P)

    fwd, inv = dft_steps()
    ins = dict(x=x[0], ctx=ctx[0], vecs=vecs, ada_w=ada_w, w_down=w_down, w_head=w_head.reshape(HEADS // 2, P, 8 * P),
               w_o=w_o[0], w_in=w_in[0], w_out=w_out[0], mlp_w1=w1, mlp_w2=w2, f_w1=f_w1[0], f_w2=f_w2[0], f_w3=f_w3[0],
               hy_bias=hbias[0], rope=rope_table(), ropesum=rope_sum(), ident=np.eye(P, dtype=np.float32),
               zpos=filter_positions(), decay=filter_decay(), dft_fwd=fwd, dft_inv=inv)
    nc = bacc.Bacc("TRN2", target_bir_lowering=False, num_devices=1)
    arrays, aps = {}, {}
    for name, a in ins.items():
        a = np.ascontiguousarray(a)
        arrays[f"in_{name}"] = a
        aps[name] = nc.dram_tensor(f"in_{name}", a.shape, mybir.dt.from_np(a.dtype), kind="ExternalInput").ap()
    aps["out"] = nc.dram_tensor("out_y", (T, D), F32, kind="ExternalOutput").ap()
    build_program(nc, **aps)
    res = run_bass_kernel_spmd(nc, [arrays], core_ids=[0])
    return res.results[0]["out_y"].reshape(1, T, D)
```
